# Optimizing a Trainium2 kernel written in Bass

```python
import math
import jax, jax.numpy as jnp
from jax import lax
import numpy as np

D_MODEL = 1024
BATCH = 1
SEQ = 256
DEPTH = 2

CHUNK = 64
HEAD_DIM = 64
N_HEADS = D_MODEL // HEAD_DIM
N_SB_HEADS = N_HEADS // 2
N_RET_HEADS = N_HEADS - N_SB_HEADS
D_SB = N_SB_HEADS * HEAD_DIM
D_RET = N_RET_HEADS * HEAD_DIM
D_IN_EVEN = 3 * D_SB + 4 * D_RET
SB_BLOCK = 128
N_C_HEADS = N_HEADS
LEFT_CHUNKS = 8
BAND = (LEFT_CHUNKS + 1) * CHUNK
MAX_REL = 4 * CHUNK
D_FF_DENSE = 256 * (-(-(8 * D_MODEL // 3) // 256))
D_FF_EXPERT = 7 * D_MODEL // 2
N_EXPERTS = 8
TOP_K = 2
ROPE_BASE = 10000.0
LN_EPS = 1e-5
N_EVEN = (DEPTH + 1) // 2
N_ODD = DEPTH // 2
DEEPNORM_ALPHA = (2 * DEPTH) ** 0.25
DEEPNORM_BETA = (8 * DEPTH) ** -0.25

kernel_name = "hybrid_stickbreak_retention_chunkattn_moe"

def layer_norm(x, g, b):
    xf = x.astype(jnp.float32)
    mu = jnp.mean(xf, axis=-1, keepdims=True)
    var = jnp.mean(jnp.square(xf - mu), axis=-1, keepdims=True)
    return ((xf - mu) * lax.rsqrt(var + LN_EPS) * g + b).astype(x.dtype)

def rotary(x, pos):
    half = HEAD_DIM // 2
    inv_freq = ROPE_BASE ** (-jnp.arange(half, dtype=jnp.float32) / half)
    ang = pos.astype(jnp.float32)[:, None] * inv_freq[None, :]
    cos = jnp.cos(ang)[None, :, None, :]
    sin = jnp.sin(ang)[None, :, None, :]
    x1, x2 = x[..., :half], x[..., half:]
    return jnp.concatenate([x1 * cos - x2 * sin, x1 * sin + x2 * cos], axis=-1)

def stick_breaking(q, k, v):
    S = q.shape[2]
    scale = HEAD_DIM ** -0.5
    outs = []
    for blk in range(S // SB_BLOCK):
        t0 = blk * SB_BLOCK
        t1 = t0 + SB_BLOCK
        z = jnp.einsum('bhqd,bhkd->bhqk', q[:, :, t0:t1], k[:, :, :t1]) * scale
        valid = jnp.arange(t1)[None, :] < (t0 + jnp.arange(SB_BLOCK))[:, None]
        log_1m = jnp.where(valid, jax.nn.log_sigmoid(-z), 0.0)
        suffix = lax.cumsum(log_1m, axis=3, reverse=True) - log_1m
        w = jnp.where(valid, jnp.exp(jax.nn.log_sigmoid(z) + suffix), 0.0)
        outs.append(jnp.einsum('bhqk,bhkd->bhqd', w, v[:, :, :t1]))
    return jnp.concatenate(outs, axis=2)

def retention(q, k, v):
    B, S, H, d = q.shape
    n_chunks = S // CHUNK
    gamma = 1.0 - 2.0 ** (-5.0 - jnp.arange(H, dtype=jnp.float32))
    log_g = jnp.log(gamma)
    i = jnp.arange(CHUNK, dtype=jnp.float32)
    diff = i[:, None] - i[None, :]
    decay_in = jnp.where(diff >= 0, jnp.exp(log_g[:, None, None] * jnp.maximum(diff, 0.0)), 0.0)
    decay_q = jnp.exp(log_g[:, None] * (i + 1.0))[..., None]
    decay_k = jnp.exp(log_g[:, None] * (CHUNK - 1.0 - i))[..., None]
    decay_c = jnp.exp(log_g * CHUNK)[:, None, None]

    def to_chunks(t):
        return t.reshape(B, n_chunks, CHUNK, H, d).transpose(1, 0, 3, 2, 4)

    def step(state, inp):
        qc, kc, vc = inp
        inner = jnp.einsum('bhid,bhjd->bhij', qc, kc) * decay_in
        out = (jnp.einsum('bhij,bhjd->bhid', inner, vc)
               + jnp.einsum('bhid,bhde->bhie', qc, state) * decay_q)
        state = state * decay_c + jnp.einsum('bhjd,bhje->bhde', kc * decay_k, vc)
        return state, out

    state0 = jnp.zeros((B, H, d, d), jnp.float32)
    _, o = lax.scan(step, state0, (to_chunks(q), to_chunks(k), to_chunks(v)))
    return o.transpose(1, 0, 3, 2, 4).reshape(B, S, H, d)

def chunk_attention(q, k, v, bias_table):
    B, S, H, d = q.shape
    n_chunks = S // CHUNK
    pad = LEFT_CHUNKS * CHUNK
    scale = HEAD_DIM ** -0.5
    k_pad = jnp.pad(k, ((0, 0), (pad, 0), (0, 0), (0, 0)))
    v_pad = jnp.pad(v, ((0, 0), (pad, 0), (0, 0), (0, 0)))
    rel = jnp.arange(CHUNK)[:, None] + pad - jnp.arange(BAND)[None, :]
    rel_idx = jnp.clip(rel, -MAX_REL, MAX_REL) + MAX_REL
    bias = bias_table[:, rel_idx].astype(jnp.float32)

    def one_chunk(c):
        start = c * CHUNK
        q_c = lax.dynamic_slice_in_dim(q, start, CHUNK, axis=1)
        k_b = lax.dynamic_slice_in_dim(k_pad, start, BAND, axis=1)
        v_b = lax.dynamic_slice_in_dim(v_pad, start, BAND, axis=1)
        s = jnp.einsum('bqhd,bkhd->bhqk', q_c, k_b).astype(jnp.float32) * scale + bias
        key_pos = start - pad + jnp.arange(BAND)
        s = jnp.where((key_pos >= 0)[None, None, None, :], s, -jnp.inf)
        p = jax.nn.softmax(s, axis=-1)
        return jnp.einsum('bhqk,bkhd->bqhd', p.astype(v.dtype), v_b)

    o = lax.map(one_chunk, jnp.arange(n_chunks))
    return o.transpose(1, 0, 2, 3, 4).reshape(B, S, H * d)

def even_mixer(x, w_in, ret_gn_g, w_out):
    B, S, _ = x.shape
    h = x @ w_in
    splits = [D_SB, 2 * D_SB, 3 * D_SB, 3 * D_SB + D_RET, 3 * D_SB + 2 * D_RET, 3 * D_SB + 3 * D_RET]
    q_sb, k_sb, v_sb, q_r, k_r, v_r, g_r = jnp.split(h, splits, axis=-1)

    def sb_heads(t):
        return t.reshape(B, S, N_SB_HEADS, HEAD_DIM).transpose(0, 2, 1, 3).astype(jnp.float32)

    o_sb = stick_breaking(sb_heads(q_sb), sb_heads(k_sb), sb_heads(v_sb))
    o_sb = o_sb.transpose(0, 2, 1, 3).reshape(B, S, D_SB)

    def ret_heads(t):
        return t.reshape(B, S, N_RET_HEADS, HEAD_DIM).astype(jnp.float32)

    pos = jnp.arange(S)
    qr = rotary(ret_heads(q_r), pos) * HEAD_DIM ** -0.5
    kr = rotary(ret_heads(k_r), pos)
    o_r = retention(qr, kr, ret_heads(v_r))
    mu = jnp.mean(o_r, axis=-1, keepdims=True)
    var = jnp.mean(jnp.square(o_r - mu), axis=-1, keepdims=True)
    o_r = ((o_r - mu) * lax.rsqrt(var + LN_EPS)).reshape(B, S, D_RET) * ret_gn_g
    o_r = jax.nn.silu(g_r.astype(jnp.float32)) * o_r

    o = jnp.concatenate([o_sb, o_r], axis=-1).astype(x.dtype)
    return o @ w_out

def odd_mixer(x, w_qkv, rel_bias, w_out):
    B, S, _ = x.shape
    q, k, v = jnp.split(x @ w_qkv, 3, axis=-1)
    shp = (B, S, N_C_HEADS, HEAD_DIM)
    o = chunk_attention(q.reshape(shp), k.reshape(shp), v.reshape(shp), rel_bias)
    return o.astype(x.dtype) @ w_out

def swiglu(x, w_gate, w_up, w_down):
    return (jax.nn.silu(x @ w_gate) * (x @ w_up)) @ w_down

def moe_swiglu(x, w_router, b_router, w_gate, w_up, w_down):
    B, S, D = x.shape
    xt = x.reshape(B * S, D)
    logits = xt.astype(jnp.float32) @ w_router.astype(jnp.float32) + b_router.astype(jnp.float32)
    top_val, top_idx = lax.top_k(logits, TOP_K)
    gates = jax.nn.softmax(top_val, axis=-1)
    combine = jnp.sum(jax.nn.one_hot(top_idx, N_EXPERTS, dtype=jnp.float32) * gates[..., None], axis=1)
    y = jnp.zeros((B * S, D), jnp.float32)
    for e in range(N_EXPERTS):
        h = jax.nn.silu(xt @ w_gate[e]) * (xt @ w_up[e])
        y = y + combine[:, e:e + 1] * (h @ w_down[e]).astype(jnp.float32)
    return y.astype(x.dtype).reshape(B, S, D)

def setup_inputs(seed: int = 0) -> dict:
    key = jax.random.key(seed)
    ks = jax.random.split(key, 24)

    def nrm(k, shape, scale):
        return jax.random.normal(k, shape, jnp.float32) * scale

    d = D_MODEL
    beta = DEEPNORM_BETA
    return {
        'x': nrm(ks[0], (BATCH, SEQ, d), 1.0),
        'even_ln1_g': 1.0 + nrm(ks[1], (N_EVEN, d), 0.02),
        'even_ln1_b': nrm(ks[2], (N_EVEN, d), 0.02),
        'even_w_in': nrm(ks[3], (N_EVEN, d, D_IN_EVEN), d ** -0.5),
        'even_ret_gn_g': 1.0 + nrm(ks[4], (N_EVEN, D_RET), 0.02),
        'even_w_out': nrm(ks[5], (N_EVEN, d, d), d ** -0.5 * beta),
        'even_ln2_g': 1.0 + nrm(ks[6], (N_EVEN, d), 0.02),
        'even_ln2_b': nrm(ks[7], (N_EVEN, d), 0.02),
        'even_w_gate': nrm(ks[8], (N_EVEN, d, D_FF_DENSE), d ** -0.5),
        'even_w_up': nrm(ks[9], (N_EVEN, d, D_FF_DENSE), d ** -0.5),
        'even_w_down': nrm(ks[10], (N_EVEN, D_FF_DENSE, d), D_FF_DENSE ** -0.5 * beta),
        'odd_ln1_g': 1.0 + nrm(ks[11], (N_ODD, d), 0.02),
        'odd_ln1_b': nrm(ks[12], (N_ODD, d), 0.02),
        'odd_w_qkv': nrm(ks[13], (N_ODD, d, 3 * d), d ** -0.5),
        'odd_rel_bias': nrm(ks[14], (N_ODD, N_C_HEADS, 2 * MAX_REL + 1), 0.5),
        'odd_w_out': nrm(ks[15], (N_ODD, d, d), d ** -0.5 * beta),
        'odd_ln2_g': 1.0 + nrm(ks[16], (N_ODD, d), 0.02),
        'odd_ln2_b': nrm(ks[17], (N_ODD, d), 0.02),
        'odd_w_router': nrm(ks[18], (N_ODD, d, N_EXPERTS), d ** -0.5),
        'odd_b_router': nrm(ks[19], (N_ODD, N_EXPERTS), 0.01),
        'odd_w_gate': nrm(ks[20], (N_ODD, N_EXPERTS, d, D_FF_EXPERT), d ** -0.5),
        'odd_w_up': nrm(ks[21], (N_ODD, N_EXPERTS, d, D_FF_EXPERT), d ** -0.5),
        'odd_w_down': nrm(ks[22], (N_ODD, N_EXPERTS, D_FF_EXPERT, d), D_FF_EXPERT ** -0.5 * beta),
    }

def reference(x, even_ln1_g, even_ln1_b, even_w_in, even_ret_gn_g, even_w_out,
              even_ln2_g, even_ln2_b, even_w_gate, even_w_up, even_w_down,
              odd_ln1_g, odd_ln1_b, odd_w_qkv, odd_rel_bias, odd_w_out,
              odd_ln2_g, odd_ln2_b, odd_w_router, odd_b_router,
              odd_w_gate, odd_w_up, odd_w_down):
    alpha = DEEPNORM_ALPHA
    for layer in range(DEPTH):
        i = layer // 2
        if layer % 2 == 0:
            mix = even_mixer(x, even_w_in[i], even_ret_gn_g[i], even_w_out[i])
            x = layer_norm(alpha * x + mix, even_ln1_g[i], even_ln1_b[i])
            ffn = swiglu(x, even_w_gate[i], even_w_up[i], even_w_down[i])
            x = layer_norm(alpha * x + ffn, even_ln2_g[i], even_ln2_b[i])
        else:
            mix = odd_mixer(x, odd_w_qkv[i], odd_rel_bias[i], odd_w_out[i])
            x = layer_norm(alpha * x + mix, odd_ln1_g[i], odd_ln1_b[i])
            ffn = moe_swiglu(x, odd_w_router[i], odd_b_router[i],
                             odd_w_gate[i], odd_w_up[i], odd_w_down[i])
            x = layer_norm(alpha * x + ffn, odd_ln2_g[i], odd_ln2_b[i])
    return x


_drawn_inputs = setup_inputs


def setup_inputs(seed=0):
    import zlib

    import numpy as np

    out = dict(_drawn_inputs(seed))
    spreads = {}
    factors = {'even_ret_gn_g': 20.936, 'odd_ln2_g': 8.153, 'odd_ln2_b': 8.214, 'odd_b_router': 6.632}
    for name, (base, spread) in spreads.items():
        noise = np.random.default_rng([zlib.crc32(name.encode()), seed]).standard_normal(out[name].shape)
        drawn = base * np.exp(spread * noise) if base else spread * noise
        out[name] = __import__('jax').numpy.asarray(drawn.astype(out[name].dtype))
    for name, factor in factors.items():
        out[name] = (out[name] * factor).astype(out[name].dtype)
    return out
```

```python
from contextlib import ExitStack

import concourse.bass as bass
import numpy as np
from concourse import mybir

F32 = mybir.dt.float32
F32R = mybir.dt.float32r
I32 = mybir.dt.int32
ALU = mybir.AluOpType
ACT = mybir.ActivationFunctionType
AX = mybir.AxisListType.X

P = 128
D = 1024
T = 256
TT = T // P
KC = D // P
HD = 64
CHUNK = 64
N_SB = 8
N_RET = 8
N_C = 16
F_DENSE = 2816
F_EXP = 3584
N_EXP = 8
MAX_REL = 256
ALPHA = 4.0 ** 0.25
EPS = 1e-5
UC = 2048
RAW = 6
SPLIT = 3
MASKED = -1e30

IN_BLOCKS = 7
OUT_UNITS = 4
FF_BLOCKS = F_DENSE // 256
DOWN_UNITS = F_DENSE // 256
QKV_BLOCKS = 6
U_IN = 0
U_OUT = U_IN + 2 * IN_BLOCKS
U_FF = U_OUT + OUT_UNITS
U_DOWN = U_FF + 2 * FF_BLOCKS
U_QKV = U_DOWN + DOWN_UNITS
U_OUT2 = U_QKV + 2 * QKV_BLOCKS
U_MOE = U_OUT2 + OUT_UNITS
E_BLOCKS = F_EXP // 512
ITEM_UNITS = 6 * E_BLOCKS
MAX_SECOND = (2 * T) // (P + 1)


def item_units():
    units = []
    for b in range(E_BLOCKS + 1):
        if b < E_BLOCKS:
            units += [("gate", b, 0), ("gate", b, 1), ("up", b, 0), ("up", b, 1)]
        if b >= 1:
            units += [("down", b - 1, 0), ("down", b - 1, 1)]
    return units


def trunk_kernel(nc, x, xT, ln_g, ln_b, w_in, gn_g, w_out, w_gate, w_up, w_down, w_qkv, bias_win,
                 w_out2, w_router, b_router, e_gate, e_up, e_down, tables, consts, out):
    ctx = ExitStack()
    with ctx:
        def sem(name):
            return ctx.enter_context(nc.semaphore(name))

        def sb(stack, name, shape, dt=F32):
            return stack.enter_context(nc.sbuf_tensor(name, shape, dt))

        raw = sb(ctx, "raw", [P, RAW, UC])
        w_hi = sb(ctx, "w_hi", [P, SPLIT, UC], F32R)
        w_lo = sb(ctx, "w_lo", [P, SPLIT, UC], F32R)
        x_tok = sb(ctx, "x_tok", [P, TT, D])
        xT_hi = sb(ctx, "xT_hi", [P, KC, T], F32R)
        xT_lo = sb(ctx, "xT_lo", [P, KC, T], F32R)
        norm_gb = sb(ctx, "norm_gb", [P, 2, D])
        cst = sb(ctx, "cst", [P, 6, P])
        small = sb(ctx, "small", [P, 64])
        ident, neg_tri, neg_ones, before, slots0, slots1 = (cst[:, n, :] for n in range(6))
        eps_col = small[:, 0:1]

        st = ExitStack()
        sb_qkT = sb(st, "sb_qkT", [P, 8, T])
        tokm = sb(st, "tokm", [P, TT, 5, 512])
        rot = sb(st, "rot", [P, TT, 4, 256])
        rot_t = sb(st, "rot_t", [P, 4, 256])
        ret_qkT = sb(st, "ret_qkT", [P, 8, T])
        sb_e = sb(st, "sb_e", [P, 2, 2, 384])
        sb_l = sb(st, "sb_l", [P, 2, 2, 384])
        sb_w = sb(st, "sb_w", [P, 2, 2, 384])
        ret_s = sb(st, "ret_s", [P, 2, 2, 384])
        xT_raw = ret_qkT
        oT_hi, oT_lo = xT_hi, xT_lo
        gn_row = rot_t[:, 0:2, :].rearrange("p a b -> p (a b)")
        ret_o = sb_l[:, :, :, :].rearrange("p a b c -> p (a b c)")[:, 0:1024].rearrange("p (t n) -> p t n", t=TT)
        ret_sq = sb_e[:, :, :, :].rearrange("p a b c -> p (a b c)")[:, 0:1024].rearrange("p (t n) -> p t n", t=TT)
        gn_s = small[:, 16:64].rearrange("p (a t h) -> p a t h", a=3, t=TT)
        st.close()
        st = ExitStack()
        hT_hi = sb(st, "hT_hi", [P, 2 * FF_BLOCKS, T], F32R)
        hT_lo = sb(st, "hT_lo", [P, 2 * FF_BLOCKS, T], F32R)
        ff_g = sb(st, "ff_g", [P, 2, 512])
        ff_h = sb(st, "ff_h", [P, 2, 512])
        st.close()
        st = ExitStack()
        c_qkT = sb(st, "c_qkT", [P, 16, T])
        c_v = sb(st, "c_v", [P, TT, D])
        c_bias = sb(st, "c_bias", [P, N_C, T])
        c_s = sb(st, "c_s", [P, 2, 2, 384])
        c_p = sb(st, "c_p", [P, 2, 2, 384])
        c_pT = sb(st, "c_pT", [P, 2, 2, 384])
        c_max = sb(st, "c_max", [P, 8, 2, 2])
        c_sum = sb(st, "c_sum", [P, 8, 2, 2])
        c_inv = sb(st, "c_inv", [P, 8, 2, 2])
        st.close()
        st = ExitStack()
        xk_hi = sb(st, "xk_hi", [P, TT, D], F32R)
        xk_lo = sb(st, "xk_lo", [P, TT, D], F32R)
        g_hi = sb(st, "g_hi", [P, KC, P], F32R)
        g_lo = sb(st, "g_lo", [P, KC, P], F32R)
        m_g = sb(st, "m_g", [P, 2, 512])
        m_h = sb(st, "m_h", [P, 2, 512])
        mT_hi = sb(st, "mT_hi", [P, 2, 4, P], F32R)
        mT_lo = sb(st, "mT_lo", [P, 2, 4, P], F32R)
        y_hi = sb(st, "y_hi", [P, D], F32R)
        y_lo = sb(st, "y_lo", [P, D], F32R)
        pick = sb(st, "pick", [P, TT, P])
        pick_r = sb(st, "pick_r", [P, TT, P], F32R)
        place_r = sb(st, "place_r", [P, TT, P], F32R)
        cur = sb(st, "cur", [P, 2, TT])
        route = sb(st, "route", [P, N_EXP, 2, TT])
        wr = sb(st, "wr", [P, KC, N_EXP])
        wr_hi = sb(st, "wr_hi", [P, KC, N_EXP], F32R)
        wr_lo = sb(st, "wr_lo", [P, KC, N_EXP], F32R)
        br = sb(st, "br", [P, N_EXP])
        logit = sb(st, "logit", [P, TT, N_EXP])
        gt = sb(st, "gt", [P, TT, N_EXP, N_EXP])
        eq = sb(st, "eq", [P, TT, N_EXP, N_EXP])
        tri8 = sb(st, "tri8", [P, 2, N_EXP, N_EXP])
        num8 = sb(st, "num8", [P, N_EXP])
        rank = sb(st, "rank", [P, TT, N_EXP])
        picked = sb(st, "picked", [P, TT, N_EXP])
        top = sb(st, "top", [P, 4, TT])
        ex = sb(st, "ex", [P, TT, N_EXP])
        over = sb(st, "over", [P, 4, N_EXP])
        second_f = sb(st, "second_f", [P, 4])
        second = sb(st, "second", [P, 4], I32)
        st.close()

        ps = ctx.enter_context(nc.psum_tensor("ps", [P, 8, 512], F32))

        def bank(n):
            return ps[:, n, :]

        raw_landed = [sem(f"raw_landed{n}") for n in range(RAW)]
        consts_landed = sem("consts_landed")
        xT_landed = sem("xT_landed")
        aux_landed = [sem(f"aux_landed{n}") for n in range(8)]
        hi_ready = sem("hi_ready")
        lo_ready = sem("lo_ready")
        unit_used = sem("unit_used")
        xT_hi_ready = sem("xT_hi_ready")
        xT_lo_ready = sem("xT_lo_ready")
        eps_ready = sem("eps_ready")
        in_done = sem("in_done")
        in_out = sem("in_out")
        rot_step = sem("rot_step")
        rot_done = sem("rot_done")
        ret_turned = sem("ret_turned")
        ret_qkT_ready = sem("ret_qkT_ready")
        sb_scored = sem("sb_scored")
        sb_abs = sem("sb_abs")
        sb_exp = sem("sb_exp")
        sb_log = sem("sb_log")
        sb_softplus = sem("sb_softplus")
        sb_l_masked = sem("sb_l_masked")
        sb_summed = sem("sb_summed")
        sb_weights = sem("sb_weights")
        sb_w_masked = sem("sb_w_masked")
        sb_pv = sem("sb_pv")
        oT_hi_ready = sem("oT_hi_ready")
        oT_lo_ready = sem("oT_lo_ready")
        ret_scored = sem("ret_scored")
        ret_copied = sem("ret_copied")
        ret_masked = sem("ret_masked")
        ret_pv = sem("ret_pv")
        gn_step = sem("gn_step")
        gn_sq = sem("gn_sq")
        gn_std = sem("gn_std")
        ret_out = sem("ret_out")
        ret_oT = sem("ret_oT")
        branch_done = [sem(f"branch_done{n}") for n in range(4)]
        ln_res = sem("ln_res")
        ln_step = sem("ln_step")
        ln_sum = sem("ln_sum")
        ln_sc = sem("ln_sc")
        ln_sq_done = sem("ln_sq_done")
        ln_std = sem("ln_std")
        ln_done = sem("ln_done")
        x_turned = sem("x_turned")
        ff_done = sem("ff_done")
        ff_silu = sem("ff_silu")
        ff_prod = sem("ff_prod")
        hT_hi_ready = sem("hT_hi_ready")
        hT_lo_ready = sem("hT_lo_ready")
        qkv_done = sem("qkv_done")
        qkv_out = sem("qkv_out")
        c_scored = sem("c_scored")
        c_biased = sem("c_biased")
        c_masked = sem("c_masked")
        c_maxed = sem("c_maxed")
        c_exped = sem("c_exped")
        c_recip = sem("c_recip")
        c_normed = sem("c_normed")
        c_turned = sem("c_turned")
        c_pT_ready = sem("c_pT_ready")
        c_pv = sem("c_pv")
        c_oT_hi = sem("c_oT_hi")
        c_oT_lo = sem("c_oT_lo")
        wr_split = sem("wr_split")
        xk_hi_ready = sem("xk_hi_ready")
        xk_lo_ready = sem("xk_lo_ready")
        logits_done = sem("logits_done")
        r_step = sem("r_step")
        r_exp = sem("r_exp")
        picked_ready = sem("picked_ready")
        slots_done = sem("slots_done")
        routed = sem("routed")
        pick_ready = sem("pick_ready")
        place_turned = sem("place_turned")
        place_ready = sem("place_ready")
        gathered = sem("gathered")
        g_hi_ready = sem("g_hi_ready")
        g_lo_ready = sem("g_lo_ready")
        gate_done = sem("gate_done")
        up_done = sem("up_done")
        m_silu = sem("m_silu")
        m_prod = sem("m_prod")
        m_turned = sem("m_turned")
        mT_hi_ready = sem("mT_hi_ready")
        mT_lo_ready = sem("mT_lo_ready")
        y_done = sem("y_done")
        y_hi_ready = sem("y_hi_ready")
        y_lo_ready = sem("y_lo_ready")
        scattered = sem("scattered")
        combined = sem("combined")
        stored = sem("stored")

        dense = []
        for c in range(IN_BLOCKS):
            for k in range(2):
                dense.append(w_in[k * 512:(k + 1) * 512, c * 512:(c + 1) * 512].rearrange("(k p) n -> p k n", p=P))
        for k in range(OUT_UNITS):
            dense.append(w_out[k * 256:(k + 1) * 256, :].rearrange("(k p) n -> p k n", p=P))
        for b in range(FF_BLOCKS):
            for w in (w_gate, w_up):
                dense.append(w[:, b * 256:(b + 1) * 256].rearrange("(k p) n -> p k n", p=P))
        for k in range(DOWN_UNITS):
            dense.append(w_down[k * 256:(k + 1) * 256, :].rearrange("(k p) n -> p k n", p=P))
        for c in range(QKV_BLOCKS):
            for k in range(2):
                dense.append(w_qkv[k * 512:(k + 1) * 512, c * 512:(c + 1) * 512].rearrange("(k p) n -> p k n", p=P))
        for k in range(OUT_UNITS):
            dense.append(w_out2[k * 256:(k + 1) * 256, :].rearrange("(k p) n -> p k n", p=P))
        assert len(dense) == U_MOE
        units = item_units()
        assert len(units) == ITEM_UNITS and ITEM_UNITS % RAW == 0 and ITEM_UNITS % SPLIT == 0

        def raw_slot(u, n):
            return raw[:, u % RAW, :].rearrange("p (k n) -> p k n", n=n)

        def hi_slot(u, n):
            return w_hi[:, u % SPLIT, :].rearrange("p (k n) -> p k n", n=n)

        def lo_slot(u, n):
            return w_lo[:, u % SPLIT, :].rearrange("p (k n) -> p k n", n=n)

        def landed(item, j):
            u = U_MOE + j
            return item * (16 * (ITEM_UNITS // RAW)) + 16 * (u // RAW + 1)

        block = ctx.enter_context(nc.Block())

        @block.sync
        def _(sp):
            def free(u):
                sp.wait_ge(lo_ready, u - RAW + 1)

            sp.dma_start(xT_raw[:, :, :], xT.rearrange("(k p) t -> p k t", p=P)).then_inc(xT_landed, 16)
            for u, src in enumerate(dense):
                if u >= RAW:
                    free(u)
                sp.dma_start(raw_slot(u, src.shape[2]), src).then_inc(raw_landed[u % RAW], 16)

            def load_item(item, e):
                for j, (kind, b, half) in enumerate(units):
                    u = U_MOE + j
                    free(item * ITEM_UNITS + u)
                    if kind == "down":
                        src = e_down[e, b * 512 + half * 256:b * 512 + (half + 1) * 256, :]
                        n = D
                    else:
                        w = e_gate if kind == "gate" else e_up
                        src = w[e, half * 512:(half + 1) * 512, b * 512:(b + 1) * 512]
                        n = 512
                    sp.dma_start(raw_slot(u, n), src.rearrange("(k p) n -> p k n", p=P)).then_inc(
                        raw_landed[u % RAW], 16)

            with sp.Fori(0, N_EXP) as item:
                load_item(item, item)
            sp.wait_ge(routed, 1)
            n_second = sp.value_load(second[0:1, 0:1], min_val=0, max_val=MAX_SECOND)
            with sp.Fori(0, MAX_SECOND) as s:
                with sp.If(n_second > s):
                    e = sp.value_load(second[0:1, bass.ds(s + 1, 1)], min_val=0, max_val=N_EXP - 1)
                    load_item(s + N_EXP, e)
            sp.wait_ge(ln_done, 4 * TT)
            sp.dma_start(out.rearrange("(t p) d -> p t d", p=P), x_tok[:, :, :]).then_inc(stored, 16)
            sp.wait_ge(stored, 16)

        @block.gpsimd
        def _(pool):
            pool.memset(eps_col, EPS).then_inc(eps_ready, 1)
            pool.dma_start(cst[:, :, :], consts).then_inc(consts_landed, 16)
            pool.dma_start(x_tok[:, :, :], x.rearrange("(t p) d -> p t d", p=P)).then_inc(aux_landed[0], 16)
            pool.dma_start(rot[:, :, :, :], tables).then_inc(aux_landed[1], 16)

            def load_norm(n):
                if n >= 1:
                    pool.wait_ge(ln_done, n * TT)
                pool.dma_start(norm_gb[:, 0, :], ln_g[n:n + 1, :].broadcast_to((P, D))).then_inc(aux_landed[2], 16)
                pool.dma_start(norm_gb[:, 1, :], ln_b[n:n + 1, :].broadcast_to((P, D))).then_inc(aux_landed[2], 16)

            load_norm(0)

            for qk in range(2):
                for t in range(TT):
                    n = 2 * qk + t
                    pool.wait_ge(in_out, 2 * (3 + qk) + t + 1)
                    if n == 0:
                        pool.wait_ge(aux_landed[1], 16)
                    else:
                        pool.wait_ge(rot_done, 2 * n)
                    v = tokm[:, t, 1 + qk, :].rearrange("p (h a f) -> p h a f", h=N_RET, a=2)
                    x1, x2 = v[:, :, 0, :], v[:, :, 1, :]
                    c = rot[:, t, 2 * qk, :].rearrange("p (h f) -> p h f", h=N_RET)
                    s = rot[:, t, 2 * qk + 1, :].rearrange("p (h f) -> p h f", h=N_RET)
                    w = [rot_t[:, m, :].rearrange("p (h f) -> p h f", h=N_RET) for m in range(4)]
                    pool.tensor_tensor(w[0], x1, c, ALU.mult).then_inc(rot_step, 1)
                    pool.tensor_tensor(w[1], x2, s, ALU.mult).then_inc(rot_step, 1)
                    pool.tensor_tensor(w[2], x1, s, ALU.mult).then_inc(rot_step, 1)
                    pool.tensor_tensor(w[3], x2, c, ALU.mult).then_inc(rot_step, 1)
                    pool.wait_ge(rot_step, 4 * (n + 1))
                    pool.tensor_tensor(x1, w[0], w[1], ALU.subtract).then_inc(rot_done, 1)
                    pool.tensor_tensor(x2, w[2], w[3], ALU.add).then_inc(rot_done, 1)
            pool.wait_ge(rot_done, 8)
            pool.dma_start(gn_row, gn_g.broadcast_to((P, 512))).then_inc(aux_landed[3], 16)

            def mask_diagonals(t, strict):
                for h in range(2):
                    v = t[:, h, :].rearrange("p (b q) -> p b q", q=P)[:, 0:3:2, :]
                    m = pool.affine_select(out=v, in_=v, compare_op=ALU.is_gt if strict else ALU.is_ge, fill=0.0,
                                           base=0, pattern=[[0, 2], [1, P]], channel_multiplier=-1)
                return m

            for p in range(4):
                pool.wait_ge(sb_softplus, p + 1)
                mask_diagonals(sb_l[:, p % 2], True).then_inc(sb_l_masked, 1)
                pool.wait_ge(ret_copied, p + 1)
                mask_diagonals(ret_s[:, p % 2], False).then_inc(ret_masked, 1)
                pool.wait_ge(sb_weights, p + 1)
                mask_diagonals(sb_w[:, p % 2], True).then_inc(sb_w_masked, 1)

            load_norm(1)

            pool.wait_ge(branch_done[1], 1)
            pool.dma_start(c_bias[:, :, :], bias_win).then_inc(aux_landed[4], 16)
            load_norm(2)
            for p in range(N_C // 2):
                pool.wait_ge(c_biased, 2 * (p + 1))
                pool.memset(c_s[0:CHUNK, p % 2, :, CHUNK:P], MASKED).then_inc(c_masked, 1)
                pool.memset(c_s[0:CHUNK, p % 2, :, 2 * P + CHUNK:3 * P], MASKED).then_inc(c_masked, 1)

            pool.wait_ge(branch_done[2], 1)
            pool.dma_start(wr[:, :, :], w_router.rearrange("(k p) e -> p k e", p=P)).then_inc(aux_landed[5], 16)
            pool.dma_start(br[:, :], b_router.broadcast_to((P, N_EXP))).then_inc(aux_landed[6], 16)
            pool.memset(tri8[:, :, :, :], 1.0).then_inc(r_step, 1)
            pool.iota(num8[:, :], pattern=[[1, N_EXP]], base=0, channel_multiplier=0,
                      allow_small_or_imprecise_dtypes=True).then_inc(r_step, 1)
            pool.wait_ge(r_step, 1)
            pool.affine_select(out=tri8[:, 0], in_=tri8[:, 0], compare_op=ALU.is_gt, fill=0.0, base=0,
                               pattern=[[1, N_EXP], [-1, N_EXP]], channel_multiplier=0).then_inc(r_step, 1)
            pool.affine_select(out=tri8[:, 1], in_=tri8[:, 1], compare_op=ALU.is_ge, fill=0.0, base=0,
                               pattern=[[1, N_EXP], [-1, N_EXP]], channel_multiplier=0).then_inc(r_step, 1)
            load_norm(3)

        @block.tensor
        def _(pe):
            def mm3(o, a, b, first, last):
                (a_hi, a_lo), (b_hi, b_lo) = a, b
                pe.matmul(o, a_hi, b_hi, start=first, stop=False, skip_group_check=True)
                pe.matmul(o, a_lo, b_hi, start=False, stop=False, skip_group_check=True)
                return pe.matmul(o, a_hi, b_lo, start=False, stop=last, skip_group_check=True)

            def split_ready(u):
                pe.wait_ge(hi_ready, u + 1)
                pe.wait_ge(lo_ready, u + 1)

            def project(c, u, scored, tokens):
                for k2 in range(2):
                    split_ready(u + k2)
                    hi, lo = hi_slot(u + k2, 512), lo_slot(u + k2, 512)
                    for o in range(2):
                        b = bank(2 * (c % 2) + o)
                        for kk in range(4):
                            k = 4 * k2 + kk
                            if tokens:
                                m = mm3(b, (xT_hi[:, k, o * P:(o + 1) * P], xT_lo[:, k, o * P:(o + 1) * P]),
                                        (hi[:, kk, :], lo[:, kk, :]), k == 0, k == KC - 1)
                            else:
                                for h in range(2):
                                    w = slice((2 * o + h) * P, (2 * o + h + 1) * P)
                                    m = mm3(b[:, h * T:(h + 1) * T], (hi[:, kk, w], lo[:, kk, w]),
                                            (xT_hi[:, k, :], xT_lo[:, k, :]), k == 0 and h == 0, k == KC - 1)
                        if k2 == 1:
                            if o == 0:
                                m.then_inc(scored, 1)
                    if k2 == 1:
                        done = m
                    else:
                        m.then_inc(unit_used, 1)
                return done

            def close_block(done, scored):
                pe.nop().then_inc(unit_used, 1)

            def rows(u, n_chunk, aT, first, last, done):
                split_ready(u)
                hi, lo = hi_slot(u, D), lo_slot(u, D)
                for kk in range(2):
                    k = n_chunk + kk
                    for t in range(TT):
                        a = (aT[0][:, k, t * P:(t + 1) * P], aT[1][:, k, t * P:(t + 1) * P])
                        for h in range(2):
                            m = mm3(bank(4 + 2 * t + h), a,
                                    (hi[:, kk, h * 512:(h + 1) * 512], lo[:, kk, h * 512:(h + 1) * 512]),
                                    first and kk == 0, last and kk == 1)
                m.then_inc(unit_used, 1)
                if last:
                    pe.wait_ge(unit_used, u + 1)
                    pe.nop().then_inc(done, 1)

            def turn_x(n):
                for t in range(TT):
                    pe.wait_ge(ln_done, TT * n + t + 1)
                    for k in range(KC):
                        m = pe.transpose(bank(k // 2)[:, (k % 2) * T + t * P:(k % 2) * T + (t + 1) * P],
                                         x_tok[:, t, k * P:(k + 1) * P], ident)
                        if t == TT - 1 and k % 2 == 1:
                            m.then_inc(x_turned, 1)

            for c in range(IN_BLOCKS):
                if c == 0:
                    pe.wait_ge(xT_hi_ready, 4)
                    pe.wait_ge(xT_lo_ready, 4)
                if c >= 2:
                    pe.wait_ge(in_out, 2 * (c - 1))
                m = project(c, U_IN + 2 * c, in_done, c >= 2)
                m.then_inc(in_done, 1)
                pe.wait_ge(in_done, 2 * (c + 1))
                pe.nop().then_inc(unit_used, 1)

            pe.wait_ge(consts_landed, 16)
            pe.wait_ge(rot_done, 8)
            for c in range(8):
                for t in range(TT):
                    m = pe.transpose(bank(4 + c // 2)[:, (c % 2) * T + t * P:(c % 2) * T + (t + 1) * P],
                                     tokm[:, t, 1 + c // 4, (c % 4) * P:(c % 4 + 1) * P], ident)
                if c % 2 == 1:
                    m.then_inc(ret_turned, 1)

            def scores(qT, kT, b0, done):
                for h in range(2):
                    q, k = qT[h * HD:(h + 1) * HD], kT[h * HD:(h + 1) * HD]
                    pe.matmul(bank(b0 + h)[:, 0:T], k[:, 0:P], q[:, 0:T], start=True, stop=True,
                              skip_group_check=True)
                    m = pe.matmul(bank(b0 + h)[:, T:T + P], k[:, P:T], q[:, P:T], start=False, stop=True,
                                  skip_group_check=True)
                m.then_inc(done, 1)

            def weighted(o, v0, v1, wt, done):
                for h in range(2):
                    r = slice(h * HD, (h + 1) * HD)
                    pe.matmul(o[r, 0:T], v0[:, r], wt[:, h, 0:T], start=True, stop=False, skip_group_check=True)
                    m = pe.matmul(o[r, P:T], v1[:, r], wt[:, h, T:T + P], start=False, stop=True,
                                  skip_group_check=True)
                m.then_inc(done, 1)

            def sb_scores(p):
                if p == 0:
                    pe.wait_ge(in_out, 2 * IN_BLOCKS)
                else:
                    pe.wait_ge(sb_weights, p)
                scores(sb_qkT[:, p, :], sb_qkT[:, 4 + p, :], 0, sb_scored)

            def ret_scores(p):
                if p == 0:
                    pe.wait_ge(ret_qkT_ready, 4)
                else:
                    pe.wait_ge(ret_copied, p)
                scores(ret_qkT[:, p, :], ret_qkT[:, 4 + p, :], 2, ret_scored)

            def sb_sums(p):
                pe.wait_ge(sb_l_masked, p + 1)
                for h in range(2):
                    b, sp_ = bank(h), sb_l[:, p % 2, h, :]
                    pe.matmul(b[:, 0:T], neg_tri, sp_[:, 0:T], start=False, stop=False, skip_group_check=True)
                    pe.matmul(b[:, P:T], neg_ones, sp_[:, T:T + P], start=False, stop=False, skip_group_check=True)
                    m = pe.matmul(b[:, T:T + P], neg_tri, sp_[:, T:T + P], start=False, stop=True,
                                  skip_group_check=True)
                m.then_inc(sb_summed, 1)

            def ret_values(p):
                pe.wait_ge(ret_masked, p + 1)
                for h in range(2):
                    n = 2 * p + h
                    c = slice(n * HD, (n + 1) * HD)
                    s = ret_s[:, p % 2, h, :]
                    pe.matmul(bank(6)[:, c], s[:, 0:P], tokm[:, 0, 3, c], start=n == 0, stop=True,
                              skip_group_check=True)
                    pe.matmul(bank(7)[:, c], s[:, P:T], tokm[:, 0, 3, c], start=n == 0, stop=False,
                              skip_group_check=True)
                    m = pe.matmul(bank(7)[:, c], s[:, T:T + P], tokm[:, 1, 3, c], start=False, stop=True,
                                  skip_group_check=True)
                m.then_inc(ret_pv, 1)

            sb_scores(0)
            ret_scores(0)
            for p in range(4):
                sb_sums(p)
                ret_values(p)
                if p < 3:
                    ret_scores(p + 1)
                pe.wait_ge(sb_w_masked, p + 1)
                if p >= 2:
                    pe.wait_ge(oT_lo_ready, p - 1)
                if p < 3:
                    sb_scores(p + 1)
                v = slice(p * P, (p + 1) * P)
                weighted(bank(4 + p % 2), tokm[:, 0, 0, v], tokm[:, 1, 0, v], sb_w[:, p % 2], sb_pv)

            for t in range(TT):
                pe.wait_ge(ret_out, t + 1)
                for c in range(4):
                    m = pe.transpose(bank(c // 2)[:, (c % 2) * T + t * P:(c % 2) * T + (t + 1) * P],
                                     ret_o[:, t, c * P:(c + 1) * P], ident)
                    if t == TT - 1 and c % 2 == 1:
                        m.then_inc(ret_oT, 1)

            for k in range(OUT_UNITS):
                pe.wait_ge(oT_lo_ready, 4 if k < 2 else 4 + (k - 1))
                rows(U_OUT + k, 2 * k, (oT_hi, oT_lo), k == 0, k == OUT_UNITS - 1, branch_done[0])
            turn_x(0)

            for b in range(FF_BLOCKS):
                if b == 0:
                    pe.wait_ge(xT_hi_ready, 8)
                    pe.wait_ge(xT_lo_ready, 8)
                if b >= 2:
                    pe.wait_ge(ff_prod, b - 1)
                for g in range(2):
                    u = U_FF + 2 * b + g
                    split_ready(u)
                    hi, lo = hi_slot(u, 256), lo_slot(u, 256)
                    for h in range(2):
                        for k in range(KC):
                            w = slice(h * P, (h + 1) * P)
                            m = mm3(bank(2 * (b % 2) + g)[:, h * T:(h + 1) * T], (hi[:, k, w], lo[:, k, w]),
                                    (xT_hi[:, k, :], xT_lo[:, k, :]), k == 0 and h == 0, k == KC - 1)
                    m.then_inc(unit_used, 1)
                    pe.wait_ge(unit_used, u + 1)
                    pe.nop().then_inc(ff_done, 1)
            for k in range(DOWN_UNITS):
                pe.wait_ge(hT_hi_ready, k + 1)
                pe.wait_ge(hT_lo_ready, k + 1)
                if k == 0:
                    pe.wait_ge(ln_res, 4)
                rows(U_DOWN + k, 2 * k, (hT_hi, hT_lo), k == 0, k == DOWN_UNITS - 1, branch_done[1])
            turn_x(1)

            for c in range(QKV_BLOCKS):
                if c == 0:
                    pe.wait_ge(xT_hi_ready, 12)
                    pe.wait_ge(xT_lo_ready, 12)
                if c >= 2:
                    pe.wait_ge(qkv_out, 2 * (c - 1))
                m = project(c, U_QKV + 2 * c, qkv_done, c >= 4)
                m.then_inc(qkv_done, 1)
                pe.wait_ge(qkv_done, 2 * (c + 1))
                pe.nop().then_inc(unit_used, 1)

            def c_scores(p):
                if p >= 2:
                    pe.wait_ge(c_biased, 2 * (p - 1))
                for h in range(2):
                    q, k = (c_qkT[h * HD:(h + 1) * HD, n, :] for n in (p, 8 + p))
                    b = bank(2 * (p % 2) + h)
                    pe.matmul(b[:, 0:P], q[:, 0:P], k[:, 0:P], start=True, stop=True, skip_group_check=True)
                    m = pe.matmul(b[:, P:P + T], q[:, P:T], k[:, 0:T], start=False, stop=True,
                                  skip_group_check=True)
                m.then_inc(c_scored, 1)

            def c_turn(p):
                pe.wait_ge(c_normed, 4 * (p + 1))
                if p >= 1:
                    pe.wait_ge(c_pT_ready, p)
                for h in range(2):
                    w = c_p[:, p % 2, h, :]
                    for s, d in ((0, 0), (1, 1), (2, 2)):
                        m = pe.transpose(bank(6 + h)[:, d * P:(d + 1) * P], w[:, s * P:(s + 1) * P], ident)
                m.then_inc(c_turned, 1)

            def c_values(p):
                pe.wait_ge(c_pT_ready, p + 1)
                if p >= 2:
                    pe.wait_ge(c_oT_lo, p - 1)
                v = slice(p * P, (p + 1) * P)
                weighted(bank(4 + p % 2), c_v[:, 0, v], c_v[:, 1, v], c_pT[:, p % 2], c_pv)

            pe.wait_ge(qkv_out, 2 * QKV_BLOCKS)
            pe.wait_ge(ln_res, 8)
            c_scores(0)
            for p in range(N_C // 2):
                if p + 1 < N_C // 2:
                    c_scores(p + 1)
                if p >= 1:
                    c_values(p - 1)
                c_turn(p)
            c_values(N_C // 2 - 1)
            for k in range(OUT_UNITS):
                pe.wait_ge(c_oT_lo, 8)
                rows(U_OUT2 + k, 2 * k, (oT_hi, oT_lo), k == 0, k == OUT_UNITS - 1, branch_done[2])
            turn_x(2)

            pe.wait_ge(xT_hi_ready, 16)
            pe.wait_ge(xT_lo_ready, 16)
            pe.wait_ge(wr_split, 2)
            pe.wait_ge(ln_res, 12)
            for t in range(TT):
                for k in range(KC):
                    m = mm3(bank(4)[:, t * N_EXP:(t + 1) * N_EXP],
                            (xT_hi[:, k, t * P:(t + 1) * P], xT_lo[:, k, t * P:(t + 1) * P]),
                            (wr_hi[:, k, :], wr_lo[:, k, :]), t == 0 and k == 0, k == KC - 1)
            m.then_inc(logits_done, 1)
            pe.wait_ge(picked_ready, 1)
            c5 = bank(5)
            pe.matmul(c5[:, 0:8], before, picked[:, 0, :], start=True, stop=True, skip_group_check=True)
            pe.matmul(c5[:, 8:16], before, picked[:, 1, :], start=False, stop=True, skip_group_check=True)
            pe.matmul(c5[:, 16:24], neg_ones, picked[:, 0, :], start=False, stop=True, skip_group_check=True)
            m = pe.matmul(c5[:, 24:32], neg_ones, picked[:, 1, :], start=False, stop=True, skip_group_check=True)
            m.then_inc(slots_done, 1)

            def run_item(item):
                base = item * ITEM_UNITS + U_MOE
                blocks = item * E_BLOCKS

                pe.wait_ge(pick_ready, item * 3 + 3)
                for part, xk in enumerate((xk_hi, xk_lo)):
                    for k in range(KC):
                        for t in range(TT):
                            m = pe.matmul(bank(2 * part + k // 4)[:, (k % 4) * P:(k % 4 + 1) * P],
                                          xk[:, t, k * P:(k + 1) * P], pick_r[:, t, :],
                                          start=k % 4 == 0 and t == 0, stop=t == TT - 1, skip_group_check=True)
                        if k % 4 == 3:
                            m.then_inc(gathered, 1)
                for t in range(TT):
                    m = pe.transpose(bank(6)[:, t * P:(t + 1) * P], pick[:, t, :], ident)
                m.then_inc(place_turned, 1)

                def first_product(j, b, g, done):
                    for k2 in range(2):
                        u = j + k2
                        pe.wait_ge(hi_ready, base + (u + 1))
                        pe.wait_ge(lo_ready, base + (u + 1))
                        hi, lo = hi_slot(U_MOE + u, 512), lo_slot(U_MOE + u, 512)
                        for kk in range(4):
                            k = 4 * k2 + kk
                            m = mm3(bank(2 * (b % 2) + g), (g_hi[:, k, :], g_lo[:, k, :]),
                                    (hi[:, kk, :], lo[:, kk, :]), k == 0, k == KC - 1)
                        if k2 == 0:
                            m.then_inc(unit_used, 1)
                    m.then_inc(done, 1)
                    pe.wait_ge(done, blocks + (b + 1))
                    pe.nop().then_inc(unit_used, 1)

                j = 0
                for b in range(E_BLOCKS + 1):
                    if b < E_BLOCKS:
                        if b < 2:
                            pe.wait_ge(g_hi_ready, item * 2 + 2)
                            pe.wait_ge(g_lo_ready, item * 2 + 2)
                        else:
                            pe.wait_ge(m_prod, blocks + (b - 1))
                        first_product(j, b, 0, gate_done)
                        j += 2
                    if b >= 1:
                        pe.wait_ge(m_prod, blocks + b)
                        if b == 1:
                            pe.wait_ge(place_ready, item + 1)
                        if b >= 3:
                            pe.wait_ge(mT_lo_ready, blocks + (b - 2))
                        for c in range(4):
                            m = pe.transpose(bank(6 + (b - 1) % 2)[:, c * P:(c + 1) * P],
                                             m_h[:, (b - 1) % 2, c * P:(c + 1) * P], ident)
                        m.then_inc(m_turned, 1)
                    if b < E_BLOCKS:
                        first_product(j, b, 1, up_done)
                        j += 2
                    if b >= 1:
                        pe.wait_ge(mT_hi_ready, blocks + b)
                        pe.wait_ge(mT_lo_ready, blocks + b)
                        for k2 in range(2):
                            u = j + k2
                            pe.wait_ge(hi_ready, base + (u + 1))
                            pe.wait_ge(lo_ready, base + (u + 1))
                            hi, lo = hi_slot(U_MOE + u, D), lo_slot(U_MOE + u, D)
                            for kk in range(2):
                                c = 2 * k2 + kk
                                for h in range(2):
                                    m = mm3(bank(4 + h), (mT_hi[:, (b - 1) % 2, c, :], mT_lo[:, (b - 1) % 2, c, :]),
                                            (hi[:, kk, h * 512:(h + 1) * 512], lo[:, kk, h * 512:(h + 1) * 512]),
                                            b == 1 and c == 0, b == E_BLOCKS and c == 3)
                            m.then_inc(unit_used, 1)
                        j += 2
                pe.wait_ge(unit_used, base + ITEM_UNITS)
                pe.nop().then_inc(y_done, 1)

                pe.wait_ge(y_hi_ready, item * 2 + 2)
                pe.wait_ge(y_lo_ready, item * 2 + 2)
                for t in range(TT):
                    for h in range(2):
                        b = bank(2 * t + h)
                        pe.matmul(b, place_r[:, t, :], y_hi[:, h * 512:(h + 1) * 512], start=True, stop=False,
                                  skip_group_check=True)
                        m = pe.matmul(b, place_r[:, t, :], y_lo[:, h * 512:(h + 1) * 512], start=False, stop=True,
                                      skip_group_check=True)
                        m.then_inc(scattered, 1)
                pe.wait_ge(combined, item * 4 + (4 + TT))

            with pe.Fori(0, N_EXP) as item:
                run_item(item)
            pe.wait_ge(routed, 1)
            n_second = pe.value_load(second[0:1, 0:1], min_val=0, max_val=MAX_SECOND)
            with pe.Fori(0, MAX_SECOND) as s:
                with pe.If(n_second > s):
                    run_item(s + N_EXP)

        @block.scalar
        def _(act):
            def round_unit(u):
                act.wait_ge(raw_landed[u % RAW], 16 * (u // RAW + 1))
                if u >= SPLIT:
                    act.wait_ge(unit_used, u - SPLIT + 1)
                act.activation(w_hi[:, u % SPLIT, :], raw[:, u % RAW, :], ACT.Copy).then_inc(hi_ready, 1)

            def copy(o, i, s, scale=1.0):
                act.activation(o, i, ACT.Copy, scale=scale).then_inc(s, 1)

            act.wait_ge(xT_landed, 16)
            for j in range(4):
                copy(xT_hi[:, 2 * j:2 * j + 2, :], xT_raw[:, 2 * j:2 * j + 2, :], xT_hi_ready)
            for u in range(SPLIT):
                round_unit(u)

            for c in range(IN_BLOCKS):
                for o in range(2):
                    act.wait_ge(in_done, 2 * c + o + 1)
                    b = bank(2 * (c % 2) + o)
                    if c < 2:
                        dst = sb_qkT[:, 4 * c + 2 * o:4 * c + 2 * o + 2, :].rearrange("p a t -> p (a t)")
                        copy(dst, b, in_out, HD ** -0.5 if c == 0 else 1.0)
                    elif c < 6:
                        copy(tokm[:, o, c - 2, :], b, in_out)
                    else:
                        act.activation(tokm[:, o, 4, :], b, ACT.Silu).then_inc(in_out, 1)
                for k2 in range(2):
                    round_unit(U_IN + 2 * c + k2 + SPLIT)
            for j in range(4):
                act.wait_ge(ret_turned, j + 1)
                copy(ret_qkT[:, 2 * j:2 * j + 2, :].rearrange("p a t -> p (a t)"), bank(4 + j), ret_qkT_ready)

            for p in range(4):
                e = sb_e[:, p % 2]
                act.wait_ge(sb_scored, p + 1)
                act.activation(e, ps[:, 0:2, 0:384], ACT.Abs).then_inc(sb_abs, 1)
                act.wait_ge(sb_abs, p + 1)
                act.activation(e, e, ACT.Exp, scale=-1.0).then_inc(sb_exp, 1)
                act.wait_ge(sb_exp, p + 1)
                act.activation(e, e, ACT.Ln, bias=1.0).then_inc(sb_log, 1)
                act.wait_ge(sb_summed, p + 1)
                if p >= 2:
                    act.wait_ge(sb_pv, p - 1)
                act.activation(sb_w[:, p % 2], ps[:, 0:2, 0:384], ACT.Exp).then_inc(sb_weights, 1)
                act.wait_ge(sb_pv, p + 1)
                copy(oT_hi[:, p, :], bank(4 + p % 2)[:, 0:T], oT_hi_ready)

            for t in range(TT):
                act.wait_ge(gn_step, 2 * t + 2)
                act.activation(ret_sq[:, t, :], ret_o[:, t, :], ACT.Square).then_inc(gn_sq, 1)
            for t in range(TT):
                act.wait_ge(gn_step, 4 + t + 1)
                act.activation(gn_s[:, 2, t, :], gn_s[:, 1, t, :], ACT.Sqrt, scale=1.0 / HD,
                               bias=eps_col).then_inc(gn_std, 1)
            for j in range(2):
                act.wait_ge(ret_oT, j + 1)
                copy(oT_hi[:, 4 + 2 * j:6 + 2 * j, :].rearrange("p a t -> p (a t)"), bank(j), oT_hi_ready)
            for k in range(OUT_UNITS):
                round_unit(U_OUT + k + SPLIT)

            def norm(n):
                for t in range(TT):
                    act.wait_ge(ln_step, 4 * n + t + 1)
                    act.activation(ps[:, 2 * t:2 * t + 2, :], x_tok[:, t, :].rearrange("p (a b) -> p a b", a=2),
                                   ACT.Square, bias=small[:, 4 + t:5 + t], accum_out=small[:, 6 + t:7 + t]
                                   ).then_inc(ln_sq_done, 1)
                for t in range(TT):
                    act.wait_ge(ln_sq_done, TT * n + t + 1)
                    act.activation(small[:, 8 + t:9 + t], small[:, 6 + t:7 + t], ACT.Sqrt, scale=1.0 / D,
                                   bias=eps_col).then_inc(ln_std, 1)

            def split_xT(n):
                for j in range(4):
                    act.wait_ge(x_turned, 4 * n + j + 1)
                    copy(xT_hi[:, 2 * j:2 * j + 2, :].rearrange("p a t -> p (a t)"), bank(j), xT_hi_ready)

            act.wait_ge(eps_ready, 1)
            norm(0)
            split_xT(0)

            def ff_hi(b):
                act.wait_ge(ff_prod, b + 1)
                copy(hT_hi[:, 2 * b:2 * b + 2, :].rearrange("p a t -> p (a t)"), ff_h[:, b % 2, :], hT_hi_ready)

            for b in range(FF_BLOCKS):
                act.wait_ge(ff_done, 2 * b + 1)
                if b >= 2:
                    act.wait_ge(ff_prod, b - 1)
                act.activation(ff_g[:, b % 2, :], bank(2 * (b % 2)), ACT.Silu).then_inc(ff_silu, 1)
                round_unit(U_FF + 2 * b + SPLIT)
                if b >= 1:
                    ff_hi(b - 1)
                round_unit(U_FF + 2 * b + 1 + SPLIT)
            ff_hi(FF_BLOCKS - 1)
            for k in range(DOWN_UNITS):
                round_unit(U_DOWN + k + SPLIT)
            norm(1)
            split_xT(1)

            for c in range(QKV_BLOCKS):
                for o in range(2):
                    act.wait_ge(qkv_done, 2 * c + o + 1)
                    b = bank(2 * (c % 2) + o)
                    if c < 4:
                        copy(c_qkT[:, 4 * c + 2 * o:4 * c + 2 * o + 2, :].rearrange("p a t -> p (a t)"), b, qkv_out)
                    else:
                        copy(c_v[:, o, (c - 4) * 512:(c - 3) * 512], b, qkv_out)
                for k2 in range(2):
                    round_unit(U_QKV + 2 * c + k2 + SPLIT)

            def c_tail(p):
                act.wait_ge(c_turned, p + 1)
                if p >= 2:
                    act.wait_ge(c_pv, p - 1)
                copy(c_pT[:, p % 2], ps[:, 6:8, 0:384], c_pT_ready)
                act.wait_ge(c_pv, p + 1)
                copy(oT_hi[:, p, :], bank(4 + p % 2)[:, 0:T], c_oT_hi)

            for p in range(N_C // 2):
                act.wait_ge(c_maxed, 2 * (p + 1))
                if p >= 2:
                    act.wait_ge(c_turned, p - 1)
                for h in range(2):
                    for t, s in ((0, slice(0, P)), (1, slice(P, P + T))):
                        act.activation(c_p[:, p % 2, h, s], c_s[:, p % 2, h, s], ACT.Exp,
                                       bias=c_max[:, p, h, t:t + 1], accum_out=c_sum[:, p, h, t:t + 1]
                                       ).then_inc(c_exped, 1)
                if p >= 1:
                    c_tail(p - 1)
            c_tail(N_C // 2 - 1)
            for k in range(OUT_UNITS):
                round_unit(U_OUT2 + k + SPLIT)
            norm(2)
            for t in range(TT):
                act.wait_ge(ln_done, 2 * TT + TT)
                copy(xk_hi[:, t, :], x_tok[:, t, :], xk_hi_ready)
            act.wait_ge(aux_landed[5], 16)
            copy(wr_hi[:, :, :], wr[:, :, :], wr_split)
            split_xT(2)
            act.wait_ge(r_step, 4 + 3)
            for t in range(TT):
                act.activation(ex[:, t, :], logit[:, t, :], ACT.Exp, bias=top[:, 0, t:t + 1]).then_inc(r_exp, 1)

            def item_round(item, j):
                u = U_MOE + j
                act.wait_ge(raw_landed[u % RAW], landed(item, j))
                act.wait_ge(unit_used, item * ITEM_UNITS + (u - SPLIT + 1))
                act.activation(w_hi[:, u % SPLIT, :], raw[:, u % RAW, :], ACT.Copy).then_inc(hi_ready, 1)

            def run_item(item, carried, carries):
                blocks = item * E_BLOCKS

                def used(j):
                    if j + SPLIT < ITEM_UNITS:
                        item_round(item, j + SPLIT)
                    elif carries:
                        item_round(item + 1, j + SPLIT - ITEM_UNITS)

                for h in range(2):
                    act.wait_ge(gathered, item * 4 + (h + 1))
                    copy(g_hi[:, 4 * h:4 * h + 4, :].rearrange("p a t -> p (a t)"), bank(h), g_hi_ready)
                act.wait_ge(place_turned, item + 1)
                copy(place_r[:, :, :].rearrange("p a t -> p (a t)"), bank(6)[:, 0:T], place_ready)
                if not carried:
                    for j in range(SPLIT):
                        item_round(item, j)
                j = 0
                for b in range(E_BLOCKS + 1):
                    if b < E_BLOCKS:
                        used(j)
                        used(j + 1)
                        j += 2
                    if b >= 1:
                        act.wait_ge(m_turned, blocks + b)
                        copy(mT_hi[:, (b - 1) % 2].rearrange("p a t -> p (a t)"), bank(6 + (b - 1) % 2), mT_hi_ready)
                    if b < E_BLOCKS:
                        act.wait_ge(gate_done, blocks + (b + 1))
                        act.activation(m_g[:, b % 2, :], bank(2 * (b % 2)), ACT.Silu).then_inc(m_silu, 1)
                        used(j)
                        used(j + 1)
                        j += 2
                    if b >= 1:
                        used(j)
                        used(j + 1)
                        j += 2
                act.wait_ge(y_done, item + 1)
                for h in range(2):
                    copy(y_hi[:, h * 512:(h + 1) * 512], bank(4 + h), y_hi_ready)

            with act.Fori(0, N_EXP - 1) as item:
                run_item(item, True, True)
            run_item(N_EXP - 1, True, False)
            act.wait_ge(routed, 1)
            n_second = act.value_load(second[0:1, 0:1], min_val=0, max_val=MAX_SECOND)
            with act.Fori(0, MAX_SECOND) as s:
                with act.If(n_second > s):
                    run_item(s + N_EXP, False, False)
            norm(3)

        @block.vector
        def _(dve):
            def rest_unit(u):
                dve.wait_ge(hi_ready, u + 1)
                dve.tensor_tensor(w_lo[:, u % SPLIT, :], raw[:, u % RAW, :], w_hi[:, u % SPLIT, :].bitcast(F32),
                                  ALU.subtract).then_inc(lo_ready, 1)

            def rest(o, i, hi, s):
                dve.tensor_tensor(o, i, hi.bitcast(F32), ALU.subtract).then_inc(s, 1)

            for j in range(4):
                dve.wait_ge(xT_hi_ready, j + 1)
                rest(xT_lo[:, 2 * j:2 * j + 2, :], xT_raw[:, 2 * j:2 * j + 2, :], xT_hi[:, 2 * j:2 * j + 2, :], xT_lo_ready)
            for u in range(2 * IN_BLOCKS + SPLIT):
                rest_unit(u)

            for p in range(4):
                z = ps[:, 0:2, 0:384]
                dve.wait_ge(ret_scored, p + 1)
                if p >= 2:
                    dve.wait_ge(ret_pv, p - 1)
                dve.tensor_copy(ret_s[:, p % 2], ps[:, 2:4, 0:384]).then_inc(ret_copied, 1)
                dve.wait_ge(sb_log, p + 1)
                if p >= 2:
                    dve.wait_ge(sb_summed, p - 1)
                dve.scalar_tensor_tensor(out=sb_l[:, p % 2], in0=z, scalar=0.0, in1=sb_e[:, p % 2], op0=ALU.max,
                                         op1=ALU.add).then_inc(sb_softplus, 1)
                dve.wait_ge(oT_hi_ready, p + 1)
                rest(oT_lo[:, p, :], bank(4 + p % 2)[:, 0:T], oT_hi[:, p, :], oT_lo_ready)

            def heads(v):
                return v.rearrange("p (h d) -> p h d", d=HD)

            def per_head(v):
                return v.unsqueeze(2).broadcast_to((P, N_RET, HD))

            dve.wait_ge(ret_pv, 4)
            for t in range(TT):
                dve.tensor_reduce(gn_s[:, 0, t, :], heads(bank(6 + t)), AX, ALU.add).then_inc(gn_step, 1)
                dve.wait_ge(gn_step, 2 * t + 1)
                dve.scalar_tensor_tensor(out=heads(ret_o[:, t, :]), in0=per_head(gn_s[:, 0, t, :]),
                                         scalar=-1.0 / HD, in1=heads(bank(6 + t)), op0=ALU.mult,
                                         op1=ALU.add).then_inc(gn_step, 1)
            for t in range(TT):
                dve.wait_ge(gn_sq, t + 1)
                dve.tensor_reduce(gn_s[:, 1, t, :], heads(ret_sq[:, t, :]), AX, ALU.add).then_inc(gn_step, 1)
            dve.wait_ge(aux_landed[3], 16)
            n = 4 + TT
            for t in range(TT):
                dve.wait_ge(gn_std, t + 1)
                dve.reciprocal(gn_s[:, 0, t, :], gn_s[:, 2, t, :]).then_inc(gn_step, 1)
                n += 1
                dve.wait_ge(gn_step, n)
                dve.tensor_tensor(heads(ret_o[:, t, :]), heads(ret_o[:, t, :]), per_head(gn_s[:, 0, t, :]),
                                  ALU.mult).then_inc(gn_step, 1)
                n += 1
                dve.wait_ge(gn_step, n)
                dve.tensor_tensor(ret_o[:, t, :], ret_o[:, t, :], gn_row, ALU.mult).then_inc(gn_step, 1)
                n += 1
                dve.wait_ge(gn_step, n)
                dve.tensor_tensor(ret_o[:, t, :], ret_o[:, t, :], tokm[:, t, 4, :], ALU.mult).then_inc(ret_out, 1)
            for j in range(2):
                dve.wait_ge(oT_hi_ready, 4 + j + 1)
                c = slice(4 + 2 * j, 6 + 2 * j)
                rest(oT_lo[:, c, :].rearrange("p a t -> p (a t)"), bank(j),
                     oT_hi[:, c, :].rearrange("p a t -> p (a t)"), oT_lo_ready)
            for k in range(OUT_UNITS):
                rest_unit(U_OUT + k + SPLIT)

            def norm(n, branch):
                if branch:
                    dve.wait_ge(branch_done[n], 1)
                    for t in range(TT):
                        for h in range(2):
                            s = x_tok[:, t, h * 512:(h + 1) * 512]
                            if n == 0 and t == 0 and h == 0:
                                dve.wait_ge(aux_landed[0], 16)
                            dve.scalar_tensor_tensor(out=s, in0=s, scalar=ALPHA, in1=bank(4 + 2 * t + h),
                                                     op0=ALU.mult, op1=ALU.add).then_inc(ln_res, 1)
                    dve.wait_ge(ln_res, 4 * (n + 1))
                k = 4 * n
                for t in range(TT):
                    dve.tensor_reduce(small[:, 1 + t:2 + t], x_tok[:, t, :], AX, ALU.add).then_inc(ln_sum, 1)
                for t in range(TT):
                    dve.wait_ge(ln_sum, TT * n + t + 1)
                    dve.tensor_scalar(small[:, 4 + t:5 + t], small[:, 1 + t:2 + t], -1.0 / D, None,
                                      ALU.mult).then_inc(ln_step, 1)
                for t in range(TT):
                    dve.wait_ge(ln_std, TT * n + t + 1)
                    dve.reciprocal(small[:, 10 + t:11 + t], small[:, 8 + t:9 + t]).then_inc(ln_step, 1)
                dve.wait_ge(aux_landed[2], 32 * (n + 1))
                for t in range(TT):
                    dve.wait_ge(ln_step, k + 2 + t + 1)
                    dve.tensor_scalar(x_tok[:, t, :], x_tok[:, t, :], small[:, 4 + t:5 + t], small[:, 10 + t:11 + t],
                                      ALU.add, ALU.mult).then_inc(ln_sc, 1)
                    dve.wait_ge(ln_sc, 2 * (TT * n + t) + 1)
                    dve.tensor_tensor(x_tok[:, t, :], x_tok[:, t, :], norm_gb[:, 0, :], ALU.mult).then_inc(ln_sc, 1)
                    dve.wait_ge(ln_sc, 2 * (TT * n + t) + 2)
                    dve.tensor_tensor(x_tok[:, t, :], x_tok[:, t, :], norm_gb[:, 1, :], ALU.add).then_inc(ln_done, 1)

            def split_xT(n):
                for j in range(4):
                    dve.wait_ge(xT_hi_ready, 4 * (n + 1) + j + 1)
                    c = slice(2 * j, 2 * j + 2)
                    rest(xT_lo[:, c, :].rearrange("p a t -> p (a t)"), bank(j),
                         xT_hi[:, c, :].rearrange("p a t -> p (a t)"), xT_lo_ready)

            norm(0, True)
            split_xT(0)

            def ff_lo(b):
                dve.wait_ge(hT_hi_ready, b + 1)
                c = slice(2 * b, 2 * b + 2)
                rest(hT_lo[:, c, :].rearrange("p a t -> p (a t)"), ff_h[:, b % 2, :],
                     hT_hi[:, c, :].rearrange("p a t -> p (a t)"), hT_lo_ready)

            for b in range(FF_BLOCKS):
                rest_unit(U_FF + 2 * b + SPLIT)
                if b >= 1:
                    ff_lo(b - 1)
                dve.wait_ge(ff_silu, b + 1)
                dve.wait_ge(ff_done, 2 * b + 2)
                dve.tensor_tensor(ff_h[:, b % 2, :], ff_g[:, b % 2, :], bank(2 * (b % 2) + 1),
                                  ALU.mult).then_inc(ff_prod, 1)
                rest_unit(U_FF + 2 * b + 1 + SPLIT)
            ff_lo(FF_BLOCKS - 1)
            for k in range(DOWN_UNITS):
                rest_unit(U_DOWN + k + SPLIT)
            norm(1, True)
            split_xT(1)
            for u in range(U_QKV, U_OUT2):
                rest_unit(u + SPLIT)

            def c_lo(p):
                dve.wait_ge(c_oT_hi, p + 1)
                rest(oT_lo[:, p, :], bank(4 + p % 2)[:, 0:T], oT_hi[:, p, :], c_oT_lo)

            dve.wait_ge(aux_landed[4], 16)
            for p in range(N_C // 2):
                b0 = 2 * (p % 2)
                dve.wait_ge(c_scored, p + 1)
                if p >= 2:
                    dve.wait_ge(c_exped, 4 * (p - 1))
                bias = c_bias[:, 2 * p:2 * p + 2, :]
                dve.scalar_tensor_tensor(out=c_s[:, p % 2, :, 0:P], in0=ps[:, b0:b0 + 2, 0:P], scalar=HD ** -0.5,
                                         in1=bias[:, :, P:T], op0=ALU.mult, op1=ALU.add).then_inc(c_biased, 1)
                dve.scalar_tensor_tensor(out=c_s[:, p % 2, :, P:P + T], in0=ps[:, b0:b0 + 2, P:P + T],
                                         scalar=HD ** -0.5, in1=bias, op0=ALU.mult, op1=ALU.add).then_inc(c_biased, 1)
                dve.wait_ge(c_masked, 2 * (p + 1))
                dve.tensor_reduce(c_max[:, p, :, 0], c_s[:, p % 2, :, 0:P], AX, ALU.max,
                                  negate=True).then_inc(c_maxed, 1)
                dve.tensor_reduce(c_max[:, p, :, 1], c_s[:, p % 2, :, P:P + T], AX, ALU.max,
                                  negate=True).then_inc(c_maxed, 1)
                if p >= 1:
                    c_lo(p - 2) if p >= 2 else None
                dve.wait_ge(c_exped, 4 * (p + 1))
                dve.reciprocal(c_inv[:, p], c_sum[:, p]).then_inc(c_recip, 1)
                dve.wait_ge(c_recip, p + 1)
                for h in range(2):
                    for t, s in ((0, slice(0, P)), (1, slice(P, P + T))):
                        dve.tensor_scalar(c_p[:, p % 2, h, s], c_p[:, p % 2, h, s], c_inv[:, p, h, t:t + 1], None,
                                          ALU.mult).then_inc(c_normed, 1)
            c_lo(N_C // 2 - 2)
            c_lo(N_C // 2 - 1)
            for k in range(OUT_UNITS):
                rest_unit(U_OUT2 + k + SPLIT)
            norm(2, True)

            for t in range(TT):
                dve.wait_ge(xk_hi_ready, t + 1)
                rest(xk_lo[:, t, :], x_tok[:, t, :], xk_hi[:, t, :], xk_lo_ready)
            dve.wait_ge(wr_split, 1)
            rest(wr_lo[:, :, :], wr[:, :, :], wr_hi[:, :, :], wr_split)
            split_xT(2)
            done = [4]

            def step(i):
                i.then_inc(r_step, 1)
                done[0] += 1
                dve.wait_ge(r_step, done[0])

            dve.wait_ge(x_turned, 12)
            for t in range(TT):
                dve.wait_ge(xk_lo_ready, t + 1)
                dve.tensor_scalar(x_tok[:, t, :], x_tok[:, t, :], ALPHA, None, ALU.mult).then_inc(combined, 1)
            dve.wait_ge(logits_done, 1)
            dve.wait_ge(aux_landed[6], 16)
            dve.wait_ge(r_step, 4)
            step(dve.tensor_tensor(logit[:, :, :], bank(4)[:, 0:TT * N_EXP].rearrange("p (t e) -> p t e", t=TT),
                                   br[:, :].unsqueeze(1).broadcast_to((P, TT, N_EXP)), ALU.add))
            step(dve.tensor_reduce(top[:, 0, :], logit[:, :, :], AX, ALU.max, negate=True))
            step(dve.tensor_copy(top[:, 1, :], top[:, 0, :]))
            for t in range(TT):
                lj = logit[:, t, :].unsqueeze(1).broadcast_to((P, N_EXP, N_EXP))
                le = logit[:, t, :].unsqueeze(2).broadcast_to((P, N_EXP, N_EXP))
                step(dve.tensor_tensor(gt[:, t], lj, le, ALU.is_gt))
                step(dve.tensor_tensor(eq[:, t], lj, le, ALU.is_equal))
                step(dve.tensor_tensor(eq[:, t], eq[:, t], tri8[:, 0], ALU.mult))
                step(dve.tensor_tensor(gt[:, t], gt[:, t], eq[:, t], ALU.add))
                step(dve.tensor_reduce(rank[:, t, :], gt[:, t], AX, ALU.add))
            dve.tensor_scalar(picked[:, :, :], rank[:, :, :], 2.0, None, ALU.is_lt).then_inc(picked_ready, 1)
            dve.wait_ge(picked_ready, 1)
            dve.wait_ge(r_exp, 2)
            step(dve.tensor_tensor(ex[:, :, :], ex[:, :, :], picked[:, :, :], ALU.mult))
            step(dve.tensor_reduce(top[:, 2, :], ex[:, :, :], AX, ALU.add))
            step(dve.reciprocal(top[:, 3, :], top[:, 2, :]))
            for t in range(TT):
                step(dve.tensor_scalar(route[:, :, 1, t], ex[:, t, :], top[:, 3, t:t + 1], None, ALU.mult))
            dve.wait_ge(slots_done, 1)
            c5 = bank(5)
            step(dve.tensor_copy(over[:, 0, :], c5[:, 16:24]))
            step(dve.tensor_tensor(over[:, 1, :], over[:, 0, :], c5[:, 24:32], ALU.add))
            step(dve.scalar_tensor_tensor(out=rank[:, 0, :], in0=c5[:, 0:8], scalar=1.0, in1=picked[:, 0, :],
                                          op0=ALU.add, op1=ALU.mult))
            step(dve.tensor_tensor(rank[:, 1, :], c5[:, 8:16], over[:, 0, :], ALU.subtract))
            step(dve.scalar_tensor_tensor(out=rank[:, 1, :], in0=rank[:, 1, :], scalar=1.0, in1=picked[:, 1, :],
                                          op0=ALU.add, op1=ALU.mult))
            for t in range(TT):
                step(dve.tensor_scalar(route[:, :, 0, t], rank[:, t, :], -1.0, None, ALU.add))
            step(dve.tensor_scalar(over[:, 2, :], over[:, 1, :], -float(P), None, ALU.is_lt))
            step(dve.tensor_tensor(gt[:, 0], over[:, 2, :].unsqueeze(1).broadcast_to((P, N_EXP, N_EXP)),
                                   tri8[:, 1], ALU.mult))
            step(dve.tensor_reduce(over[:, 3, :], gt[:, 0], AX, ALU.add))
            step(dve.tensor_reduce(second_f[:, 0:1], over[:, 2, :], AX, ALU.add))
            for s in range(MAX_SECOND):
                step(dve.scalar_tensor_tensor(out=over[:, 0, :], in0=over[:, 3, :], scalar=float(s + 1),
                                              in1=over[:, 2, :], op0=ALU.is_equal, op1=ALU.mult))
                step(dve.tensor_tensor(over[:, 0, :], over[:, 0, :], num8[:, :], ALU.mult))
                step(dve.tensor_reduce(second_f[:, s + 1:s + 2], over[:, 0, :], AX, ALU.add))
            dve.tensor_copy(second[:, :], second_f[:, :]).then_inc(routed, 1)

            def item_rest(item, j):
                u = U_MOE + j
                dve.wait_ge(hi_ready, item * ITEM_UNITS + (u + 1))
                dve.tensor_tensor(w_lo[:, u % SPLIT, :], raw[:, u % RAW, :], w_hi[:, u % SPLIT, :].bitcast(F32),
                                  ALU.subtract).then_inc(lo_ready, 1)

            def run_item(item, e, slots, carried, carries):
                blocks = item * E_BLOCKS

                def used(j):
                    if j + SPLIT < ITEM_UNITS:
                        item_rest(item, j + SPLIT)
                    elif carries:
                        item_rest(item + 1, j + SPLIT - ITEM_UNITS)

                dve.wait_ge(combined, item * 4 + TT)
                dve.tensor_copy(cur[:, :, :], route[:, bass.ds(e, 1), :, :].rearrange("p a b t -> p (a b) t")).then_inc(pick_ready, 1)
                dve.wait_ge(pick_ready, item * 3 + 1)
                for t in range(TT):
                    m = dve.tensor_scalar(pick[:, t, :], slots, cur[:, 0, t:t + 1], None, ALU.is_equal)
                m.then_inc(pick_ready, 1)
                for t in range(TT):
                    m = dve.tensor_scalar(pick_r[:, t, :], slots, cur[:, 0, t:t + 1], None, ALU.is_equal)
                m.then_inc(pick_ready, 1)
                for h in range(2):
                    dve.wait_ge(gathered, item * 4 + (2 + h + 1))
                    dve.tensor_copy(g_lo[:, 4 * h:4 * h + 4, :].rearrange("p a t -> p (a t)"),
                                    bank(2 + h)).then_inc(g_lo_ready, 1)
                if not carried:
                    for j in range(SPLIT):
                        item_rest(item, j)
                j = 0
                for b in range(E_BLOCKS + 1):
                    if b < E_BLOCKS:
                        used(j)
                        used(j + 1)
                        j += 2
                    if b >= 1:
                        dve.wait_ge(mT_hi_ready, blocks + b)
                        rest(mT_lo[:, (b - 1) % 2].rearrange("p a t -> p (a t)"), bank(6 + (b - 1) % 2),
                             mT_hi[:, (b - 1) % 2].rearrange("p a t -> p (a t)"), mT_lo_ready)
                    if b < E_BLOCKS:
                        used(j)
                        used(j + 1)
                        j += 2
                        dve.wait_ge(m_silu, blocks + (b + 1))
                        dve.wait_ge(up_done, blocks + (b + 1))
                        dve.tensor_tensor(m_h[:, b % 2, :], m_g[:, b % 2, :], bank(2 * (b % 2) + 1),
                                          ALU.mult).then_inc(m_prod, 1)
                    if b >= 1:
                        used(j)
                        used(j + 1)
                        j += 2
                for h in range(2):
                    dve.wait_ge(y_hi_ready, item * 2 + (h + 1))
                    rest(y_lo[:, h * 512:(h + 1) * 512], bank(4 + h), y_hi[:, h * 512:(h + 1) * 512], y_lo_ready)
                for t in range(TT):
                    for h in range(2):
                        dve.wait_ge(scattered, item * 4 + (2 * t + h + 1))
                        s = x_tok[:, t, h * 512:(h + 1) * 512]
                        dve.scalar_tensor_tensor(out=s, in0=bank(2 * t + h), scalar=cur[:, 1, t:t + 1], in1=s,
                                                 op0=ALU.mult, op1=ALU.add).then_inc(combined, 1)

            with dve.Fori(0, N_EXP - 1) as item:
                run_item(item, item, slots0, True, True)
            run_item(N_EXP - 1, N_EXP - 1, slots0, True, False)
            dve.wait_ge(routed, 1)
            n_second = dve.value_load(second[0:1, 0:1], min_val=0, max_val=MAX_SECOND)
            with dve.Fori(0, MAX_SECOND) as s:
                with dve.If(n_second > s):
                    e = dve.value_load(second[0:1, bass.ds(s + 1, 1)], min_val=0, max_val=N_EXP - 1)
                    run_item(s + N_EXP, e, slots1, False, False)
            dve.wait_ge(combined, n_second * 4 + (N_EXP * 4 + TT))
            norm(3, False)


def constants():
    r, c = np.arange(P)[:, None], np.arange(P)[None, :]
    full = np.ones((P, P))
    parts = [r == c, -1.0 * (r >= c), -full, r < c, full * c, full * (c + P)]
    return np.stack([np.asarray(a, np.float32) for a in parts], axis=1)


def rotation_tables():
    half = HD // 2
    pos = np.arange(T, dtype=np.float64)
    ang = pos[:, None] * 10000.0 ** (-np.arange(half, dtype=np.float64) / half)[None, :]
    gamma = 1.0 - 2.0 ** (-5.0 - np.arange(N_RET, dtype=np.float64))
    grow = gamma[None, :] ** pos[:, None]
    q, k = (grow * HD ** -0.5)[:, :, None], (1.0 / grow)[:, :, None]
    cos, sin = np.cos(ang)[:, None, :], np.sin(ang)[:, None, :]
    tab = np.stack([q * cos, q * sin, k * cos, k * sin], axis=1).reshape(T, 4, N_RET * half)
    return np.ascontiguousarray(tab.reshape(TT, P, 4, 256).transpose(1, 0, 2, 3).astype(np.float32))


def kernel(**inputs):
    import concourse.bacc as bacc
    from concourse.bass_utils import run_bass_kernel_spmd as run

    a = {k: np.asarray(v) for k, v in inputs.items()}
    x = a["x"].reshape(T, D)
    at = MAX_REL + P + np.arange(P)[:, None] - np.arange(T)[None, :]
    arrays = {
        "x": x, "xT": x.T,
        "ln_g": np.concatenate([a["even_ln1_g"], a["even_ln2_g"], a["odd_ln1_g"], a["odd_ln2_g"]]),
        "ln_b": np.concatenate([a["even_ln1_b"], a["even_ln2_b"], a["odd_ln1_b"], a["odd_ln2_b"]]),
        "w_in": a["even_w_in"][0], "gn_g": a["even_ret_gn_g"], "w_out": a["even_w_out"][0],
        "w_gate": a["even_w_gate"][0], "w_up": a["even_w_up"][0], "w_down": a["even_w_down"][0],
        "w_qkv": a["odd_w_qkv"][0], "bias_win": a["odd_rel_bias"][0][:, at].transpose(1, 0, 2),
        "w_out2": a["odd_w_out"][0], "w_router": a["odd_w_router"][0], "b_router": a["odd_b_router"],
        "e_gate": a["odd_w_gate"][0], "e_up": a["odd_w_up"][0], "e_down": a["odd_w_down"][0],
        "tables": rotation_tables(), "consts": constants(),
    }
    nc = bacc.Bacc("TRN2", target_bir_lowering=False, num_devices=1)
    arrays = {k: np.ascontiguousarray(v) for k, v in arrays.items()}
    args = [nc.dram_tensor(k, v.shape, F32, kind="ExternalInput").ap() for k, v in arrays.items()]
    out = nc.dram_tensor("out", (T, D), F32, kind="ExternalOutput").ap()
    trunk_kernel(nc, *args, out)
    return run(nc, [arrays], core_ids=[0]).results[0]["out"].reshape(1, T, D)
```

```python
from contextlib import ExitStack

import concourse.bass as bass
import numpy as np
from concourse import mybir

F32 = mybir.dt.float32
F32R = mybir.dt.float32r
I32 = mybir.dt.int32
ALU = mybir.AluOpType
ACT = mybir.ActivationFunctionType
AX = mybir.AxisListType.X

P = 128
D = 1024
T = 256
TT = T // P
KC = D // P
HD = 64
CHUNK = 64
N_SB = 8
N_RET = 8
N_C = 16
F_DENSE = 2816
F_EXP = 3584
N_EXP = 8
MAX_REL = 256
ALPHA = 4.0 ** 0.25
EPS = 1e-5
UC = 2048
RAW = 6
SPLIT = 3
MASKED = -1e30

IN_BLOCKS = 7
OUT_UNITS = 4
FF_BLOCKS = F_DENSE // 256
DOWN_UNITS = F_DENSE // 256
QKV_BLOCKS = 6
U_IN = 0
U_OUT = U_IN + 2 * IN_BLOCKS
U_FF = U_OUT + OUT_UNITS
U_DOWN = U_FF + 2 * FF_BLOCKS
U_QKV = U_DOWN + DOWN_UNITS
U_OUT2 = U_QKV + 2 * QKV_BLOCKS
U_MOE = U_OUT2 + OUT_UNITS
E_BLOCKS = F_EXP // 512
ITEM_UNITS = 6 * E_BLOCKS
MAX_SECOND = (2 * T) // (P + 1)
N_ITEMS = N_EXP + MAX_SECOND


def item_units():
    units = []
    for b in range(E_BLOCKS + 1):
        if b < E_BLOCKS:
            units += [("gate", b, 0), ("gate", b, 1), ("up", b, 0), ("up", b, 1)]
        if b >= 1:
            units += [("down", b - 1, 0), ("down", b - 1, 1)]
    return units


def trunk_kernel(nc, x, xT, ln_g, ln_b, w_in, gn_g, w_out, w_gate, w_up, w_down, w_qkv, bias_win,
                 w_out2, w_router, b_router, e_gate, e_up, e_down, tables, consts, out):
    ctx = ExitStack()
    with ctx:
        def sem(name):
            return ctx.enter_context(nc.semaphore(name))

        def sb(stack, name, shape, dt=F32):
            return stack.enter_context(nc.sbuf_tensor(name, shape, dt))

        raw = sb(ctx, "raw", [P, RAW, UC])
        w_hi = sb(ctx, "w_hi", [P, SPLIT, UC], F32R)
        w_lo = sb(ctx, "w_lo", [P, SPLIT, UC], F32R)
        x_tok = sb(ctx, "x_tok", [P, TT, D])
        xT_hi = sb(ctx, "xT_hi", [P, KC, T], F32R)
        xT_lo = sb(ctx, "xT_lo", [P, KC, T], F32R)
        norm_gb = sb(ctx, "norm_gb", [P, 2, D])
        cst = sb(ctx, "cst", [P, 5, P])
        small = sb(ctx, "small", [P, 64])
        ident, neg_tri, neg_ones, before, slots = (cst[:, n, :] for n in range(5))
        eps_col = small[:, 0:1]
        sums = small[:, 2:6].rearrange("p (t h) -> p t h", t=TT)
        neg_mean, squares, std, rstd = (small[:, n:n + TT] for n in (6, 8, 10, 12))
        spare = small[:, 14:15]

        st = ExitStack()
        sb_qkT = sb(st, "sb_qkT", [P, 8, T])
        tokm = sb(st, "tokm", [P, TT, 5, 512])
        rot = sb(st, "rot", [P, TT, 4, 256])
        rot_t = sb(st, "rot_t", [P, 4, 256])
        ret_qkT = sb(st, "ret_qkT", [P, 8, T])
        sb_e = sb(st, "sb_e", [P, 2, 2, 384])
        sb_l = sb(st, "sb_l", [P, 2, 2, 384])
        sb_w = sb(st, "sb_w", [P, 2, 2, 384])
        ret_s = sb(st, "ret_s", [P, 2, 2, 384])
        xT_raw = ret_qkT
        oT_hi, oT_lo = xT_hi, xT_lo
        gn_row = rot_t[:, 0:2, :].rearrange("p a b -> p (a b)")
        ret_o = sb_l[:, :, :, :].rearrange("p a b c -> p (a b c)")[:, 0:1024].rearrange("p (t n) -> p t n", t=TT)
        ret_sq = sb_e[:, :, :, :].rearrange("p a b c -> p (a b c)")[:, 0:1024].rearrange("p (t n) -> p t n", t=TT)
        gn_s = small[:, 16:64].rearrange("p (a t h) -> p a t h", a=3, t=TT)
        st.close()
        st = ExitStack()
        hT_hi = sb(st, "hT_hi", [P, 2 * FF_BLOCKS, T], F32R)
        hT_lo = sb(st, "hT_lo", [P, 2 * FF_BLOCKS, T], F32R)
        ff_g = sb(st, "ff_g", [P, 2, 512])
        ff_h = sb(st, "ff_h", [P, 2, 512])
        st.close()
        st = ExitStack()
        c_qkT = sb(st, "c_qkT", [P, 16, T])
        c_v = sb(st, "c_v", [P, TT, D])
        c_bias = sb(st, "c_bias", [P, N_C, T])
        c_s = sb(st, "c_s", [P, 2, 2, 384])
        c_p = sb(st, "c_p", [P, 2, 2, 384])
        c_pT = sb(st, "c_pT", [P, 2, 2, 384])
        c_max = sb(st, "c_max", [P, 8, 2, 2])
        c_sum = sb(st, "c_sum", [P, 8, 2, 2])
        c_inv = sb(st, "c_inv", [P, 8, 2, 2])
        st.close()
        st = ExitStack()
        y_sum = sb(st, "y_sum", [P, TT, D])
        g_hi = sb(st, "g_hi", [P, KC, P], F32R)
        g_lo = sb(st, "g_lo", [P, KC, P], F32R)
        m_g = sb(st, "m_g", [P, 2, 512])
        m_h = sb(st, "m_h", [P, 2, 512])
        mT_hi = sb(st, "mT_hi", [P, 2, 4, P], F32R)
        mT_lo = sb(st, "mT_lo", [P, 2, 4, P], F32R)
        y_hi = sb(st, "y_hi", [P, D], F32R)
        y_lo = sb(st, "y_lo", [P, D], F32R)
        pick = sb(st, "pick", [P, TT, P])
        place_r = sb(st, "place_r", [P, TT, P], F32R)
        cur = sb(st, "cur", [P, TT])
        weight = sb(st, "weight", [P, TT])
        route = sb(st, "route", [P, N_ITEMS + 1, 2, TT])
        wr = sb(st, "wr", [P, KC, N_EXP])
        wr_hi = sb(st, "wr_hi", [P, KC, P], F32R)
        wr_lo = sb(st, "wr_lo", [P, KC, P], F32R)
        logitT = sb(st, "logitT", [N_EXP, T])
        br = sb(st, "br", [P, N_EXP])
        logit = sb(st, "logit", [P, TT, N_EXP])
        gt = sb(st, "gt", [P, TT, N_EXP, N_EXP])
        eq = sb(st, "eq", [P, TT, N_EXP, N_EXP])
        tri8 = sb(st, "tri8", [P, 2, N_EXP, N_EXP])
        num8 = sb(st, "num8", [P, N_EXP])
        rank = sb(st, "rank", [P, TT, N_EXP])
        picked = sb(st, "picked", [P, TT, N_EXP])
        top = sb(st, "top", [P, 4, TT])
        ex = sb(st, "ex", [P, TT, N_EXP])
        over = sb(st, "over", [P, 5, N_EXP])
        second_f = sb(st, "second_f", [P, 4])
        second = sb(st, "second", [P, 4], I32)
        st.close()

        ps = ctx.enter_context(nc.psum_tensor("ps", [P, 8, 512], F32))

        def bank(n):
            return ps[:, n, :]

        def two(v):
            return v.rearrange("p (b n) -> p b n", b=2)

        raw_landed = [sem(f"raw_landed{n}") for n in range(RAW)]
        consts_landed = sem("consts_landed")
        xT_landed = sem("xT_landed")
        aux_landed = [sem(f"aux_landed{n}") for n in range(8)]
        hi_ready = sem("hi_ready")
        lo_ready = sem("lo_ready")
        unit_used = sem("unit_used")
        xT_hi_ready = sem("xT_hi_ready")
        xT_lo_ready = sem("xT_lo_ready")
        eps_ready = sem("eps_ready")
        in_out = sem("in_out")
        rot_step = sem("rot_step")
        rot_done = sem("rot_done")
        ret_turned = sem("ret_turned")
        ret_qkT_ready = sem("ret_qkT_ready")
        sb_scored = sem("sb_scored")
        sb_abs = sem("sb_abs")
        sb_exp = sem("sb_exp")
        sb_log = sem("sb_log")
        sb_softplus = sem("sb_softplus")
        sb_l_masked = sem("sb_l_masked")
        sb_summed = sem("sb_summed")
        sb_weights = sem("sb_weights")
        sb_w_masked = sem("sb_w_masked")
        sb_pv = sem("sb_pv")
        oT_hi_ready = sem("oT_hi_ready")
        oT_lo_ready = sem("oT_lo_ready")
        ret_scored = sem("ret_scored")
        ret_copied = sem("ret_copied")
        ret_masked = sem("ret_masked")
        ret_pv = sem("ret_pv")
        gn_step = sem("gn_step")
        gn_sq = sem("gn_sq")
        gn_std = sem("gn_std")
        ret_out = sem("ret_out")
        ret_oT = sem("ret_oT")
        ln_res = sem("ln_res")
        ln_mean = sem("ln_mean")
        ln_centred = sem("ln_centred")
        ln_rstd = sem("ln_rstd")
        tile0_done = sem("tile0_done")
        ln_sq_done = sem("ln_sq_done")
        ln_std = sem("ln_std")
        ln_done = sem("ln_done")
        x_turned = sem("x_turned")
        ff_silu = sem("ff_silu")
        ff_prod = sem("ff_prod")
        hT_hi_ready = sem("hT_hi_ready")
        hT_lo_ready = sem("hT_lo_ready")
        qkv_out = sem("qkv_out")
        c_scored = sem("c_scored")
        c_biased = sem("c_biased")
        c_masked = sem("c_masked")
        c_maxed = sem("c_maxed")
        c_exped = sem("c_exped")
        c_recip = sem("c_recip")
        c_normed = sem("c_normed")
        c_turned = sem("c_turned")
        c_pT_ready = sem("c_pT_ready")
        c_pv = sem("c_pv")
        c_oT_hi = sem("c_oT_hi")
        c_oT_lo = sem("c_oT_lo")
        wr_zeroed = sem("wr_zeroed")
        wr_split = sem("wr_split")
        logitsT_out = sem("logitsT_out")
        logits_done = sem("logits_done")
        logits_turned = sem("logits_turned")
        r_step = sem("r_step")
        r_exp = sem("r_exp")
        picked_ready = sem("picked_ready")
        slots_done = sem("slots_done")
        routed = sem("routed")
        pick_ready = sem("pick_ready")
        place_turned = sem("place_turned")
        place_ready = sem("place_ready")
        gathered = sem("gathered")
        g_hi_ready = sem("g_hi_ready")
        g_lo_ready = sem("g_lo_ready")
        m_silu = sem("m_silu")
        m_prod = sem("m_prod")
        m_turned = sem("m_turned")
        mT_hi_ready = sem("mT_hi_ready")
        mT_lo_ready = sem("mT_lo_ready")
        y_hi_ready = sem("y_hi_ready")
        y_lo_ready = sem("y_lo_ready")
        scattered = sem("scattered")
        y_added = sem("y_added")
        cur_ready = sem("cur_ready")
        weight_ready = sem("weight_ready")
        stored = sem("stored")

        dense = []
        for c in range(IN_BLOCKS):
            for k in range(2):
                dense.append(w_in[k * 512:(k + 1) * 512, c * 512:(c + 1) * 512].rearrange("(k p) n -> p k n", p=P))
        for k in range(OUT_UNITS):
            dense.append(w_out[k * 256:(k + 1) * 256, :].rearrange("(k p) n -> p k n", p=P))
        for b in range(FF_BLOCKS):
            for w in (w_gate, w_up):
                dense.append(w[:, b * 256:(b + 1) * 256].rearrange("(k p) n -> p k n", p=P))
        for k in range(DOWN_UNITS):
            dense.append(w_down[k * 256:(k + 1) * 256, :].rearrange("(k p) n -> p k n", p=P))
        for c in range(QKV_BLOCKS):
            for k in range(2):
                dense.append(w_qkv[k * 512:(k + 1) * 512, c * 512:(c + 1) * 512].rearrange("(k p) n -> p k n", p=P))
        for k in range(OUT_UNITS):
            dense.append(w_out2[k * 256:(k + 1) * 256, :].rearrange("(k p) n -> p k n", p=P))
        assert len(dense) == U_MOE
        units = item_units()
        assert len(units) == ITEM_UNITS and ITEM_UNITS % RAW == 0 and ITEM_UNITS % SPLIT == 0

        def raw_slot(u, n):
            return raw[:, u % RAW, :].rearrange("p (k n) -> p k n", n=n)

        def hi_slot(u, n):
            return w_hi[:, u % SPLIT, :].rearrange("p (k n) -> p k n", n=n)

        def lo_slot(u, n):
            return w_lo[:, u % SPLIT, :].rearrange("p (k n) -> p k n", n=n)

        def landed(item, j):
            u = U_MOE + j
            return item * (16 * (ITEM_UNITS // RAW)) + 16 * (u // RAW + 1)

        block = ctx.enter_context(nc.Block())

        @block.sync
        def _(sp):
            def free(u):
                sp.wait_ge(lo_ready, u - RAW + 1)

            sp.dma_start(xT_raw[:, :, :], xT.rearrange("(k p) t -> p k t", p=P)).then_inc(xT_landed, 16)
            for u, src in enumerate(dense):
                if u >= RAW:
                    free(u)
                sp.dma_start(raw_slot(u, src.shape[2]), src).then_inc(raw_landed[u % RAW], 16)

            def load_item(item, e):
                for j, (kind, b, half) in enumerate(units):
                    u = U_MOE + j
                    free(item * ITEM_UNITS + u)
                    if kind == "down":
                        src = e_down[e, b * 512 + half * 256:b * 512 + (half + 1) * 256, :]
                        n = D
                    else:
                        w = e_gate if kind == "gate" else e_up
                        src = w[e, half * 512:(half + 1) * 512, b * 512:(b + 1) * 512]
                        n = 512
                    sp.dma_start(raw_slot(u, n), src.rearrange("(k p) n -> p k n", p=P)).then_inc(
                        raw_landed[u % RAW], 16)

            with sp.Fori(0, N_EXP) as item:
                load_item(item, item)
            sp.wait_ge(routed, 1)
            n_second = sp.value_load(second[0:1, 0:1], min_val=0, max_val=MAX_SECOND)
            with sp.Fori(0, MAX_SECOND) as s:
                with sp.If(n_second > s):
                    e = sp.value_load(second[0:1, bass.ds(s + 1, 1)], min_val=0, max_val=N_EXP - 1)
                    load_item(s + N_EXP, e)
            for t in range(TT):
                sp.wait_ge(ln_done, 12 + 2 * (t + 1))
                sp.dma_start(out[t * P:(t + 1) * P, :], y_sum[:, t, :]).then_inc(stored, 16)
            sp.wait_ge(stored, 16 * TT)

        @block.gpsimd
        def _(pool):
            pool.memset(eps_col, EPS).then_inc(eps_ready, 1)
            pool.dma_start(cst[:, :, :], consts).then_inc(consts_landed, 16)
            pool.dma_start(x_tok[:, :, :], x.rearrange("(t p) d -> p t d", p=P)).then_inc(aux_landed[0], 16)
            pool.dma_start(rot[:, :, :, :], tables).then_inc(aux_landed[1], 16)

            def load_norm(n):
                if n >= 1:
                    pool.wait_ge(ln_done, 4 * n)
                pool.dma_start(norm_gb[:, 0, :], ln_g[n:n + 1, :].broadcast_to((P, D))).then_inc(aux_landed[2], 16)
                pool.dma_start(norm_gb[:, 1, :], ln_b[n:n + 1, :].broadcast_to((P, D))).then_inc(aux_landed[2], 16)

            load_norm(0)

            for qk in range(2):
                for t in range(TT):
                    n = 2 * qk + t
                    pool.wait_ge(in_out, 2 * (3 + qk) + t + 1)
                    if n == 0:
                        pool.wait_ge(aux_landed[1], 16)
                    else:
                        pool.wait_ge(rot_done, 2 * n)
                    v = tokm[:, t, 1 + qk, :].rearrange("p (h a f) -> p h a f", h=N_RET, a=2)
                    x1, x2 = v[:, :, 0, :], v[:, :, 1, :]
                    c = rot[:, t, 2 * qk, :].rearrange("p (h f) -> p h f", h=N_RET)
                    s = rot[:, t, 2 * qk + 1, :].rearrange("p (h f) -> p h f", h=N_RET)
                    w = [rot_t[:, m, :].rearrange("p (h f) -> p h f", h=N_RET) for m in range(4)]
                    pool.tensor_tensor(w[0], x1, c, ALU.mult).then_inc(rot_step, 1)
                    pool.tensor_tensor(w[1], x2, s, ALU.mult).then_inc(rot_step, 1)
                    pool.tensor_tensor(w[2], x1, s, ALU.mult).then_inc(rot_step, 1)
                    pool.tensor_tensor(w[3], x2, c, ALU.mult).then_inc(rot_step, 1)
                    pool.wait_ge(rot_step, 4 * (n + 1))
                    pool.tensor_tensor(x1, w[0], w[1], ALU.subtract).then_inc(rot_done, 1)
                    pool.tensor_tensor(x2, w[2], w[3], ALU.add).then_inc(rot_done, 1)
            pool.wait_ge(rot_done, 8)
            pool.dma_start(gn_row, gn_g.broadcast_to((P, 512))).then_inc(aux_landed[3], 16)

            def mask_diagonals(t, strict):
                for h in range(2):
                    v = t[:, h, :].rearrange("p (b q) -> p b q", q=P)[:, 0:3:2, :]
                    m = pool.affine_select(out=v, in_=v, compare_op=ALU.is_gt if strict else ALU.is_ge, fill=0.0,
                                           base=0, pattern=[[0, 2], [1, P]], channel_multiplier=-1)
                return m

            for p in range(4):
                pool.wait_ge(sb_softplus, p + 1)
                mask_diagonals(sb_l[:, p % 2], True).then_inc(sb_l_masked, 1)
                pool.wait_ge(ret_copied, p + 1)
                mask_diagonals(ret_s[:, p % 2], False).then_inc(ret_masked, 1)
                pool.wait_ge(sb_weights, p + 1)
                mask_diagonals(sb_w[:, p % 2], True).then_inc(sb_w_masked, 1)

            load_norm(1)

            pool.wait_ge(unit_used, U_QKV)
            pool.dma_start(c_bias[:, :, :], bias_win).then_inc(aux_landed[4], 16)
            load_norm(2)
            for p in range(N_C // 2):
                pool.wait_ge(c_biased, 2 * (p + 1))
                pool.memset(c_s[0:CHUNK, p % 2, :, CHUNK:P], MASKED).then_inc(c_masked, 1)
                pool.memset(c_s[0:CHUNK, p % 2, :, 2 * P + CHUNK:3 * P], MASKED).then_inc(c_masked, 1)

            pool.wait_ge(unit_used, U_MOE)
            pool.dma_start(wr[:, :, :], w_router.rearrange("(k p) e -> p k e", p=P)).then_inc(aux_landed[5], 16)
            pool.memset(wr_hi[:, :, :].bitcast(F32), 0.0).then_inc(wr_zeroed, 1)
            pool.memset(wr_lo[:, :, :].bitcast(F32), 0.0).then_inc(wr_zeroed, 1)
            pool.dma_start(br[:, :], b_router.broadcast_to((P, N_EXP))).then_inc(aux_landed[6], 16)
            pool.memset(tri8[:, :, :, :], 1.0).then_inc(r_step, 1)
            pool.iota(num8[:, :], pattern=[[1, N_EXP]], base=0, channel_multiplier=0,
                      allow_small_or_imprecise_dtypes=True).then_inc(r_step, 1)
            pool.wait_ge(r_step, 1)
            pool.affine_select(out=tri8[:, 0], in_=tri8[:, 0], compare_op=ALU.is_gt, fill=0.0, base=0,
                               pattern=[[1, N_EXP], [-1, N_EXP]], channel_multiplier=0).then_inc(r_step, 1)
            pool.affine_select(out=tri8[:, 1], in_=tri8[:, 1], compare_op=ALU.is_ge, fill=0.0, base=0,
                               pattern=[[1, N_EXP], [-1, N_EXP]], channel_multiplier=0).then_inc(r_step, 1)
            load_norm(3)

        @block.tensor
        def _(pe):
            def mm3(o, a, b, first, last):
                (a_hi, a_lo), (b_hi, b_lo) = a, b
                pe.matmul(o, a_hi, b_hi, start=first, stop=False, skip_group_check=True)
                pe.matmul(o, a_lo, b_hi, start=False, stop=False, skip_group_check=True)
                return pe.matmul(o, a_hi, b_lo, start=False, stop=last, skip_group_check=True)

            def split_ready(u):
                pe.wait_ge(hi_ready, u + 1)
                pe.wait_ge(lo_ready, u + 1)

            def project(c, u, tokens):
                for k2 in range(2):
                    split_ready(u + k2)
                    hi, lo = hi_slot(u + k2, 512), lo_slot(u + k2, 512)
                    for o in range(2):
                        b = bank(2 * (c % 2) + o)
                        for kk in range(4):
                            k = 4 * k2 + kk
                            if tokens:
                                m = mm3(b, (xT_hi[:, k, o * P:(o + 1) * P], xT_lo[:, k, o * P:(o + 1) * P]),
                                        (hi[:, kk, :], lo[:, kk, :]), k == 0, k == KC - 1)
                            else:
                                for h in range(2):
                                    w = slice((2 * o + h) * P, (2 * o + h + 1) * P)
                                    m = mm3(b[:, h * T:(h + 1) * T], (hi[:, kk, w], lo[:, kk, w]),
                                            (xT_hi[:, k, :], xT_lo[:, k, :]), k == 0 and h == 0, k == KC - 1)
                    m.then_inc(unit_used, 1)

            def rows(u, n_chunk, aT, first, last):
                split_ready(u)
                hi, lo = hi_slot(u, D), lo_slot(u, D)
                for t in range(TT):
                    for kk in range(2):
                        k = n_chunk + kk
                        a = (aT[0][:, k, t * P:(t + 1) * P], aT[1][:, k, t * P:(t + 1) * P])
                        for h in range(2):
                            m = mm3(bank(4 + 2 * t + h), a,
                                    (hi[:, kk, h * 512:(h + 1) * 512], lo[:, kk, h * 512:(h + 1) * 512]),
                                    first and kk == 0, last and kk == 1)
                    if last and t == 0:
                        m.then_inc(tile0_done, 1)
                m.then_inc(unit_used, 1)

            def turn_x(n):
                pe.wait_ge(ln_sq_done, TT * (n + 1))
                for t in range(TT):
                    for k in range(KC):
                        if k % 4 == 0:
                            pe.wait_ge(ln_done, 4 * n + 2 * t + k // 4 + 1)
                        m = pe.transpose(bank(k // 2)[:, (k % 2) * T + t * P:(k % 2) * T + (t + 1) * P],
                                         x_tok[:, t, k * P:(k + 1) * P], ident)
                        if t == TT - 1 and k % 2 == 1:
                            m.then_inc(x_turned, 1)

            for c in range(IN_BLOCKS):
                if c == 0:
                    pe.wait_ge(xT_hi_ready, 4)
                    pe.wait_ge(xT_lo_ready, 4)
                if c >= 2:
                    pe.wait_ge(in_out, 2 * (c - 1))
                project(c, U_IN + 2 * c, c >= 2)

            pe.wait_ge(consts_landed, 16)
            pe.wait_ge(rot_done, 8)
            for c in range(8):
                for t in range(TT):
                    m = pe.transpose(bank(4 + c // 2)[:, (c % 2) * T + t * P:(c % 2) * T + (t + 1) * P],
                                     tokm[:, t, 1 + c // 4, (c % 4) * P:(c % 4 + 1) * P], ident)
                if c % 2 == 1:
                    m.then_inc(ret_turned, 1)

            def scores(qT, kT, b0, done):
                for h in range(2):
                    q, k = qT[h * HD:(h + 1) * HD], kT[h * HD:(h + 1) * HD]
                    pe.matmul(bank(b0 + h)[:, 0:T], k[:, 0:P], q[:, 0:T], start=True, stop=True,
                              skip_group_check=True)
                    m = pe.matmul(bank(b0 + h)[:, T:T + P], k[:, P:T], q[:, P:T], start=False, stop=True,
                                  skip_group_check=True)
                m.then_inc(done, 1)

            def weighted(o, v0, v1, wt, done):
                for h in range(2):
                    r = slice(h * HD, (h + 1) * HD)
                    pe.matmul(o[r, 0:T], v0[:, r], wt[:, h, 0:T], start=True, stop=False, skip_group_check=True)
                    m = pe.matmul(o[r, P:T], v1[:, r], wt[:, h, T:T + P], start=False, stop=True,
                                  skip_group_check=True)
                m.then_inc(done, 1)

            def sb_scores(p):
                if p == 0:
                    pe.wait_ge(in_out, 2 * IN_BLOCKS)
                else:
                    pe.wait_ge(sb_weights, p)
                scores(sb_qkT[:, p, :], sb_qkT[:, 4 + p, :], 0, sb_scored)

            def ret_scores(p):
                if p == 0:
                    pe.wait_ge(ret_qkT_ready, 4)
                else:
                    pe.wait_ge(ret_copied, p)
                scores(ret_qkT[:, p, :], ret_qkT[:, 4 + p, :], 2, ret_scored)

            def sb_sums(p):
                pe.wait_ge(sb_l_masked, p + 1)
                for h in range(2):
                    b, sp_ = bank(h), sb_l[:, p % 2, h, :]
                    pe.matmul(b[:, 0:T], neg_tri, sp_[:, 0:T], start=False, stop=False, skip_group_check=True)
                    pe.matmul(b[:, P:T], neg_ones, sp_[:, T:T + P], start=False, stop=False, skip_group_check=True)
                    m = pe.matmul(b[:, T:T + P], neg_tri, sp_[:, T:T + P], start=False, stop=True,
                                  skip_group_check=True)
                m.then_inc(sb_summed, 1)

            def ret_values(p):
                pe.wait_ge(ret_masked, p + 1)
                for h in range(2):
                    n = 2 * p + h
                    c = slice(n * HD, (n + 1) * HD)
                    s = ret_s[:, p % 2, h, :]
                    pe.matmul(bank(6)[:, c], s[:, 0:P], tokm[:, 0, 3, c], start=n == 0, stop=True,
                              skip_group_check=True)
                    pe.matmul(bank(7)[:, c], s[:, P:T], tokm[:, 0, 3, c], start=n == 0, stop=False,
                              skip_group_check=True)
                    m = pe.matmul(bank(7)[:, c], s[:, T:T + P], tokm[:, 1, 3, c], start=False, stop=True,
                                  skip_group_check=True)
                m.then_inc(ret_pv, 1)

            sb_scores(0)
            ret_scores(0)
            for p in range(4):
                sb_sums(p)
                ret_values(p)
                if p < 3:
                    ret_scores(p + 1)
                pe.wait_ge(sb_w_masked, p + 1)
                if p >= 2:
                    pe.wait_ge(oT_lo_ready, p - 1)
                if p < 3:
                    sb_scores(p + 1)
                v = slice(p * P, (p + 1) * P)
                weighted(bank(4 + p % 2), tokm[:, 0, 0, v], tokm[:, 1, 0, v], sb_w[:, p % 2], sb_pv)

            for t in range(TT):
                pe.wait_ge(ret_out, t + 1)
                for c in range(4):
                    m = pe.transpose(bank(c // 2)[:, (c % 2) * T + t * P:(c % 2) * T + (t + 1) * P],
                                     ret_o[:, t, c * P:(c + 1) * P], ident)
                    if t == TT - 1 and c % 2 == 1:
                        m.then_inc(ret_oT, 1)

            for k in range(OUT_UNITS):
                pe.wait_ge(oT_lo_ready, 4 if k < 2 else 4 + (k - 1))
                rows(U_OUT + k, 2 * k, (oT_hi, oT_lo), k == 0, k == OUT_UNITS - 1)
            turn_x(0)

            for b in range(FF_BLOCKS):
                if b == 0:
                    pe.wait_ge(xT_hi_ready, 8)
                    pe.wait_ge(xT_lo_ready, 8)
                if b >= 2:
                    pe.wait_ge(ff_prod, b - 1)
                for g in range(2):
                    u = U_FF + 2 * b + g
                    split_ready(u)
                    hi, lo = hi_slot(u, 256), lo_slot(u, 256)
                    for h in range(2):
                        for k in range(KC):
                            w = slice(h * P, (h + 1) * P)
                            m = mm3(bank(2 * (b % 2) + g)[:, h * T:(h + 1) * T], (hi[:, k, w], lo[:, k, w]),
                                    (xT_hi[:, k, :], xT_lo[:, k, :]), k == 0 and h == 0, k == KC - 1)
                    m.then_inc(unit_used, 1)
            for k in range(DOWN_UNITS):
                pe.wait_ge(hT_hi_ready, k + 1)
                pe.wait_ge(hT_lo_ready, k + 1)
                if k == 0:
                    pe.wait_ge(ln_done, 4)
                rows(U_DOWN + k, 2 * k, (hT_hi, hT_lo), k == 0, k == DOWN_UNITS - 1)
            turn_x(1)

            for c in range(QKV_BLOCKS):
                if c == 0:
                    pe.wait_ge(xT_hi_ready, 12)
                    pe.wait_ge(xT_lo_ready, 12)
                if c >= 2:
                    pe.wait_ge(qkv_out, 2 * (c - 1))
                project(c, U_QKV + 2 * c, c >= 4)

            def c_scores(p):
                if p >= 2:
                    pe.wait_ge(c_biased, 2 * (p - 1))
                for h in range(2):
                    q, k = (c_qkT[h * HD:(h + 1) * HD, n, :] for n in (p, 8 + p))
                    b = bank(2 * (p % 2) + h)
                    pe.matmul(b[:, 0:P], q[:, 0:P], k[:, 0:P], start=True, stop=True, skip_group_check=True)
                    m = pe.matmul(b[:, P:P + T], q[:, P:T], k[:, 0:T], start=False, stop=True,
                                  skip_group_check=True)
                m.then_inc(c_scored, 1)

            def c_turn(p):
                pe.wait_ge(c_normed, 4 * (p + 1))
                if p >= 1:
                    pe.wait_ge(c_pT_ready, p)
                for h in range(2):
                    w = c_p[:, p % 2, h, :]
                    for s, d in ((0, 0), (1, 1), (2, 2)):
                        m = pe.transpose(bank(6 + h)[:, d * P:(d + 1) * P], w[:, s * P:(s + 1) * P], ident)
                m.then_inc(c_turned, 1)

            def c_values(p):
                pe.wait_ge(c_pT_ready, p + 1)
                if p >= 2:
                    pe.wait_ge(c_oT_lo, p - 1)
                v = slice(p * P, (p + 1) * P)
                weighted(bank(4 + p % 2), c_v[:, 0, v], c_v[:, 1, v], c_pT[:, p % 2], c_pv)

            pe.wait_ge(qkv_out, 2 * QKV_BLOCKS)
            pe.wait_ge(ln_done, 8)
            c_scores(0)
            for p in range(N_C // 2):
                if p + 1 < N_C // 2:
                    c_scores(p + 1)
                if p >= 1:
                    c_values(p - 1)
                c_turn(p)
            c_values(N_C // 2 - 1)
            for k in range(OUT_UNITS):
                pe.wait_ge(c_oT_lo, 8)
                rows(U_OUT2 + k, 2 * k, (oT_hi, oT_lo), k == 0, k == OUT_UNITS - 1)
            turn_x(2)

            pe.wait_ge(xT_hi_ready, 16)
            pe.wait_ge(xT_lo_ready, 16)
            pe.wait_ge(wr_split, 2)
            pe.wait_ge(ln_done, 12)
            for k in range(KC):
                m = mm3(bank(4)[:, 0:T], (wr_hi[:, k, :], wr_lo[:, k, :]), (xT_hi[:, k, :], xT_lo[:, k, :]),
                        k == 0, k == KC - 1)
            m.then_inc(logits_done, 1)
            pe.wait_ge(logitsT_out, 1)
            for t in range(TT):
                m = pe.transpose(bank(5)[:, 64 + 8 * t:72 + 8 * t], logitT[:, t * P:(t + 1) * P],
                                 ident[0:N_EXP, 0:N_EXP])
            m.then_inc(logits_turned, 1)
            pe.wait_ge(picked_ready, 1)
            c5 = bank(5)
            pe.matmul(c5[:, 0:8], before, picked[:, 0, :], start=True, stop=True, skip_group_check=True)
            pe.matmul(c5[:, 8:16], before, picked[:, 1, :], start=False, stop=True, skip_group_check=True)
            pe.matmul(c5[:, 16:24], neg_ones, picked[:, 0, :], start=False, stop=True, skip_group_check=True)
            m = pe.matmul(c5[:, 24:32], neg_ones, picked[:, 1, :], start=False, stop=True, skip_group_check=True)
            m.then_inc(slots_done, 1)

            def gather(item):
                pe.wait_ge(pick_ready, item + 2)
                for k in range(KC):
                    for t in range(TT):
                        m = pe.matmul(bank(2 + k // 4)[:, (k % 4) * P:(k % 4 + 1) * P],
                                      x_tok[:, t, k * P:(k + 1) * P], pick[:, t, :],
                                      start=k % 4 == 0 and t == 0, stop=t == TT - 1, skip_group_check=True)
                m.then_inc(gathered, 1)

            def scatter(item, n, b):
                t, h = n // 2, n % 2
                pe.matmul(b, place_r[:, t, :], y_hi[:, h * 512:(h + 1) * 512], start=True, stop=False,
                          skip_group_check=True)
                m = pe.matmul(b, place_r[:, t, :], y_lo[:, h * 512:(h + 1) * 512], start=False, stop=True,
                              skip_group_check=True)
                m.then_inc(scattered, 1)

            def run_item(item, first):
                base = item * ITEM_UNITS + U_MOE
                blocks = item * E_BLOCKS

                def unit_ready(j):
                    pe.wait_ge(hi_ready, base + (j + 1))
                    pe.wait_ge(lo_ready, base + (j + 1))

                def first_product(j, b, g):
                    for k2 in range(2):
                        u = j + k2
                        unit_ready(u)
                        hi, lo = hi_slot(U_MOE + u, 512), lo_slot(U_MOE + u, 512)
                        for kk in range(4):
                            k = 4 * k2 + kk
                            m = mm3(bank(2 * (b % 2) + g), (g_hi[:, k, :], g_lo[:, k, :]),
                                    (hi[:, kk, :], lo[:, kk, :]), k == 0, k == KC - 1)
                        m.then_inc(unit_used, 1)

                def turn(b):
                    pe.wait_ge(m_prod, blocks + (b + 1))
                    if not (first and b == 0):
                        pe.wait_ge(mT_lo_ready, blocks + b)
                    for c in range(4):
                        m = pe.transpose(bank(6)[:, c * P:(c + 1) * P], m_h[:, b % 2, c * P:(c + 1) * P], ident)
                    m.then_inc(m_turned, 1)

                def second_product(j, b, k2):
                    unit_ready(j)
                    hi, lo = hi_slot(U_MOE + j, D), lo_slot(U_MOE + j, D)
                    for kk in range(2):
                        c = 2 * k2 + kk
                        for h in range(2):
                            m = mm3(bank(4 + h), (mT_hi[:, b % 2, c, :], mT_lo[:, b % 2, c, :]),
                                    (hi[:, kk, h * 512:(h + 1) * 512], lo[:, kk, h * 512:(h + 1) * 512]),
                                    b == 0 and c == 0, b == E_BLOCKS - 1 and c == 3)
                    m.then_inc(unit_used, 1)

                j = 0
                for b in range(E_BLOCKS):
                    if b < 2:
                        pe.wait_ge(g_lo_ready, item + 1)
                        if not first:
                            pe.wait_ge(m_prod, blocks)
                    else:
                        pe.wait_ge(m_prod, blocks + (b - 1))
                    first_product(j, b, 0)
                    if b >= 1:
                        turn(b - 1)
                    if 1 <= b <= 4 and not first:
                        if b == 1:
                            pe.wait_ge(y_lo_ready, item)
                        pe.wait_ge(y_added, item * 4 + (b - 4))
                        scatter(item, b - 1, bank(7))
                    if b == 5:
                        if not first:
                            pe.wait_ge(y_added, item * 4 + 1)
                        for t in range(TT):
                            m = pe.transpose(bank(7)[:, t * P:(t + 1) * P], pick[:, t, :], ident)
                        m.then_inc(place_turned, 1)
                    first_product(j + 2, b, 1)
                    j += 4
                    if b == E_BLOCKS - 1:
                        gather(item)
                    if b >= 1:
                        pe.wait_ge(mT_lo_ready, blocks + b)
                        if b == 1 and not first:
                            pe.wait_ge(y_lo_ready, item)
                        second_product(j, b - 1, 0)
                        if b == E_BLOCKS - 1:
                            turn(b)
                        second_product(j + 1, b - 1, 1)
                        j += 2
                pe.wait_ge(mT_lo_ready, blocks + E_BLOCKS)
                second_product(j, E_BLOCKS - 1, 0)
                second_product(j + 1, E_BLOCKS - 1, 1)

            gather(-1)
            run_item(0, True)
            with pe.Fori(1, N_EXP) as item:
                run_item(item, False)
            pe.wait_ge(routed, 1)
            n_second = pe.value_load(second[0:1, 0:1], min_val=0, max_val=MAX_SECOND)
            with pe.Fori(N_EXP, N_ITEMS) as item:
                with pe.If(n_second > item - N_EXP):
                    run_item(item, False)
            pe.wait_ge(y_lo_ready, n_second + N_EXP)
            for n in range(4):
                scatter(None, n, bank(n))

        @block.scalar
        def _(act):
            def round_unit(u):
                act.wait_ge(raw_landed[u % RAW], 16 * (u // RAW + 1))
                if u >= SPLIT:
                    act.wait_ge(unit_used, u - SPLIT + 1)
                act.activation(w_hi[:, u % SPLIT, :], raw[:, u % RAW, :], ACT.Copy).then_inc(hi_ready, 1)

            def copy(o, i, s, scale=1.0):
                act.activation(o, i, ACT.Copy, scale=scale).then_inc(s, 1)

            act.wait_ge(xT_landed, 16)
            for j in range(4):
                copy(xT_hi[:, 2 * j:2 * j + 2, :], xT_raw[:, 2 * j:2 * j + 2, :], xT_hi_ready)
            for u in range(SPLIT):
                round_unit(u)

            for c in range(IN_BLOCKS):
                act.wait_ge(unit_used, U_IN + 2 * c + 2)
                for o in range(2):
                    b = bank(2 * (c % 2) + o)
                    if c < 2:
                        dst = sb_qkT[:, 4 * c + 2 * o:4 * c + 2 * o + 2, :].rearrange("p a t -> p (a t)")
                        copy(dst, b, in_out, HD ** -0.5 if c == 0 else 1.0)
                    elif c < 6:
                        copy(tokm[:, o, c - 2, :], b, in_out)
                    else:
                        act.activation(tokm[:, o, 4, :], b, ACT.Silu).then_inc(in_out, 1)
                for k2 in range(2):
                    round_unit(U_IN + 2 * c + k2 + SPLIT)
            for j in range(4):
                act.wait_ge(ret_turned, j + 1)
                copy(ret_qkT[:, 2 * j:2 * j + 2, :].rearrange("p a t -> p (a t)"), bank(4 + j), ret_qkT_ready)

            act.preload_act_table_set("natural_log_exp_and_others")
            for p in range(4):
                e = sb_e[:, p % 2]
                act.wait_ge(sb_scored, p + 1)
                act.activation(e, ps[:, 0:2, 0:384], ACT.Abs).then_inc(sb_abs, 1)
                act.wait_ge(sb_abs, p + 1)
                act.activation(e, e, ACT.Exp, scale=-1.0).then_inc(sb_exp, 1)
                act.wait_ge(sb_exp, p + 1)
                act.activation(e, e, ACT.Ln, bias=1.0).then_inc(sb_log, 1)
                act.wait_ge(sb_summed, p + 1)
                if p >= 2:
                    act.wait_ge(sb_pv, p - 1)
                act.activation(sb_w[:, p % 2], ps[:, 0:2, 0:384], ACT.Exp).then_inc(sb_weights, 1)
                act.wait_ge(sb_pv, p + 1)
                copy(oT_hi[:, p, :], bank(4 + p % 2)[:, 0:T], oT_hi_ready)

            for t in range(TT):
                act.wait_ge(gn_step, 2 * t + 2)
                act.activation(ret_sq[:, t, :], ret_o[:, t, :], ACT.Square).then_inc(gn_sq, 1)
            for t in range(TT):
                act.wait_ge(gn_step, 4 + t + 1)
                act.activation(gn_s[:, 2, t, :], gn_s[:, 1, t, :], ACT.Sqrt, scale=1.0 / HD,
                               bias=eps_col).then_inc(gn_std, 1)
            for j in range(2):
                act.wait_ge(ret_oT, j + 1)
                copy(oT_hi[:, 4 + 2 * j:6 + 2 * j, :].rearrange("p a t -> p (a t)"), bank(j), oT_hi_ready)
            for k in range(OUT_UNITS):
                round_unit(U_OUT + k + SPLIT)

            def norm(n, v):
                act.activation(spare, eps_col, ACT.Sqrt)
                for t in range(TT):
                    act.wait_ge(ln_mean, TT * n + t + 1)
                    act.activation(ps[:, 2 * t:2 * t + 2, :], two(v[:, t, :]), ACT.Square,
                                   bias=neg_mean[:, t:t + 1], accum_out=squares[:, t:t + 1]).then_inc(ln_sq_done, 1)
                    act.wait_ge(ln_sq_done, TT * n + t + 1)
                    act.activation(std[:, t:t + 1], squares[:, t:t + 1], ACT.Sqrt, scale=1.0 / D,
                                   bias=eps_col).then_inc(ln_std, 1)

            def split_xT(n):
                for j in range(4):
                    act.wait_ge(x_turned, 4 * n + j + 1)
                    copy(xT_hi[:, 2 * j:2 * j + 2, :].rearrange("p a t -> p (a t)"), bank(j), xT_hi_ready)

            act.wait_ge(eps_ready, 1)
            norm(0, x_tok)
            split_xT(0)

            def ff_hi(b):
                act.wait_ge(ff_prod, b + 1)
                copy(hT_hi[:, 2 * b:2 * b + 2, :].rearrange("p a t -> p (a t)"), ff_h[:, b % 2, :], hT_hi_ready)

            for b in range(FF_BLOCKS):
                act.wait_ge(unit_used, U_FF + 2 * b + 1)
                if b >= 2:
                    act.wait_ge(ff_prod, b - 1)
                act.activation(ff_g[:, b % 2, :], bank(2 * (b % 2)), ACT.Silu).then_inc(ff_silu, 1)
                round_unit(U_FF + 2 * b + SPLIT)
                if b >= 1:
                    ff_hi(b - 1)
                round_unit(U_FF + 2 * b + 1 + SPLIT)
            ff_hi(FF_BLOCKS - 1)
            for k in range(DOWN_UNITS):
                round_unit(U_DOWN + k + SPLIT)
            norm(1, x_tok)
            split_xT(1)

            for c in range(QKV_BLOCKS):
                act.wait_ge(unit_used, U_QKV + 2 * c + 2)
                for o in range(2):
                    b = bank(2 * (c % 2) + o)
                    if c < 4:
                        copy(c_qkT[:, 4 * c + 2 * o:4 * c + 2 * o + 2, :].rearrange("p a t -> p (a t)"), b, qkv_out)
                    else:
                        copy(c_v[:, o, (c - 4) * 512:(c - 3) * 512], b, qkv_out)
                for k2 in range(2):
                    round_unit(U_QKV + 2 * c + k2 + SPLIT)

            def c_tail(p):
                act.wait_ge(c_turned, p + 1)
                if p >= 2:
                    act.wait_ge(c_pv, p - 1)
                copy(c_pT[:, p % 2], ps[:, 6:8, 0:384], c_pT_ready)
                act.wait_ge(c_pv, p + 1)
                copy(oT_hi[:, p, :], bank(4 + p % 2)[:, 0:T], c_oT_hi)

            for p in range(N_C // 2):
                act.wait_ge(c_maxed, 2 * (p + 1))
                if p >= 2:
                    act.wait_ge(c_turned, p - 1)
                for h in range(2):
                    for t, s in ((0, slice(0, P)), (1, slice(P, P + T))):
                        act.activation(c_p[:, p % 2, h, s], c_s[:, p % 2, h, s], ACT.Exp,
                                       bias=c_max[:, p, h, t:t + 1], accum_out=c_sum[:, p, h, t:t + 1]
                                       ).then_inc(c_exped, 1)
                if p >= 1:
                    c_tail(p - 1)
            c_tail(N_C // 2 - 1)
            for k in range(OUT_UNITS):
                round_unit(U_OUT2 + k + SPLIT)
            norm(2, x_tok)
            act.wait_ge(aux_landed[5], 16)
            act.wait_ge(wr_zeroed, 2)
            copy(wr_hi[:, :, 0:N_EXP], wr[:, :, :], wr_split)
            split_xT(2)
            act.wait_ge(logits_done, 1)
            copy(logitT[:, :], bank(4)[0:N_EXP, 0:T], logitsT_out)
            act.wait_ge(r_step, 4 + 3)
            for t in range(TT):
                act.activation(ex[:, t, :], logit[:, t, :], ACT.Exp, bias=top[:, 0, t:t + 1]).then_inc(r_exp, 1)

            def item_round(item, j):
                u = U_MOE + j
                act.wait_ge(raw_landed[u % RAW], landed(item, j))
                act.wait_ge(unit_used, item * ITEM_UNITS + (u - SPLIT + 1))
                act.activation(w_hi[:, u % SPLIT, :], raw[:, u % RAW, :], ACT.Copy).then_inc(hi_ready, 1)

            def hidden_hi(item, b):
                act.wait_ge(m_turned, item * E_BLOCKS + (b + 1))
                copy(mT_hi[:, b % 2].rearrange("p a t -> p (a t)"), bank(6), mT_hi_ready)

            def tokens_hi(item):
                act.wait_ge(gathered, item + 2)
                copy(g_hi[:, :, :].rearrange("p (b a) t -> p b (a t)", b=2), ps[:, 2:4, :], g_hi_ready)

            def output_hi(item):
                act.wait_ge(unit_used, item * ITEM_UNITS + (U_MOE + ITEM_UNITS))
                copy(y_hi[:, :].rearrange("p (b n) -> p b n", b=2), ps[:, 4:6, :], y_hi_ready)

            def run_item(item, first):
                blocks = item * E_BLOCKS
                base = item * ITEM_UNITS + U_MOE
                j = 0
                for b in range(E_BLOCKS):
                    item_round(item, j + SPLIT)
                    if b == 0 and not first:
                        output_hi(item - 1)
                    item_round(item, j + 1 + SPLIT)
                    act.wait_ge(unit_used, base + (j + 2))
                    if b == 0 and not first:
                        act.wait_ge(m_prod, blocks - 1)
                    elif b >= 2:
                        act.wait_ge(m_prod, blocks + (b - 1))
                    act.activation(m_g[:, b % 2, :], bank(2 * (b % 2)), ACT.Silu).then_inc(m_silu, 1)
                    if b >= 1:
                        hidden_hi(item, b - 1)
                    if b == 5:
                        act.wait_ge(place_turned, item + 1)
                        copy(place_r[:, :, :].rearrange("p a t -> p (a t)"), bank(7)[:, 0:T], place_ready)
                    item_round(item, j + 2 + SPLIT)
                    item_round(item, j + 3 + SPLIT)
                    j += 4
                    if b == E_BLOCKS - 1:
                        tokens_hi(item)
                    if b >= 1:
                        item_round(item, j + SPLIT)
                        if b == E_BLOCKS - 1:
                            hidden_hi(item, b)
                        else:
                            item_round(item, j + 1 + SPLIT)
                        j += 2
                if first:
                    for n in range(SPLIT):
                        item_round(item + 1, n)
                else:
                    with act.If(n_second > item - (N_EXP - 1)):
                        for n in range(SPLIT):
                            item_round(item + 1, n)

            tokens_hi(-1)
            run_item(0, True)
            act.wait_ge(routed, 1)
            n_second = act.value_load(second[0:1, 0:1], min_val=0, max_val=MAX_SECOND)
            with act.Fori(1, N_EXP) as item:
                run_item(item, False)
            with act.Fori(N_EXP, N_ITEMS) as item:
                with act.If(n_second > item - N_EXP):
                    run_item(item, False)
            output_hi(n_second + (N_EXP - 1))
            norm(3, y_sum)

        @block.vector
        def _(dve):
            def rest_unit(u):
                dve.wait_ge(hi_ready, u + 1)
                dve.tensor_tensor(w_lo[:, u % SPLIT, :], raw[:, u % RAW, :], w_hi[:, u % SPLIT, :].bitcast(F32),
                                  ALU.subtract).then_inc(lo_ready, 1)

            def rest(o, i, hi, s):
                dve.tensor_tensor(o, i, hi.bitcast(F32), ALU.subtract).then_inc(s, 1)

            for j in range(4):
                dve.wait_ge(xT_hi_ready, j + 1)
                rest(xT_lo[:, 2 * j:2 * j + 2, :], xT_raw[:, 2 * j:2 * j + 2, :], xT_hi[:, 2 * j:2 * j + 2, :], xT_lo_ready)
            for u in range(2 * IN_BLOCKS + SPLIT):
                rest_unit(u)

            for p in range(4):
                z = ps[:, 0:2, 0:384]
                dve.wait_ge(ret_scored, p + 1)
                if p >= 2:
                    dve.wait_ge(ret_pv, p - 1)
                dve.tensor_copy(ret_s[:, p % 2], ps[:, 2:4, 0:384]).then_inc(ret_copied, 1)
                dve.wait_ge(sb_log, p + 1)
                if p >= 2:
                    dve.wait_ge(sb_summed, p - 1)
                dve.scalar_tensor_tensor(out=sb_l[:, p % 2], in0=z, scalar=0.0, in1=sb_e[:, p % 2], op0=ALU.max,
                                         op1=ALU.add).then_inc(sb_softplus, 1)
                dve.wait_ge(oT_hi_ready, p + 1)
                rest(oT_lo[:, p, :], bank(4 + p % 2)[:, 0:T], oT_hi[:, p, :], oT_lo_ready)

            def heads(v):
                return v.rearrange("p (h d) -> p h d", d=HD)

            def per_head(v):
                return v.unsqueeze(2).broadcast_to((P, N_RET, HD))

            dve.wait_ge(ret_pv, 4)
            for t in range(TT):
                dve.tensor_reduce(gn_s[:, 0, t, :], heads(bank(6 + t)), AX, ALU.add).then_inc(gn_step, 1)
                dve.wait_ge(gn_step, 2 * t + 1)
                dve.scalar_tensor_tensor(out=heads(ret_o[:, t, :]), in0=per_head(gn_s[:, 0, t, :]),
                                         scalar=-1.0 / HD, in1=heads(bank(6 + t)), op0=ALU.mult,
                                         op1=ALU.add).then_inc(gn_step, 1)
            for t in range(TT):
                dve.wait_ge(gn_sq, t + 1)
                dve.tensor_reduce(gn_s[:, 1, t, :], heads(ret_sq[:, t, :]), AX, ALU.add).then_inc(gn_step, 1)
            dve.wait_ge(aux_landed[3], 16)
            n = 4 + TT
            for t in range(TT):
                dve.wait_ge(gn_std, t + 1)
                dve.reciprocal(gn_s[:, 0, t, :], gn_s[:, 2, t, :]).then_inc(gn_step, 1)
                n += 1
                dve.wait_ge(gn_step, n)
                dve.tensor_tensor(heads(ret_o[:, t, :]), heads(ret_o[:, t, :]), per_head(gn_s[:, 0, t, :]),
                                  ALU.mult).then_inc(gn_step, 1)
                n += 1
                dve.wait_ge(gn_step, n)
                dve.tensor_tensor(ret_o[:, t, :], ret_o[:, t, :], gn_row, ALU.mult).then_inc(gn_step, 1)
                n += 1
                dve.wait_ge(gn_step, n)
                dve.tensor_tensor(ret_o[:, t, :], ret_o[:, t, :], tokm[:, t, 4, :], ALU.mult).then_inc(ret_out, 1)
            for j in range(2):
                dve.wait_ge(oT_hi_ready, 4 + j + 1)
                c = slice(4 + 2 * j, 6 + 2 * j)
                rest(oT_lo[:, c, :].rearrange("p a t -> p (a t)"), bank(j),
                     oT_hi[:, c, :].rearrange("p a t -> p (a t)"), oT_lo_ready)
            for k in range(OUT_UNITS):
                rest_unit(U_OUT + k + SPLIT)

            def norm(n, v):
                for t in range(TT):
                    if n < 3:
                        if t == 0:
                            dve.wait_ge(tile0_done, n + 1)
                        else:
                            dve.wait_ge(unit_used, (U_FF, U_QKV, U_MOE)[n])
                        for h in range(2):
                            r = v[:, t, h * 512:(h + 1) * 512]
                            if n == 0 and t == 0 and h == 0:
                                dve.wait_ge(aux_landed[0], 16)
                            dve.scalar_tensor_tensor(out=r, in0=r, scalar=ALPHA, in1=bank(4 + 2 * t + h),
                                                     op0=ALU.mult, op1=ALU.add,
                                                     accum_out=sums[:, t, h:h + 1]).then_inc(ln_res, 1)
                        dve.wait_ge(ln_res, 4 * n + 2 * (t + 1))
                    dve.tensor_scalar(neg_mean[:, t:t + 1], sums[:, t, 0:1], sums[:, t, 1:2], -1.0 / D, ALU.add,
                                      ALU.mult).then_inc(ln_mean, 1)
                dve.wait_ge(aux_landed[2], 32 * (n + 1))
                for t in range(TT):
                    dve.wait_ge(ln_mean, TT * n + t + 1)
                    dve.scalar_tensor_tensor(out=ps[:, 4 + 2 * t:6 + 2 * t, :], in0=two(v[:, t, :]),
                                             scalar=neg_mean[:, t:t + 1], in1=two(norm_gb[:, 0, :]),
                                             op0=ALU.add, op1=ALU.mult).then_inc(ln_centred, 1)
                for t in range(TT):
                    dve.wait_ge(ln_std, TT * n + t + 1)
                    dve.reciprocal(rstd[:, t:t + 1], std[:, t:t + 1]).then_inc(ln_rstd, 1)
                    dve.wait_ge(ln_rstd, TT * n + t + 1)
                    dve.wait_ge(ln_centred, TT * n + t + 1)
                    for h in range(2):
                        c = slice(h * 512, (h + 1) * 512)
                        dve.scalar_tensor_tensor(out=v[:, t, c], in0=bank(4 + 2 * t + h), scalar=rstd[:, t:t + 1],
                                                 in1=norm_gb[:, 1, c], op0=ALU.mult, op1=ALU.add
                                                 ).then_inc(ln_done, 1)

            def split_xT(n):
                for j in range(4):
                    dve.wait_ge(xT_hi_ready, 4 * (n + 1) + j + 1)
                    c = slice(2 * j, 2 * j + 2)
                    rest(xT_lo[:, c, :].rearrange("p a t -> p (a t)"), bank(j),
                         xT_hi[:, c, :].rearrange("p a t -> p (a t)"), xT_lo_ready)

            norm(0, x_tok)
            split_xT(0)

            def ff_lo(b):
                dve.wait_ge(hT_hi_ready, b + 1)
                c = slice(2 * b, 2 * b + 2)
                rest(hT_lo[:, c, :].rearrange("p a t -> p (a t)"), ff_h[:, b % 2, :],
                     hT_hi[:, c, :].rearrange("p a t -> p (a t)"), hT_lo_ready)

            for b in range(FF_BLOCKS):
                rest_unit(U_FF + 2 * b + SPLIT)
                if b >= 1:
                    ff_lo(b - 1)
                dve.wait_ge(ff_silu, b + 1)
                dve.wait_ge(unit_used, U_FF + 2 * b + 2)
                dve.tensor_tensor(ff_h[:, b % 2, :], ff_g[:, b % 2, :], bank(2 * (b % 2) + 1),
                                  ALU.mult).then_inc(ff_prod, 1)
                rest_unit(U_FF + 2 * b + 1 + SPLIT)
            ff_lo(FF_BLOCKS - 1)
            for k in range(DOWN_UNITS):
                rest_unit(U_DOWN + k + SPLIT)
            norm(1, x_tok)
            split_xT(1)
            for u in range(U_QKV, U_OUT2):
                rest_unit(u + SPLIT)

            def c_lo(p):
                dve.wait_ge(c_oT_hi, p + 1)
                rest(oT_lo[:, p, :], bank(4 + p % 2)[:, 0:T], oT_hi[:, p, :], c_oT_lo)

            dve.wait_ge(aux_landed[4], 16)
            for p in range(N_C // 2):
                b0 = 2 * (p % 2)
                dve.wait_ge(c_scored, p + 1)
                if p >= 2:
                    dve.wait_ge(c_exped, 4 * (p - 1))
                bias = c_bias[:, 2 * p:2 * p + 2, :]
                dve.scalar_tensor_tensor(out=c_s[:, p % 2, :, 0:P], in0=ps[:, b0:b0 + 2, 0:P], scalar=HD ** -0.5,
                                         in1=bias[:, :, P:T], op0=ALU.mult, op1=ALU.add).then_inc(c_biased, 1)
                dve.scalar_tensor_tensor(out=c_s[:, p % 2, :, P:P + T], in0=ps[:, b0:b0 + 2, P:P + T],
                                         scalar=HD ** -0.5, in1=bias, op0=ALU.mult, op1=ALU.add).then_inc(c_biased, 1)
                dve.wait_ge(c_masked, 2 * (p + 1))
                dve.tensor_reduce(c_max[:, p, :, 0], c_s[:, p % 2, :, 0:P], AX, ALU.max,
                                  negate=True).then_inc(c_maxed, 1)
                dve.tensor_reduce(c_max[:, p, :, 1], c_s[:, p % 2, :, P:P + T], AX, ALU.max,
                                  negate=True).then_inc(c_maxed, 1)
                if p >= 1:
                    c_lo(p - 2) if p >= 2 else None
                dve.wait_ge(c_exped, 4 * (p + 1))
                dve.reciprocal(c_inv[:, p], c_sum[:, p]).then_inc(c_recip, 1)
                dve.wait_ge(c_recip, p + 1)
                for h in range(2):
                    for t, s in ((0, slice(0, P)), (1, slice(P, P + T))):
                        dve.tensor_scalar(c_p[:, p % 2, h, s], c_p[:, p % 2, h, s], c_inv[:, p, h, t:t + 1], None,
                                          ALU.mult).then_inc(c_normed, 1)
            c_lo(N_C // 2 - 2)
            c_lo(N_C // 2 - 1)
            for k in range(OUT_UNITS):
                rest_unit(U_OUT2 + k + SPLIT)
            norm(2, x_tok)

            dve.wait_ge(wr_split, 1)
            rest(wr_lo[:, :, 0:N_EXP], wr[:, :, :], wr_hi[:, :, 0:N_EXP], wr_split)
            split_xT(2)
            done = [4]

            def step(i):
                i.then_inc(r_step, 1)
                done[0] += 1
                dve.wait_ge(r_step, done[0])

            dve.wait_ge(logits_turned, 1)
            dve.wait_ge(aux_landed[6], 16)
            dve.wait_ge(r_step, 4)
            step(dve.tensor_tensor(logit[:, :, :], bank(5)[:, 64:64 + TT * N_EXP].rearrange("p (t e) -> p t e", t=TT),
                                   br[:, :].unsqueeze(1).broadcast_to((P, TT, N_EXP)), ALU.add))
            step(dve.tensor_reduce(top[:, 0, :], logit[:, :, :], AX, ALU.max, negate=True))
            every = (P, TT, N_EXP, N_EXP)
            other, own = logit[:, :, :].unsqueeze(2).broadcast_to(every), logit[:, :, :].unsqueeze(3).broadcast_to(every)
            step(dve.tensor_tensor(gt[:, :, :, :], other, own, ALU.is_gt))
            step(dve.tensor_tensor(eq[:, :, :, :], other, own, ALU.is_equal))
            step(dve.tensor_tensor(eq[:, :, :, :], eq[:, :, :, :], tri8[:, 0:1].broadcast_to(every), ALU.mult))
            step(dve.tensor_tensor(gt[:, :, :, :], gt[:, :, :, :], eq[:, :, :, :], ALU.add))
            step(dve.tensor_reduce(rank[:, :, :], gt[:, :, :, :], AX, ALU.add))
            dve.tensor_scalar(picked[:, :, :], rank[:, :, :], 2.0, None, ALU.is_lt).then_inc(picked_ready, 1)
            dve.wait_ge(picked_ready, 1)
            dve.wait_ge(slots_done, 1)
            c5 = bank(5)
            step(dve.tensor_copy(over[:, 0, :], c5[:, 16:24]))
            step(dve.scalar_tensor_tensor(out=rank[:, 0, :], in0=c5[:, 0:8], scalar=1.0, in1=picked[:, 0, :],
                                          op0=ALU.add, op1=ALU.mult))
            step(dve.tensor_tensor(rank[:, 1, :], c5[:, 8:16], over[:, 0, :], ALU.subtract))
            step(dve.scalar_tensor_tensor(out=rank[:, 1, :], in0=rank[:, 1, :], scalar=1.0, in1=picked[:, 1, :],
                                          op0=ALU.add, op1=ALU.mult))
            step(dve.tensor_scalar(route[:, 0:N_EXP, 0, :], rank[:, :, :].rearrange("p t e -> p e t"), -1.0, None,
                                   ALU.add))

            def weigh():
                dve.wait_ge(r_exp, 2)
                step(dve.tensor_tensor(ex[:, :, :], ex[:, :, :], picked[:, :, :], ALU.mult))
                step(dve.tensor_reduce(top[:, 2, :], ex[:, :, :], AX, ALU.add))
                step(dve.reciprocal(top[:, 3, :], top[:, 2, :]))
                for t in range(TT):
                    step(dve.tensor_scalar(route[:, 0:N_EXP, 1, t], ex[:, t, :], top[:, 3, t:t + 1], None, ALU.mult))

            def second_items():
                step(dve.tensor_tensor(over[:, 1, :], over[:, 0, :], c5[:, 24:32], ALU.add))
                step(dve.tensor_scalar(over[:, 2, :], over[:, 1, :], -float(P), None, ALU.is_lt))
                step(dve.tensor_tensor(gt[:, 0], over[:, 2, :].unsqueeze(1).broadcast_to((P, N_EXP, N_EXP)),
                                       tri8[:, 1], ALU.mult))
                step(dve.tensor_reduce(over[:, 3, :], gt[:, 0], AX, ALU.add))
                step(dve.tensor_reduce(second_f[:, 0:1], over[:, 2, :], AX, ALU.add))
                step(dve.memset(route[:, N_ITEMS, :, :], -1.0))
                for s in range(MAX_SECOND):
                    step(dve.scalar_tensor_tensor(out=over[:, 0, :], in0=over[:, 3, :], scalar=float(s + 1),
                                                  in1=over[:, 2, :], op0=ALU.is_equal, op1=ALU.mult))
                    step(dve.tensor_tensor(over[:, 4, :], over[:, 0, :], num8[:, :], ALU.mult))
                    step(dve.tensor_reduce(second_f[:, s + 1:s + 2], over[:, 4, :], AX, ALU.add))
                    v = gt[:, 0].rearrange("p a b -> p (a b)")[:, 0:4 * N_EXP].rearrange("p (n e) -> p n e", n=4)
                    step(dve.tensor_tensor(v, route[:, 0:N_EXP].rearrange("p e a t -> p (a t) e"),
                                           over[:, 0, :].unsqueeze(1).broadcast_to((P, 4, N_EXP)), ALU.mult))
                    r = route[:, N_EXP + s]
                    step(dve.tensor_reduce(r.rearrange("p a t -> p (a t)"), v, AX, ALU.add))
                    step(dve.tensor_scalar(r[:, 0, :], r[:, 0, :], -float(P), None, ALU.add))
                dve.tensor_copy(second[:, :], second_f[:, :]).then_inc(routed, 1)

            def item_rest(item, j):
                u = U_MOE + j
                dve.wait_ge(hi_ready, item * ITEM_UNITS + (u + 1))
                dve.tensor_tensor(w_lo[:, u % SPLIT, :], raw[:, u % RAW, :], w_hi[:, u % SPLIT, :].bitcast(F32),
                                  ALU.subtract).then_inc(lo_ready, 1)

            def pick_tokens(item):
                dve.tensor_copy(cur[:, :], route[:, bass.ds(item + 1, 1), 0, :].rearrange("p a t -> p (a t)")
                                ).then_inc(cur_ready, 1)
                dve.wait_ge(cur_ready, item + 2)
                for t in range(TT):
                    m = dve.tensor_scalar(pick[:, t, :], slots, cur[:, t:t + 1], None, ALU.is_equal)
                m.then_inc(pick_ready, 1)

            def tokens_lo(item):
                dve.wait_ge(g_hi_ready, item + 2)
                rest(g_lo[:, :, :].rearrange("p (b a) t -> p b (a t)", b=2), ps[:, 2:4, :],
                     g_hi[:, :, :].rearrange("p (b a) t -> p b (a t)", b=2), g_lo_ready)

            def output_lo(item):
                dve.wait_ge(y_hi_ready, item + 1)
                rest(y_lo[:, :].rearrange("p (b n) -> p b n", b=2), ps[:, 4:6, :],
                     y_hi[:, :].rearrange("p (b n) -> p b n", b=2), y_lo_ready)

            def hidden_lo(item, b):
                dve.wait_ge(mT_hi_ready, item * E_BLOCKS + (b + 1))
                rest(mT_lo[:, b % 2].rearrange("p a t -> p (a t)"), bank(6),
                     mT_hi[:, b % 2].rearrange("p a t -> p (a t)"), mT_lo_ready)

            def add_output(item, n, b):
                t, h = n // 2, n % 2
                dve.wait_ge(scattered, item * 4 + (n + 1))
                v = y_sum[:, t, h * 512:(h + 1) * 512]
                dve.scalar_tensor_tensor(out=v, in0=b, scalar=weight[:, t:t + 1], in1=v, op0=ALU.mult,
                                         op1=ALU.add, accum_out=sums[:, t, h:h + 1]).then_inc(y_added, 1)

            def run_item(item, first):
                blocks = item * E_BLOCKS
                base = item * ITEM_UNITS + U_MOE
                j = 0
                for b in range(E_BLOCKS):
                    item_rest(item, j + SPLIT)
                    if b == 0 and not first:
                        output_lo(item - 1)
                    item_rest(item, j + 1 + SPLIT)
                    if b >= 1:
                        hidden_lo(item, b - 1)
                    if 1 <= b <= 4 and not first:
                        add_output(item - 1, b - 1, bank(7))
                    if b == 5:
                        if not first:
                            dve.wait_ge(y_added, item * 4 + 1)
                        dve.tensor_copy(weight[:, :], route[:, bass.ds(item, 1), 1, :].rearrange("p a t -> p (a t)")
                                        ).then_inc(weight_ready, 1)
                        dve.wait_ge(weight_ready, item + 1)
                        dve.wait_ge(place_turned, item + 1)
                        pick_tokens(item)
                    item_rest(item, j + 2 + SPLIT)
                    item_rest(item, j + 3 + SPLIT)
                    dve.wait_ge(m_silu, blocks + (b + 1))
                    dve.wait_ge(unit_used, base + (j + 4))
                    dve.tensor_tensor(m_h[:, b % 2, :], m_g[:, b % 2, :], bank(2 * (b % 2) + 1),
                                      ALU.mult).then_inc(m_prod, 1)
                    j += 4
                    if b == E_BLOCKS - 1:
                        tokens_lo(item)
                    if b >= 1:
                        item_rest(item, j + SPLIT)
                        if b == E_BLOCKS - 1:
                            hidden_lo(item, b)
                        else:
                            item_rest(item, j + 1 + SPLIT)
                        j += 2
                if first:
                    for n in range(SPLIT):
                        item_rest(item + 1, n)
                else:
                    with dve.If(n_second > item - (N_EXP - 1)):
                        for n in range(SPLIT):
                            item_rest(item + 1, n)

            pick_tokens(-1)
            weigh()
            dve.tensor_scalar(y_sum[:, :, :], x_tok[:, :, :], ALPHA, None, ALU.mult).then_inc(y_added, 1)
            tokens_lo(-1)
            second_items()
            dve.wait_ge(routed, 1)
            n_second = dve.value_load(second[0:1, 0:1], min_val=0, max_val=MAX_SECOND)
            run_item(0, True)
            with dve.Fori(1, N_EXP) as item:
                run_item(item, False)
            with dve.Fori(N_EXP, N_ITEMS) as item:
                with dve.If(n_second > item - N_EXP):
                    run_item(item, False)
            output_lo(n_second + (N_EXP - 1))
            for n in range(4):
                add_output(n_second + (N_EXP - 1), n, bank(n))
            dve.wait_ge(y_added, n_second * 4 + (N_EXP * 4 + 1))
            norm(3, y_sum)


def constants():
    r, c = np.arange(P)[:, None], np.arange(P)[None, :]
    full = np.ones((P, P))
    parts = [r == c, -1.0 * (r >= c), -full, r < c, full * c]
    return np.stack([np.asarray(a, np.float32) for a in parts], axis=1)


def rotation_tables():
    half = HD // 2
    pos = np.arange(T, dtype=np.float64)
    ang = pos[:, None] * 10000.0 ** (-np.arange(half, dtype=np.float64) / half)[None, :]
    gamma = 1.0 - 2.0 ** (-5.0 - np.arange(N_RET, dtype=np.float64))
    grow = gamma[None, :] ** pos[:, None]
    q, k = (grow * HD ** -0.5)[:, :, None], (1.0 / grow)[:, :, None]
    cos, sin = np.cos(ang)[:, None, :], np.sin(ang)[:, None, :]
    tab = np.stack([q * cos, q * sin, k * cos, k * sin], axis=1).reshape(T, 4, N_RET * half)
    return np.ascontiguousarray(tab.reshape(TT, P, 4, 256).transpose(1, 0, 2, 3).astype(np.float32))


def kernel(**inputs):
    import concourse.bacc as bacc
    from concourse.bass_utils import run_bass_kernel_spmd as run

    a = {k: np.asarray(v) for k, v in inputs.items()}
    x = a["x"].reshape(T, D)
    at = MAX_REL + P + np.arange(P)[:, None] - np.arange(T)[None, :]
    arrays = {
        "x": x, "xT": x.T,
        "ln_g": np.concatenate([a["even_ln1_g"], a["even_ln2_g"], a["odd_ln1_g"], a["odd_ln2_g"]]),
        "ln_b": np.concatenate([a["even_ln1_b"], a["even_ln2_b"], a["odd_ln1_b"], a["odd_ln2_b"]]),
        "w_in": a["even_w_in"][0], "gn_g": a["even_ret_gn_g"], "w_out": a["even_w_out"][0],
        "w_gate": a["even_w_gate"][0], "w_up": a["even_w_up"][0], "w_down": a["even_w_down"][0],
        "w_qkv": a["odd_w_qkv"][0], "bias_win": a["odd_rel_bias"][0][:, at].transpose(1, 0, 2),
        "w_out2": a["odd_w_out"][0], "w_router": a["odd_w_router"][0], "b_router": a["odd_b_router"],
        "e_gate": a["odd_w_gate"][0], "e_up": a["odd_w_up"][0], "e_down": a["odd_w_down"][0],
        "tables": rotation_tables(), "consts": constants(),
    }
    nc = bacc.Bacc("TRN2", target_bir_lowering=False, num_devices=1)
    arrays = {k: np.ascontiguousarray(v) for k, v in arrays.items()}
    args = [nc.dram_tensor(k, v.shape, F32, kind="ExternalInput").ap() for k, v in arrays.items()]
    out = nc.dram_tensor("out", (T, D), F32, kind="ExternalOutput").ap()
    trunk_kernel(nc, *args, out)
    return run(nc, [arrays], core_ids=[0]).results[0]["out"].reshape(1, T, D)
```

```python
from contextlib import ExitStack

import concourse.bass as bass
import numpy as np
from concourse import mybir

F32 = mybir.dt.float32
F32R = mybir.dt.float32r
I32 = mybir.dt.int32
ALU = mybir.AluOpType
ACT = mybir.ActivationFunctionType
AX = mybir.AxisListType.X

P = 128
D = 1024
T = 256
TT = T // P
KC = D // P
HD = 64
CHUNK = 64
N_RET = 8
N_C = 16
F_DENSE = 2816
F_EXP = 3584
N_EXP = 8
MAX_REL = 256
ALPHA = 4.0 ** 0.25
EPS = 1e-5
UC = 2048
RAW = 7
SPLIT = 3
MASKED = -1e30

IN_BLOCKS = 7
OUT_UNITS = 4
FF_BLOCKS = F_DENSE // 256
DOWN_UNITS = F_DENSE // 256
QKV_BLOCKS = 6
U_IN = 0
U_OUT = U_IN + 2 * IN_BLOCKS
U_FF = U_OUT + OUT_UNITS
U_DOWN = U_FF + 2 * FF_BLOCKS
U_QKV = U_DOWN + DOWN_UNITS
U_OUT2 = U_QKV + 2 * QKV_BLOCKS
U_MOE = U_OUT2 + OUT_UNITS
E_BLOCKS = F_EXP // 512
ITEM_UNITS = 6 * E_BLOCKS
MAX_SECOND = (2 * T) // (P + 1)
N_ITEMS = N_EXP + MAX_SECOND


IN_ORDER = (3, 4, 5, 0, 1, 6, 2)
OUT_CHUNKS = (4, 6, 0, 2)
PLAN_0 = (
    ("unit", 0), ("round", 3), ("rest", 3), ("unit", 1), ("round", 4), ("rest", 4), ("rotate", 0),
    ("unit", 2), ("round", 5), ("rest", 5), ("unit", 3), ("round", 6), ("rest", 6), ("rotate", 1),
    ("unit", 4), ("round", 7), ("rest", 7), ("turn", 0),
    ("unit", 5), ("round", 8), ("rest", 8), ("turn", 1),
    ("unit", 6), ("round", 9), ("rest", 9), ("ret_scores", 0),
    ("unit", 7), ("round", 10), ("rest", 10), ("ret_scores", 1), ("ret_values", 0),
    ("unit", 8), ("round", 11), ("rest", 11), ("ret_scores", 2), ("ret_values", 1),
    ("unit", 9), ("round", 12), ("rest", 12), ("ret_scores", 3), ("ret_values", 2),
    ("unit", 10), ("ret_values", 3), ("ret_centre", 0), ("round", 13), ("rest", 13),
    ("ret_scale", 0), ("sb_scores", 0), ("ret_scale", 1),
    ("unit", 11), ("ret_gate", 0), ("round", 14), ("rest", 14), ("sb_scores", 1),
    ("unit", 12), ("round", 15), ("rest", 15), ("sb_sums", 0), ("ret_turn", 0),
    ("unit", 13), ("sb_sums", 1), ("sb_values", 0), ("round", 16), ("rest", 16),
    ("out", 0), ("sb_scores", 2), ("sb_values", 1),
    ("out", 1), ("sb_scores", 3), ("round", 17), ("rest", 17),
    ("out", 2), ("out", 3), ("round", 18), ("rest", 18), ("sb_sums", 2),
    ("out", 4), ("sb_sums", 3), ("sb_values", 2),
    ("out", 5), ("sb_values", 3), ("round", 19),
    ("out", 6), ("out", 7),
)

QKV_ORDER = (0, 2, 4, 1, 3, 5)
PLAN_1 = (
    ("unit", 0), ("round", 3), ("rest", 3), ("unit", 1), ("round", 4), ("rest", 4),
    ("unit", 2), ("round", 5), ("rest", 5), ("unit", 3), ("round", 6), ("rest", 6),
    ("unit", 4), ("scores", 0), ("round", 7), ("rest", 7), ("weights", 0),
    ("unit", 5), ("turn", 0), ("scores", 1), ("round", 8), ("rest", 8), ("weights", 1),
    ("unit", 6), ("values", 0), ("turn", 1), ("scores", 2), ("round", 9), ("rest", 9), ("weights", 2),
    ("unit", 7), ("values", 1), ("turn", 2), ("scores", 3), ("round", 10), ("rest", 10), ("weights", 3),
    ("unit", 8), ("values", 2), ("turn", 3), ("round", 11), ("rest", 11),
    ("unit", 9), ("values", 3), ("round", 12), ("rest", 12),
    ("unit", 10), ("scores", 4), ("scores", 5), ("round", 13), ("weights", 4), ("rest", 13), ("weights", 5),
    ("unit", 11), ("turn", 4), ("round", 14), ("rest", 14),
    ("out", 0), ("values", 4), ("turn", 5),
    ("out", 1), ("values", 5), ("scores", 6), ("round", 15), ("weights", 6),
    ("out", 2), ("scores", 7), ("rest", 15),
    ("out", 3), ("turn", 6), ("weights", 7), ("round", 16), ("rest", 16),
    ("out", 4), ("values", 6), ("turn", 7),
    ("out", 5), ("values", 7), ("round", 17),
    ("out", 6), ("out", 7),
)


def item_units():
    units = []
    for b in range(E_BLOCKS + 1):
        if b < E_BLOCKS:
            units += [("gate", b, 0), ("gate", b, 1), ("up", b, 0), ("up", b, 1)]
        if b >= 1:
            units += [("down", b - 1, 0), ("down", b - 1, 1)]
    return units


def trunk_kernel(nc, x, xT, ln_g, ln_b, w_in, gn_g, w_out, w_gate, w_up, w_down, w_qkv, bias_win,
                 w_out2, w_router, b_router, e_gate, e_up, e_down, tables, consts, out):
    ctx = ExitStack()
    with ctx:
        def sem(name):
            return ctx.enter_context(nc.semaphore(name))

        def sb(stack, name, shape, dt=F32):
            return stack.enter_context(nc.sbuf_tensor(name, shape, dt))

        raw = sb(ctx, "raw", [P, RAW, UC])
        w_hi = sb(ctx, "w_hi", [P, SPLIT, UC], F32R)
        w_lo = sb(ctx, "w_lo", [P, SPLIT, UC], F32R)
        x_tok = sb(ctx, "x_tok", [P, TT, D])
        xT_hi = sb(ctx, "xT_hi", [P, KC, T], F32R)
        xT_lo = sb(ctx, "xT_lo", [P, KC, T], F32R)
        norm_gb = sb(ctx, "norm_gb", [P, 2, D])
        cst = sb(ctx, "cst", [P, 5, P])
        small = sb(ctx, "small", [P, 64])
        ident, neg_tri, neg_ones, before, slots = (cst[:, n, :] for n in range(5))
        eps_col = small[:, 0:1]
        sums = small[:, 2:6].rearrange("p (t h) -> p t h", t=TT)
        neg_mean, squares, std, rstd = (small[:, n:n + TT] for n in (6, 8, 10, 12))
        spare = small[:, 14:15]

        st = ExitStack()
        sb_qkT = sb(st, "sb_qkT", [P, 8, T])
        tokm = sb(st, "tokm", [P, TT, 5, 512])
        rot = sb(st, "rot", [P, TT, 4, 256])
        sb_e = sb(st, "sb_e", [P, 2, 2, 384])
        sb_l = sb(st, "sb_l", [P, 2, 2, 384])
        sb_w = sb(st, "sb_w", [P, 2, 2, 384])
        ret_s = sb(st, "ret_s", [P, 2, 2, 384])
        qk_st = ExitStack()
        ret_qkT = sb(qk_st, "ret_qkT", [P, 8, T])
        qk_st.close()
        ret_oT_hi = sb(st, "ret_oT_hi", [P, 4, T], F32R)
        ret_oT_lo = sb(st, "ret_oT_lo", [P, 4, T], F32R)
        xT_raw = ret_qkT
        oT_hi, oT_lo = xT_hi, xT_lo
        sb_w_words = sb_w[:, :, :, :].rearrange("p a b c -> p (a b c)")
        rot_t = sb_w_words[:, 0:1024].rearrange("p (n f) -> p n f", n=4)
        gn_row = sb_w_words[:, 1024:1536]
        ret_o = rot[:, 0].rearrange("p a b -> p (a b)").rearrange("p (t n) -> p t n", t=TT)
        ret_sq = rot[:, 1].rearrange("p a b -> p (a b)").rearrange("p (t n) -> p t n", t=TT)
        gn_s = small[:, 16:64].rearrange("p (a t h) -> p a t h", a=3, t=TT)
        st.close()
        st = ExitStack()
        hT_hi = sb(st, "hT_hi", [P, 2 * FF_BLOCKS, T], F32R)
        hT_lo = sb(st, "hT_lo", [P, 2 * FF_BLOCKS, T], F32R)
        ff_g = sb(st, "ff_g", [P, 2, 512])
        ff_h = sb(st, "ff_h", [P, 2, 512])
        st.close()
        st = ExitStack()
        c_qkT = sb(st, "c_qkT", [P, 16, T])
        c_v = sb(st, "c_v", [P, TT, D])
        c_bias = sb(st, "c_bias", [P, N_C, T])
        c_s = sb(st, "c_s", [P, 2, 2, 384])
        c_p = sb(st, "c_p", [P, 2, 2, 384])
        c_pT = sb(st, "c_pT", [P, 2, 2, 384])
        c_oT_hi = sb(st, "c_oT_hi", [P, 4, T], F32R)
        c_oT_lo = sb(st, "c_oT_lo", [P, 4, T], F32R)
        c_max = sb(st, "c_max", [P, 8, 2, 2])
        c_sum = sb(st, "c_sum", [P, 8, 2, 2])
        c_inv = sb(st, "c_inv", [P, 8, 2, 2])
        st.close()
        st = ExitStack()
        y_sum = sb(st, "y_sum", [P, TT, D])
        g_hi = sb(st, "g_hi", [P, KC, P], F32R)
        g_lo = sb(st, "g_lo", [P, KC, P], F32R)
        m_g = sb(st, "m_g", [P, 2, 512])
        m_h = sb(st, "m_h", [P, 2, 512])
        mT_hi = sb(st, "mT_hi", [P, 2, 4, P], F32R)
        mT_lo = sb(st, "mT_lo", [P, 2, 4, P], F32R)
        y_hi = sb(st, "y_hi", [P, D], F32R)
        y_lo = sb(st, "y_lo", [P, D], F32R)
        pick = sb(st, "pick", [P, TT, P])
        place_r = sb(st, "place_r", [P, TT, P], F32R)
        cur = sb(st, "cur", [P, TT])
        weight = sb(st, "weight", [P, TT])
        route = sb(st, "route", [P, N_ITEMS + 1, 2, TT])
        wr = sb(st, "wr", [P, KC, N_EXP])
        wr_hi = sb(st, "wr_hi", [P, KC, P], F32R)
        wr_lo = sb(st, "wr_lo", [P, KC, P], F32R)
        logitT = sb(st, "logitT", [N_EXP, T])
        br = sb(st, "br", [P, N_EXP])
        logit = sb(st, "logit", [P, TT, N_EXP])
        gt = sb(st, "gt", [P, TT, N_EXP, N_EXP])
        eq = sb(st, "eq", [P, TT, N_EXP, N_EXP])
        tri8 = sb(st, "tri8", [P, 2, N_EXP, N_EXP])
        ones = sb(st, "ones", [P, P])
        num8 = sb(st, "num8", [P, N_EXP])
        rank = sb(st, "rank", [P, TT, N_EXP])
        picked = sb(st, "picked", [P, TT, N_EXP])
        top = sb(st, "top", [P, 4, TT])
        ex = sb(st, "ex", [P, TT, N_EXP])
        over = sb(st, "over", [P, 5, N_EXP])
        second_f = sb(st, "second_f", [P, 4])
        second = sb(st, "second", [P, 4], I32)
        st.close()

        ps = ctx.enter_context(nc.psum_tensor("ps", [P, 8, 512], F32))

        def bank(n):
            return ps[:, n, :]

        def c_out(p, hi):
            if p < 4:
                return (c_oT_hi if hi else c_oT_lo)[:, p, :]
            return (oT_hi if hi else oT_lo)[:, p, :]

        def by_tile(v):
            return v.rearrange("p (t n) -> p t n", t=TT)

        def two(v):
            return v.rearrange("p (b n) -> p b n", b=2)

        first_landed = sem("first_landed")
        first_hi_ready = sem("first_hi_ready")
        first_lo_ready = sem("first_lo_ready")
        raw_landed = [sem(f"raw_landed{n}") for n in range(RAW)]
        consts_landed = sem("consts_landed")
        xT_landed = [sem(f"xT_landed{n}") for n in range(2)]
        aux_landed = [sem(f"aux_landed{n}") for n in range(8)]
        hi_ready = sem("hi_ready")
        lo_ready = sem("lo_ready")
        unit_used = sem("unit_used")
        xT_hi_ready = sem("xT_hi_ready")
        xT_lo_ready = sem("xT_lo_ready")
        eps_ready = sem("eps_ready")
        in_out = sem("in_out")
        rot_step = sem("rot_step")
        rot_done = sem("rot_done")
        ret_turned = sem("ret_turned")
        ret_qkT_ready = sem("ret_qkT_ready")
        sb_scored = sem("sb_scored")
        sb_abs = sem("sb_abs")
        sb_exp = sem("sb_exp")
        sb_log = sem("sb_log")
        sb_softplus = sem("sb_softplus")
        sb_l_masked = sem("sb_l_masked")
        sb_summed = sem("sb_summed")
        sb_weights = sem("sb_weights")
        sb_w_masked = sem("sb_w_masked")
        sb_pv = sem("sb_pv")
        oT_hi_ready = sem("oT_hi_ready")
        oT_lo_ready = sem("oT_lo_ready")
        ret_scored = sem("ret_scored")
        ret_copied = sem("ret_copied")
        ret_masked = sem("ret_masked")
        ret_pv = sem("ret_pv")
        gn_step = sem("gn_step")
        gn_sq = sem("gn_sq")
        gn_std = sem("gn_std")
        ret_out = sem("ret_out")
        ret_o_turned = sem("ret_o_turned")
        ret_oT_hi_ready = sem("ret_oT_hi_ready")
        ret_oT_lo_ready = sem("ret_oT_lo_ready")
        ln_res = sem("ln_res")
        ln_mean = sem("ln_mean")
        ln_centred = sem("ln_centred")
        ln_rstd = sem("ln_rstd")
        tile0_done = sem("tile0_done")
        ln_sq_done = sem("ln_sq_done")
        ln_std = sem("ln_std")
        ln_done = sem("ln_done")
        x_turned = sem("x_turned")
        ff_silu = sem("ff_silu")
        ff_prod = sem("ff_prod")
        hT_hi_ready = sem("hT_hi_ready")
        hT_lo_ready = sem("hT_lo_ready")
        qkv_out = sem("qkv_out")
        c_scored = sem("c_scored")
        c_biased = sem("c_biased")
        c_masked = sem("c_masked")
        c_maxed = sem("c_maxed")
        c_exped = sem("c_exped")
        c_recip = sem("c_recip")
        c_normed = sem("c_normed")
        c_turned = sem("c_turned")
        c_pT_ready = sem("c_pT_ready")
        c_pv = sem("c_pv")
        c_o_hi_ready = sem("c_o_hi_ready")
        c_o_lo_ready = sem("c_o_lo_ready")
        wr_zeroed = sem("wr_zeroed")
        wr_split = sem("wr_split")
        logitsT_out = sem("logitsT_out")
        logits_done = sem("logits_done")
        logits_turned = sem("logits_turned")
        r_step = sem("r_step")
        r_exp = sem("r_exp")
        ones_ready = sem("ones_ready")
        picked_ready = sem("picked_ready")
        slots_done = sem("slots_done")
        routed = sem("routed")
        pick_ready = sem("pick_ready")
        place_turned = sem("place_turned")
        place_ready = sem("place_ready")
        gathered = sem("gathered")
        g_hi_ready = sem("g_hi_ready")
        g_lo_ready = sem("g_lo_ready")
        m_silu = sem("m_silu")
        m_prod = sem("m_prod")
        m_turned = sem("m_turned")
        mT_hi_ready = sem("mT_hi_ready")
        mT_lo_ready = sem("mT_lo_ready")
        y_hi_ready = sem("y_hi_ready")
        y_lo_ready = sem("y_lo_ready")
        scattered = sem("scattered")
        y_added = sem("y_added")
        cur_ready = sem("cur_ready")
        weight_ready = sem("weight_ready")
        stored = sem("stored")

        dense = []
        for c in IN_ORDER:
            for k in range(2):
                dense.append(w_in[k * 512:(k + 1) * 512, c * 512:(c + 1) * 512].rearrange("(k p) n -> p k n", p=P))
        for c in OUT_CHUNKS:
            dense.append(w_out[c * P:(c + 2) * P, :].rearrange("(k p) n -> p k n", p=P))
        for b in range(FF_BLOCKS):
            for w in (w_gate, w_up):
                dense.append(w[:, b * 256:(b + 1) * 256].rearrange("(k p) n -> p k n", p=P))
        for k in range(DOWN_UNITS):
            dense.append(w_down[k * 256:(k + 1) * 256, :].rearrange("(k p) n -> p k n", p=P))
        for c in QKV_ORDER:
            for k in range(2):
                dense.append(w_qkv[k * 512:(k + 1) * 512, c * 512:(c + 1) * 512].rearrange("(k p) n -> p k n", p=P))
        for k in range(OUT_UNITS):
            dense.append(w_out2[k * 256:(k + 1) * 256, :].rearrange("(k p) n -> p k n", p=P))
        assert len(dense) == U_MOE
        units = item_units()
        assert len(units) == ITEM_UNITS and ITEM_UNITS % RAW == 0 and ITEM_UNITS % SPLIT == 0

        def raw_slot(u, n):
            return raw[:, u % RAW, :].rearrange("p (k n) -> p k n", n=n)

        def hi_slot(u, n):
            return w_hi[:, u % SPLIT, :].rearrange("p (k n) -> p k n", n=n)

        def lo_slot(u, n):
            return w_lo[:, u % SPLIT, :].rearrange("p (k n) -> p k n", n=n)

        def landed(item, j):
            u = U_MOE + j
            return item * (16 * (ITEM_UNITS // RAW)) + 16 * (u // RAW + 1)

        block = ctx.enter_context(nc.Block())

        @block.sync
        def _(sp):
            def free(u):
                sp.wait_ge(lo_ready, u - RAW + 1)

            x_src = xT.rearrange("(k p) t -> p k t", p=P)
            for h in range(2):
                k = slice(4 * h, 4 * h + 4)
                sp.dma_start(xT_raw[:, k, :], x_src[:, k, :]).then_inc(xT_landed[h], 16)
                kk = slice(2 * h, 2 * h + 2)
                sp.dma_start(raw_slot(0, 512)[:, kk, :], dense[0][:, kk, :]).then_inc(
                    raw_landed[0] if h == 1 else first_landed, 16)
            for u, src in enumerate(dense):
                if u == 0:
                    continue
                if u >= RAW:
                    free(u)
                sp.dma_start(raw_slot(u, src.shape[2]), src).then_inc(raw_landed[u % RAW], 16)
                if u == 2:
                    sp.dma_start(rot[:, :, :, :], tables).then_inc(aux_landed[1], 16)

            def load_item(item, e):
                for j, (kind, b, half) in enumerate(units):
                    u = U_MOE + j
                    free(item * ITEM_UNITS + u)
                    if kind == "down":
                        src = e_down[e, b * 512 + half * 256:b * 512 + (half + 1) * 256, :]
                        n = D
                    else:
                        w = e_gate if kind == "gate" else e_up
                        src = w[e, half * 512:(half + 1) * 512, b * 512:(b + 1) * 512]
                        n = 512
                    sp.dma_start(raw_slot(u, n), src.rearrange("(k p) n -> p k n", p=P)).then_inc(
                        raw_landed[u % RAW], 16)

            with sp.Fori(0, N_EXP) as item:
                load_item(item, item)
            sp.wait_ge(routed, 1)
            n_second = sp.value_load(second[0:1, 0:1], min_val=0, max_val=MAX_SECOND)
            with sp.Fori(0, MAX_SECOND) as s:
                with sp.If(n_second > s):
                    e = sp.value_load(second[0:1, bass.ds(s + 1, 1)], min_val=0, max_val=N_EXP - 1)
                    load_item(s + N_EXP, e)
            for t in range(TT):
                for h in range(2):
                    sp.wait_ge(ln_done, 12 + 2 * t + h + 1)
                    c = slice(h * 512, (h + 1) * 512)
                    sp.dma_start(out[t * P:(t + 1) * P, c], y_sum[:, t, c]).then_inc(stored, 16)
            sp.wait_ge(stored, 16 * 2 * TT)

        @block.gpsimd
        def _(pool):
            pool.memset(eps_col, EPS).then_inc(eps_ready, 1)
            pool.dma_start(cst[:, :, :], consts).then_inc(consts_landed, 16)
            pool.wait_ge(unit_used, 4)
            pool.dma_start(x_tok[:, :, :], x.rearrange("(t p) d -> p t d", p=P)).then_inc(aux_landed[0], 16)

            def load_norm(n):
                if n >= 1:
                    pool.wait_ge(ln_done, 4 * n)
                pool.dma_start(norm_gb[:, 0, :], ln_g[n:n + 1, :].broadcast_to((P, D))).then_inc(aux_landed[2], 16)
                pool.dma_start(norm_gb[:, 1, :], ln_b[n:n + 1, :].broadcast_to((P, D))).then_inc(aux_landed[2], 16)

            load_norm(0)
            pool.wait_ge(rot_done, 8)
            pool.dma_start(gn_row, gn_g.broadcast_to((P, 512))).then_inc(aux_landed[3], 16)

            def mask_diagonals(t, strict):
                for h in range(2):
                    v = t[:, h, :].rearrange("p (b q) -> p b q", q=P)[:, 0:3:2, :]
                    m = pool.affine_select(out=v, in_=v, compare_op=ALU.is_gt if strict else ALU.is_ge, fill=0.0,
                                           base=0, pattern=[[0, 2], [1, P]], channel_multiplier=-1)
                return m

            for step, p in PLAN_0:
                if step == "ret_scores":
                    pool.wait_ge(ret_copied, p + 1)
                    mask_diagonals(ret_s[:, p % 2], False).then_inc(ret_masked, 1)
                elif step == "sb_scores":
                    pool.wait_ge(sb_softplus, p + 1)
                    mask_diagonals(sb_l[:, p % 2], True).then_inc(sb_l_masked, 1)
                elif step == "sb_sums":
                    pool.wait_ge(sb_weights, p + 1)
                    mask_diagonals(sb_w[:, p % 2], True).then_inc(sb_w_masked, 1)

            load_norm(1)

            pool.wait_ge(unit_used, U_QKV)
            pool.dma_start(c_bias[:, :, :], bias_win).then_inc(aux_landed[4], 16)
            load_norm(2)
            for p in range(N_C // 2):
                pool.wait_ge(c_biased, 2 * (p + 1))
                pool.memset(c_s[0:CHUNK, p % 2, :, CHUNK:P], MASKED).then_inc(c_masked, 1)
                pool.memset(c_s[0:CHUNK, p % 2, :, 2 * P + CHUNK:3 * P], MASKED).then_inc(c_masked, 1)

            pool.wait_ge(unit_used, U_MOE)
            pool.dma_start(wr[:, :, :], w_router.rearrange("(k p) e -> p k e", p=P)).then_inc(aux_landed[5], 16)
            pool.memset(wr_hi[:, :, :].bitcast(F32), 0.0).then_inc(wr_zeroed, 1)
            pool.memset(wr_lo[:, :, :].bitcast(F32), 0.0).then_inc(wr_zeroed, 1)
            pool.dma_start(br[:, :], b_router.broadcast_to((P, N_EXP))).then_inc(aux_landed[6], 16)
            pool.memset(ones[:, :], 1.0).then_inc(ones_ready, 1)
            pool.memset(tri8[:, :, :, :], 1.0).then_inc(r_step, 1)
            pool.iota(num8[:, :], pattern=[[1, N_EXP]], base=0, channel_multiplier=0,
                      allow_small_or_imprecise_dtypes=True).then_inc(r_step, 1)
            pool.wait_ge(r_step, 1)
            pool.affine_select(out=tri8[:, 0], in_=tri8[:, 0], compare_op=ALU.is_gt, fill=0.0, base=0,
                               pattern=[[1, N_EXP], [-1, N_EXP]], channel_multiplier=0).then_inc(r_step, 1)
            pool.affine_select(out=tri8[:, 1], in_=tri8[:, 1], compare_op=ALU.is_ge, fill=0.0, base=0,
                               pattern=[[1, N_EXP], [-1, N_EXP]], channel_multiplier=0).then_inc(r_step, 1)
            load_norm(3)

        @block.tensor
        def _(pe):
            def mm3(o, a, b, first, last):
                (a_hi, a_lo), (b_hi, b_lo) = a, b
                pe.matmul(o, a_hi, b_hi, start=first, stop=False, skip_group_check=True)
                pe.matmul(o, a_lo, b_hi, start=False, stop=False, skip_group_check=True)
                return pe.matmul(o, a_hi, b_lo, start=False, stop=last, skip_group_check=True)

            def split_ready(u):
                pe.wait_ge(hi_ready, u + 1)
                pe.wait_ge(lo_ready, u + 1)

            def project(c, u, k2, tokens, xT_ready):
                if u > 0:
                    split_ready(u)
                hi, lo = hi_slot(u, 512), lo_slot(u, 512)
                for o in range(2):
                    b = bank(2 * (c % 2) + o)
                    for kk in range(4):
                        k = 4 * k2 + kk
                        if u == 0 and o == 0 and kk == 0:
                            pe.wait_ge(first_hi_ready, 1)
                            pe.wait_ge(first_lo_ready, 1)
                        if u == 0 and o == 0 and kk == 2:
                            split_ready(u)
                        if xT_ready is not None and o == 0 and kk % 2 == 0:
                            pe.wait_ge(xT_hi_ready, xT_ready + k // 2 + 1)
                            pe.wait_ge(xT_lo_ready, xT_ready + k // 2 + 1)
                        if tokens:
                            m = mm3(b, (xT_hi[:, k, o * P:(o + 1) * P], xT_lo[:, k, o * P:(o + 1) * P]),
                                    (hi[:, kk, :], lo[:, kk, :]), k == 0, k == KC - 1)
                        else:
                            for h in range(2):
                                w = slice((2 * o + h) * P, (2 * o + h + 1) * P)
                                m = mm3(b[:, h * T:(h + 1) * T], (hi[:, kk, w], lo[:, kk, w]),
                                        (xT_hi[:, k, :], xT_lo[:, k, :]), k == 0 and h == 0, k == KC - 1)
                m.then_inc(unit_used, 1)

            def rows(u, chunk, aT, b0, first, last, tiles=range(TT), a_ready=None):
                split_ready(u)
                hi, lo = hi_slot(u, D), lo_slot(u, D)
                for t in tiles:
                    for kk in range(2):
                        k = chunk + kk
                        if a_ready is not None and t == 0:
                            pe.wait_ge(a_ready, k + 1)
                        a = (aT[0][:, k, t * P:(t + 1) * P], aT[1][:, k, t * P:(t + 1) * P])
                        for h in range(2):
                            m = mm3(bank(b0 + 2 * t + h), a,
                                    (hi[:, kk, h * 512:(h + 1) * 512], lo[:, kk, h * 512:(h + 1) * 512]),
                                    first and kk == 0, last and kk == 1)
                    if last and t == 0:
                        m.then_inc(tile0_done, 1)
                    if t == TT - 1:
                        m.then_inc(unit_used, 1)

            def turn_x(n, b0):
                pe.wait_ge(ln_sq_done, TT * (n + 1))
                for t in range(TT):
                    for k in range(KC):
                        if k % 4 == 0:
                            pe.wait_ge(ln_done, 4 * n + 2 * t + k // 4 + 1)
                        m = pe.transpose(bank(b0 + k // 2)[:, (k % 2) * T + t * P:(k % 2) * T + (t + 1) * P],
                                         x_tok[:, t, k * P:(k + 1) * P], ident)
                        if t == TT - 1 and k % 2 == 1:
                            m.then_inc(x_turned, 1)

            def scores(qT, kT, b0, done):
                for h in range(2):
                    q, k = qT[h * HD:(h + 1) * HD], kT[h * HD:(h + 1) * HD]
                    pe.matmul(bank(b0 + h)[:, 0:T], k[:, 0:P], q[:, 0:T], start=True, stop=True,
                              skip_group_check=True)
                    m = pe.matmul(bank(b0 + h)[:, T:T + P], k[:, P:T], q[:, P:T], start=False, stop=True,
                                  skip_group_check=True)
                m.then_inc(done, 1)

            def weighted(b0, v0, v1, wt, done):
                for h in range(2):
                    r = slice(h * HD, (h + 1) * HD)
                    o0, o1 = bank(b0)[r, 384:512], bank(b0 + 1)[r, 384:512]
                    pe.matmul(o0, v0[:, r], wt[:, h, 0:P], start=True, stop=True, skip_group_check=True)
                    pe.matmul(o1, v0[:, r], wt[:, h, P:T], start=True, stop=False, skip_group_check=True)
                    m = pe.matmul(o1, v1[:, r], wt[:, h, T:T + P], start=False, stop=True, skip_group_check=True)
                m.then_inc(done, 1)

            for step, n in PLAN_0:
                if step == "unit":
                    c = n // 2
                    if n % 2 == 0 and c >= 2:
                        pe.wait_ge(in_out, 2 * (c - 1))
                    project(c, U_IN + n, n % 2, IN_ORDER[c] >= 2, 0 if n < 2 else None)
                elif step == "turn":
                    if n == 0:
                        pe.wait_ge(consts_landed, 16)
                    pe.wait_ge(rot_done, 4 * (n + 1))
                    for c in range(4 * n, 4 * n + 4):
                        for t in range(TT):
                            m = pe.transpose(bank(4 + c // 2)[:, (c % 2) * T + t * P:(c % 2) * T + (t + 1) * P],
                                             tokm[:, t, 1 + n, (c % 4) * P:(c % 4 + 1) * P], ident)
                        if c % 2 == 1:
                            m.then_inc(ret_turned, 1)
                elif step == "ret_scores":
                    if n == 0:
                        pe.wait_ge(ret_qkT_ready, 4)
                    else:
                        pe.wait_ge(ret_copied, n)
                    scores(ret_qkT[:, n, :], ret_qkT[:, 4 + n, :], 4, ret_scored)
                elif step == "ret_values":
                    if n == 0:
                        pe.wait_ge(in_out, 2 * 3)
                    pe.wait_ge(ret_masked, n + 1)
                    for h in range(2):
                        c = slice((2 * n + h) * HD, (2 * n + h + 1) * HD)
                        s = ret_s[:, n % 2, h, :]
                        first = n == 0 and h == 0
                        pe.matmul(bank(6)[:, c], s[:, 0:P], tokm[:, 0, 3, c], start=first, stop=True,
                                  skip_group_check=True)
                        pe.matmul(bank(7)[:, c], s[:, P:T], tokm[:, 0, 3, c], start=first, stop=False,
                                  skip_group_check=True)
                        m = pe.matmul(bank(7)[:, c], s[:, T:T + P], tokm[:, 1, 3, c], start=False, stop=True,
                                      skip_group_check=True)
                    m.then_inc(ret_pv, 1)
                elif step == "ret_turn":
                    pe.wait_ge(in_out, 2 * 6)
                    for t in range(TT):
                        pe.wait_ge(ret_out, t + 1)
                        for c in range(4):
                            m = pe.transpose(bank(2 + c // 2)[:, (c % 2) * T + t * P:(c % 2) * T + (t + 1) * P],
                                             ret_o[:, t, c * P:(c + 1) * P], ident)
                            if t == TT - 1 and c % 2 == 1:
                                m.then_inc(ret_o_turned, 1)
                elif step == "sb_scores":
                    if n == 0:
                        pe.wait_ge(in_out, 2 * 5)
                        pe.wait_ge(ret_copied, 4)
                    elif n == 1:
                        pe.wait_ge(gn_step, 4)
                    else:
                        pe.wait_ge(oT_lo_ready, n - 1)
                    scores(sb_qkT[:, n, :], sb_qkT[:, 4 + n, :], 4 + 2 * (n % 2), sb_scored)
                elif step == "sb_sums":
                    pe.wait_ge(sb_l_masked, n + 1)
                    for h in range(2):
                        b, softplus = bank(4 + 2 * (n % 2) + h), sb_l[:, n % 2, h, :]
                        pe.matmul(b[:, 0:T], neg_tri, softplus[:, 0:T], start=False, stop=False,
                                  skip_group_check=True)
                        pe.matmul(b[:, P:T], neg_ones, softplus[:, T:T + P], start=False, stop=False,
                                  skip_group_check=True)
                        m = pe.matmul(b[:, T:T + P], neg_tri, softplus[:, T:T + P], start=False, stop=True,
                                      skip_group_check=True)
                    m.then_inc(sb_summed, 1)
                elif step == "sb_values":
                    if n == 0:
                        pe.wait_ge(in_out, 2 * IN_BLOCKS)
                    pe.wait_ge(sb_w_masked, n + 1)
                    v = slice(n * P, (n + 1) * P)
                    weighted(4 + 2 * (n % 2), tokm[:, 0, 0, v], tokm[:, 1, 0, v], sb_w[:, n % 2], sb_pv)
                elif step == "out":
                    k, t = n // 2, n % 2
                    if k < 2:
                        pe.wait_ge(ret_oT_lo_ready, 2 if k == 0 else k + 1)
                        if n == 0:
                            pe.wait_ge(in_out, 2 * IN_BLOCKS)
                        rows(U_OUT + k, OUT_CHUNKS[k] - 4, (ret_oT_hi, ret_oT_lo), 0, k == 0, False, [t])
                    else:
                        rows(U_OUT + k, OUT_CHUNKS[k], (oT_hi, oT_lo), 0, False, k == OUT_UNITS - 1, [t],
                             oT_lo_ready)
            turn_x(0, 4)

            for b in range(FF_BLOCKS):
                if b >= 2:
                    pe.wait_ge(ff_prod, b - 1)
                for g in range(2):
                    u = U_FF + 2 * b + g
                    split_ready(u)
                    hi, lo = hi_slot(u, 256), lo_slot(u, 256)
                    for h in range(2):
                        for k in range(KC):
                            if b == 0 and g == 0 and h == 0 and k % 2 == 0:
                                pe.wait_ge(xT_hi_ready, 4 + k // 2 + 1)
                                pe.wait_ge(xT_lo_ready, 4 + k // 2 + 1)
                            w = slice(h * P, (h + 1) * P)
                            m = mm3(bank(2 * (b % 2) + g)[:, h * T:(h + 1) * T], (hi[:, k, w], lo[:, k, w]),
                                    (xT_hi[:, k, :], xT_lo[:, k, :]), k == 0 and h == 0, k == KC - 1)
                    m.then_inc(unit_used, 1)
            for k in range(DOWN_UNITS):
                pe.wait_ge(hT_hi_ready, k + 1)
                pe.wait_ge(hT_lo_ready, k + 1)
                rows(U_DOWN + k, 2 * k, (hT_hi, hT_lo), 4, k == 0, k == DOWN_UNITS - 1)
            turn_x(1, 0)

            for step, n in PLAN_1:
                if step == "unit":
                    c = n // 2
                    if n % 2 == 0 and c >= 2:
                        pe.wait_ge(qkv_out, 2 * (c - 1))
                    project(c, U_QKV + n, n % 2, QKV_ORDER[c] >= 4, 8 if n < 2 else None)
                elif step == "scores":
                    if n == 0:
                        pe.wait_ge(ln_done, 8)
                        pe.wait_ge(qkv_out, 2 * 2)
                    elif n == 4:
                        pe.wait_ge(qkv_out, 2 * 5)
                    if n >= 2:
                        pe.wait_ge(c_o_lo_ready, n - 1)
                    for h in range(2):
                        q, k = (c_qkT[h * HD:(h + 1) * HD, m, :] for m in (n, 8 + n))
                        b = bank(4 + 2 * (n % 2) + h)
                        pe.matmul(b[:, 0:P], q[:, 0:P], k[:, 0:P], start=True, stop=True, skip_group_check=True)
                        m = pe.matmul(b[:, P:P + T], q[:, P:T], k[:, 0:T], start=False, stop=True,
                                      skip_group_check=True)
                    m.then_inc(c_scored, 1)
                elif step == "turn":
                    pe.wait_ge(c_normed, 4 * (n + 1))
                    for h in range(2):
                        w = c_p[:, n % 2, h, :]
                        for s in range(3):
                            m = pe.transpose(bank(4 + 2 * (n % 2) + h)[:, s * P:(s + 1) * P],
                                             w[:, s * P:(s + 1) * P], ident)
                    m.then_inc(c_turned, 1)
                elif step == "values":
                    if n == 0 or n == 4:
                        pe.wait_ge(qkv_out, 2 * 3 if n == 0 else 2 * 6)
                    pe.wait_ge(c_pT_ready, n + 1)
                    v = slice(n * P, (n + 1) * P)
                    weighted(4 + 2 * (n % 2), c_v[:, 0, v], c_v[:, 1, v], c_pT[:, n % 2], c_pv)
                elif step == "out":
                    k, t = n // 2, n % 2
                    if n == 0:
                        pe.wait_ge(qkv_out, 2 * QKV_BLOCKS)
                    rows(U_OUT2 + k, 2 * k, (c_oT_hi, c_oT_lo) if k < 2 else (oT_hi, oT_lo), 0, k == 0,
                         k == OUT_UNITS - 1, [t], c_o_lo_ready)
            turn_x(2, 4)

            pe.wait_ge(wr_split, 2)
            for k in range(KC):
                if k % 2 == 0:
                    pe.wait_ge(xT_hi_ready, 12 + k // 2 + 1)
                    pe.wait_ge(xT_lo_ready, 12 + k // 2 + 1)
                m = mm3(bank(0)[:, 0:T], (wr_hi[:, k, :], wr_lo[:, k, :]), (xT_hi[:, k, :], xT_lo[:, k, :]),
                        k == 0, k == KC - 1)
            m.then_inc(logits_done, 1)
            pe.wait_ge(logitsT_out, 1)
            for t in range(TT):
                m = pe.transpose(bank(5)[:, 64 + 8 * t:72 + 8 * t], logitT[:, t * P:(t + 1) * P],
                                 ident[0:N_EXP, 0:N_EXP])
            m.then_inc(logits_turned, 1)
            pe.wait_ge(picked_ready, 1)
            c5 = bank(5)
            pe.wait_ge(ones_ready, 1)
            both = picked[:, :, :].rearrange("p t e -> p (t e)")
            pe.matmul(c5[:, 0:16], before, both, start=True, stop=False, skip_group_check=True)
            pe.matmul(c5[:, 8:16], ones[:, :], picked[:, 0, :], start=False, stop=True, skip_group_check=True)
            m = pe.matmul(c5[:, 16:32], neg_ones, both, start=False, stop=True, skip_group_check=True)
            m.then_inc(slots_done, 1)

            def gather(item):
                pe.wait_ge(pick_ready, item + 2)
                for k in range(KC):
                    for t in range(TT):
                        m = pe.matmul(bank(2 + k // 4)[:, (k % 4) * P:(k % 4 + 1) * P],
                                      x_tok[:, t, k * P:(k + 1) * P], pick[:, t, :],
                                      start=k % 4 == 0 and t == 0, stop=t == TT - 1, skip_group_check=True)
                    if k % 4 == 3:
                        m.then_inc(gathered, 1)

            def scatter(item, n, b):
                t, h = n // 2, n % 2
                pe.matmul(b, place_r[:, t, :], y_hi[:, h * 512:(h + 1) * 512], start=True, stop=False,
                          skip_group_check=True)
                m = pe.matmul(b, place_r[:, t, :], y_lo[:, h * 512:(h + 1) * 512], start=False, stop=True,
                              skip_group_check=True)
                m.then_inc(scattered, 1)

            def run_item(item, first):
                base = item * ITEM_UNITS + U_MOE
                blocks = item * E_BLOCKS

                def unit_ready(j):
                    pe.wait_ge(hi_ready, base + (j + 1))
                    pe.wait_ge(lo_ready, base + (j + 1))

                def first_product(j, b, g):
                    for k2 in range(2):
                        u = j + k2
                        unit_ready(u)
                        hi, lo = hi_slot(U_MOE + u, 512), lo_slot(U_MOE + u, 512)
                        if b == 0 and g == 0:
                            pe.wait_ge(g_lo_ready, item * 2 + (k2 + 1))
                        for kk in range(4):
                            k = 4 * k2 + kk
                            m = mm3(bank(2 * (b % 2) + g), (g_hi[:, k, :], g_lo[:, k, :]),
                                    (hi[:, kk, :], lo[:, kk, :]), k == 0, k == KC - 1)
                        m.then_inc(unit_used, 1)

                def turn(b):
                    pe.wait_ge(m_prod, blocks + (b + 1))
                    if not (first and b == 0):
                        pe.wait_ge(mT_lo_ready, blocks + b)
                    for c in range(4):
                        m = pe.transpose(bank(6)[:, c * P:(c + 1) * P], m_h[:, b % 2, c * P:(c + 1) * P], ident)
                    m.then_inc(m_turned, 1)

                def second_product(j, b, k2):
                    unit_ready(j)
                    hi, lo = hi_slot(U_MOE + j, D), lo_slot(U_MOE + j, D)
                    for kk in range(2):
                        c = 2 * k2 + kk
                        for h in range(2):
                            m = mm3(bank(4 + h), (mT_hi[:, b % 2, c, :], mT_lo[:, b % 2, c, :]),
                                    (hi[:, kk, h * 512:(h + 1) * 512], lo[:, kk, h * 512:(h + 1) * 512]),
                                    b == 0 and c == 0, b == E_BLOCKS - 1 and c == 3)
                    m.then_inc(unit_used, 1)

                j = 0
                for b in range(E_BLOCKS):
                    if b < 2:
                        if not first:
                            pe.wait_ge(m_prod, blocks)
                    else:
                        pe.wait_ge(m_prod, blocks + (b - 1))
                    first_product(j, b, 0)
                    if b >= 1:
                        turn(b - 1)
                    if 1 <= b <= 4 and not first:
                        if b == 1:
                            pe.wait_ge(y_lo_ready, item * 2)
                        pe.wait_ge(y_added, item * 4 + (b - 4))
                        scatter(item, b - 1, bank(7))
                    if b == 5:
                        if not first:
                            pe.wait_ge(y_added, item * 4 + 1)
                        for t in range(TT):
                            m = pe.transpose(bank(7)[:, t * P:(t + 1) * P], pick[:, t, :], ident)
                        m.then_inc(place_turned, 1)
                    first_product(j + 2, b, 1)
                    j += 4
                    if b >= 1:
                        pe.wait_ge(mT_lo_ready, blocks + b)
                        if b == 1 and not first:
                            pe.wait_ge(y_lo_ready, item * 2)
                        second_product(j, b - 1, 0)
                        if b == E_BLOCKS - 1:
                            turn(b)
                        second_product(j + 1, b - 1, 1)
                        j += 2
                pe.wait_ge(mT_lo_ready, blocks + E_BLOCKS)
                second_product(j, E_BLOCKS - 1, 0)
                if first:
                    gather(item)
                else:
                    with pe.If(n_second > item - (N_EXP - 1)):
                        gather(item)
                second_product(j + 1, E_BLOCKS - 1, 1)

            gather(-1)
            run_item(0, True)
            pe.wait_ge(routed, 1)
            n_second = pe.value_load(second[0:1, 0:1], min_val=0, max_val=MAX_SECOND)
            with pe.Fori(1, N_EXP) as item:
                run_item(item, False)
            with pe.Fori(N_EXP, N_ITEMS) as item:
                with pe.If(n_second > item - N_EXP):
                    run_item(item, False)
            for n in range(4):
                if n < 2:
                    pe.wait_ge(y_lo_ready, n_second * 2 + (2 * N_EXP - 1 + n))
                scatter(None, n, bank(n))

        @block.scalar
        def _(act):
            def round_unit(u):
                act.wait_ge(raw_landed[u % RAW], 16 * (u // RAW + 1))
                if u >= SPLIT:
                    act.wait_ge(unit_used, u - SPLIT + 1)
                act.activation(w_hi[:, u % SPLIT, :], raw[:, u % RAW, :], ACT.Copy).then_inc(hi_ready, 1)

            def copy(o, i, s, scale=1.0):
                act.activation(o, i, ACT.Copy, scale=scale).then_inc(s, 1)

            for h in range(2):
                act.wait_ge(xT_landed[h], 16)
                for j in (2 * h, 2 * h + 1):
                    copy(xT_hi[:, 2 * j:2 * j + 2, :], xT_raw[:, 2 * j:2 * j + 2, :], xT_hi_ready)
                act.wait_ge(first_landed if h == 0 else raw_landed[0], 16)
                c = slice(h * (UC // 2), (h + 1) * (UC // 2))
                copy(w_hi[:, 0, c], raw[:, 0, c], first_hi_ready if h == 0 else hi_ready)
            for u in range(1, SPLIT):
                round_unit(u)

            for step, n in PLAN_0:
                if step == "unit":
                    if n % 2 == 1:
                        c = n // 2
                        act.wait_ge(unit_used, U_IN + n + 1)
                        for o in range(2):
                            b = bank(2 * (c % 2) + o)
                            i = IN_ORDER[c]
                            if i < 2:
                                dst = sb_qkT[:, 4 * i + 2 * o:4 * i + 2 * o + 2, :].rearrange("p a t -> p (a t)")
                                copy(dst, b, in_out, HD ** -0.5 if i == 0 else 1.0)
                            elif i < 6:
                                copy(tokm[:, o, i - 2, :], b, in_out)
                            else:
                                act.activation(tokm[:, o, 4, :], b, ACT.Silu).then_inc(in_out, 1)
                elif step == "round":
                    round_unit(U_IN + n)
                elif step == "turn":
                    for j in (2 * n, 2 * n + 1):
                        act.wait_ge(ret_turned, j + 1)
                        copy(ret_qkT[:, 2 * j:2 * j + 2, :].rearrange("p a t -> p (a t)"), bank(4 + j),
                             ret_qkT_ready)
                elif step == "ret_centre":
                    for t in range(TT):
                        act.wait_ge(gn_step, 2 * t + 2)
                        act.activation(ret_sq[:, t, :], ret_o[:, t, :], ACT.Square).then_inc(gn_sq, 1)
                    for t in range(TT):
                        act.wait_ge(gn_step, 4 + t + 1)
                        act.activation(gn_s[:, 2, t, :], gn_s[:, 1, t, :], ACT.Sqrt, scale=1.0 / HD,
                                       bias=eps_col).then_inc(gn_std, 1)
                elif step == "ret_turn":
                    for j in range(2):
                        act.wait_ge(ret_o_turned, j + 1)
                        copy(ret_oT_hi[:, 2 * j:2 * j + 2, :].rearrange("p a t -> p (a t)"), bank(2 + j),
                             ret_oT_hi_ready)
                elif step == "sb_scores":
                    if n < 2:
                        act.preload_act_table_set("natural_log_exp_and_others")
                    e = sb_e[:, n % 2]
                    b0 = 4 + 2 * (n % 2)
                    act.wait_ge(sb_scored, n + 1)
                    act.activation(e, ps[:, b0:b0 + 2, 0:384], ACT.Abs).then_inc(sb_abs, 1)
                    act.wait_ge(sb_abs, n + 1)
                    act.activation(e, e, ACT.Exp, scale=-1.0).then_inc(sb_exp, 1)
                    act.wait_ge(sb_exp, n + 1)
                    act.activation(e, e, ACT.Ln, bias=1.0).then_inc(sb_log, 1)
                elif step == "sb_sums":
                    b0 = 4 + 2 * (n % 2)
                    act.wait_ge(sb_summed, n + 1)
                    if n >= 2:
                        act.wait_ge(sb_pv, n - 1)
                    act.activation(sb_w[:, n % 2], ps[:, b0:b0 + 2, 0:384], ACT.Exp).then_inc(sb_weights, 1)
                elif step == "sb_values":
                    b0 = 4 + 2 * (n % 2)
                    act.wait_ge(sb_pv, n + 1)
                    copy(by_tile(oT_hi[:, n, :]), ps[:, b0:b0 + 2, 384:512], oT_hi_ready)

            def norm(n, v, b0):
                act.activation(spare, eps_col, ACT.Sqrt)
                for t in range(TT):
                    act.wait_ge(ln_mean, TT * n + t + 1)
                    act.activation(ps[:, b0 + 2 * t:b0 + 2 * t + 2, :], two(v[:, t, :]), ACT.Square,
                                   bias=neg_mean[:, t:t + 1], accum_out=squares[:, t:t + 1]).then_inc(ln_sq_done, 1)
                    act.wait_ge(ln_sq_done, TT * n + t + 1)
                    act.activation(std[:, t:t + 1], squares[:, t:t + 1], ACT.Sqrt, scale=1.0 / D,
                                   bias=eps_col).then_inc(ln_std, 1)

            def split_xT(n, b0):
                for j in range(4):
                    act.wait_ge(x_turned, 4 * n + j + 1)
                    copy(xT_hi[:, 2 * j:2 * j + 2, :].rearrange("p a t -> p (a t)"), bank(b0 + j), xT_hi_ready)

            act.wait_ge(eps_ready, 1)
            norm(0, x_tok, 4)
            split_xT(0, 4)
            round_unit(U_FF - 1 + SPLIT)

            def ff_hi(b):
                act.wait_ge(ff_prod, b + 1)
                copy(hT_hi[:, 2 * b:2 * b + 2, :].rearrange("p a t -> p (a t)"), ff_h[:, b % 2, :], hT_hi_ready)

            for b in range(FF_BLOCKS):
                act.wait_ge(unit_used, U_FF + 2 * b + 1)
                if b >= 2:
                    act.wait_ge(ff_prod, b - 1)
                act.activation(ff_g[:, b % 2, :], bank(2 * (b % 2)), ACT.Silu).then_inc(ff_silu, 1)
                round_unit(U_FF + 2 * b + SPLIT)
                if b >= 1:
                    ff_hi(b - 1)
                round_unit(U_FF + 2 * b + 1 + SPLIT)
            ff_hi(FF_BLOCKS - 1)
            for k in range(DOWN_UNITS - 1):
                round_unit(U_DOWN + k + SPLIT)
            norm(1, x_tok, 0)
            split_xT(1, 0)
            round_unit(U_QKV - 1 + SPLIT)

            for step, n in PLAN_1:
                b0 = 4 + 2 * (n % 2)
                if step == "unit" and n % 2 == 1:
                    c = n // 2
                    act.wait_ge(unit_used, U_QKV + n + 1)
                    for o in range(2):
                        b = bank(2 * (c % 2) + o)
                        i = QKV_ORDER[c]
                        if i < 4:
                            copy(c_qkT[:, 4 * i + 2 * o:4 * i + 2 * o + 2, :].rearrange("p a t -> p (a t)"), b,
                                 qkv_out)
                        else:
                            copy(c_v[:, o, (i - 4) * 512:(i - 3) * 512], b, qkv_out)
                elif step == "round":
                    round_unit(U_QKV + n)
                elif step == "weights":
                    act.wait_ge(c_maxed, 2 * (n + 1))
                    if n >= 2:
                        act.wait_ge(c_turned, n - 1)
                    for h in range(2):
                        for t, s in ((0, slice(0, P)), (1, slice(P, P + T))):
                            act.activation(c_p[:, n % 2, h, s], c_s[:, n % 2, h, s], ACT.Exp,
                                           bias=c_max[:, n, h, t:t + 1], accum_out=c_sum[:, n, h, t:t + 1]
                                           ).then_inc(c_exped, 1)
                elif step == "turn":
                    act.wait_ge(c_turned, n + 1)
                    if n >= 2:
                        act.wait_ge(c_pv, n - 1)
                    copy(c_pT[:, n % 2], ps[:, b0:b0 + 2, 0:384], c_pT_ready)
                elif step == "values":
                    act.wait_ge(c_pv, n + 1)
                    copy(by_tile(c_out(n, True)), ps[:, b0:b0 + 2, 384:512], c_o_hi_ready)
            norm(2, x_tok, 4)
            act.wait_ge(aux_landed[5], 16)
            act.wait_ge(wr_zeroed, 2)
            copy(wr_hi[:, :, 0:N_EXP], wr[:, :, :], wr_split)
            split_xT(2, 4)
            round_unit(U_MOE - 1 + SPLIT)
            act.wait_ge(logits_done, 1)
            copy(logitT[:, :], bank(0)[0:N_EXP, 0:T], logitsT_out)
            act.wait_ge(r_step, 4 + 3)
            for t in range(TT):
                act.activation(ex[:, t, :], logit[:, t, :], ACT.Exp, bias=top[:, 0, t:t + 1]).then_inc(r_exp, 1)

            def item_round(item, j):
                u = U_MOE + j
                act.wait_ge(raw_landed[u % RAW], landed(item, j))
                act.wait_ge(unit_used, item * ITEM_UNITS + (u - SPLIT + 1))
                act.activation(w_hi[:, u % SPLIT, :], raw[:, u % RAW, :], ACT.Copy).then_inc(hi_ready, 1)

            def hidden_hi(item, b):
                act.wait_ge(m_turned, item * E_BLOCKS + (b + 1))
                copy(mT_hi[:, b % 2].rearrange("p a t -> p (a t)"), bank(6), mT_hi_ready)

            def tokens_hi(item):
                for h in range(2):
                    act.wait_ge(gathered, item * 2 + (h + 3))
                    copy(g_hi[:, 4 * h:4 * h + 4, :].rearrange("p a t -> p (a t)"), bank(2 + h), g_hi_ready)

            def output_hi(item):
                act.wait_ge(unit_used, item * ITEM_UNITS + (U_MOE + ITEM_UNITS))
                for h in range(2):
                    copy(y_hi[:, h * 512:(h + 1) * 512], bank(4 + h), y_hi_ready)

            def next_item(item):
                item_round(item + 1, 0)
                tokens_hi(item)
                for n in range(1, SPLIT):
                    item_round(item + 1, n)

            def run_item(item, first):
                blocks = item * E_BLOCKS
                base = item * ITEM_UNITS + U_MOE
                j = 0
                for b in range(E_BLOCKS):
                    item_round(item, j + SPLIT)
                    if b == 0 and not first:
                        output_hi(item - 1)
                    item_round(item, j + 1 + SPLIT)
                    act.wait_ge(unit_used, base + (j + 2))
                    if b == 0 and not first:
                        act.wait_ge(m_prod, blocks - 1)
                    elif b >= 2:
                        act.wait_ge(m_prod, blocks + (b - 1))
                    act.activation(m_g[:, b % 2, :], bank(2 * (b % 2)), ACT.Silu).then_inc(m_silu, 1)
                    if b >= 1:
                        hidden_hi(item, b - 1)
                    if b == 5:
                        act.wait_ge(place_turned, item + 1)
                        copy(place_r[:, :, :].rearrange("p a t -> p (a t)"), bank(7)[:, 0:T], place_ready)
                    item_round(item, j + 2 + SPLIT)
                    item_round(item, j + 3 + SPLIT)
                    j += 4
                    if b == E_BLOCKS - 1:
                        hidden_hi(item, b)
                    if b >= 1:
                        item_round(item, j + SPLIT)
                        if b < E_BLOCKS - 1:
                            item_round(item, j + 1 + SPLIT)
                        j += 2
                if first:
                    next_item(item)
                else:
                    with act.If(n_second > item - (N_EXP - 1)):
                        next_item(item)

            tokens_hi(-1)
            run_item(0, True)
            act.wait_ge(routed, 1)
            n_second = act.value_load(second[0:1, 0:1], min_val=0, max_val=MAX_SECOND)
            with act.Fori(1, N_EXP) as item:
                run_item(item, False)
            with act.Fori(N_EXP, N_ITEMS) as item:
                with act.If(n_second > item - N_EXP):
                    run_item(item, False)
            output_hi(n_second + (N_EXP - 1))
            norm(3, y_sum, 0)

        @block.vector
        def _(dve):
            def rest_unit(u):
                dve.wait_ge(hi_ready, u + 1)
                dve.tensor_tensor(w_lo[:, u % SPLIT, :], raw[:, u % RAW, :], w_hi[:, u % SPLIT, :].bitcast(F32),
                                  ALU.subtract).then_inc(lo_ready, 1)

            def rest(o, i, hi, s):
                dve.tensor_tensor(o, i, hi.bitcast(F32), ALU.subtract).then_inc(s, 1)

            for h in range(2):
                for j in (2 * h, 2 * h + 1):
                    dve.wait_ge(xT_hi_ready, j + 1)
                    c = slice(2 * j, 2 * j + 2)
                    rest(xT_lo[:, c, :], xT_raw[:, c, :], xT_hi[:, c, :], xT_lo_ready)
                dve.wait_ge(first_hi_ready if h == 0 else hi_ready, 1)
                c = slice(h * (UC // 2), (h + 1) * (UC // 2))
                rest(w_lo[:, 0, c], raw[:, 0, c], w_hi[:, 0, c], first_lo_ready if h == 0 else lo_ready)
            for u in range(1, SPLIT):
                rest_unit(u)

            def heads(v):
                return v.rearrange("p (h d) -> p h d", d=HD)

            def per_head(v):
                return v.unsqueeze(2).broadcast_to((P, N_RET, HD))

            def rotate(qk):
                for t in range(TT):
                    n = 2 * qk + t
                    dve.wait_ge(in_out, n + 1)
                    if n == 0:
                        dve.wait_ge(aux_landed[1], 16)
                    else:
                        dve.wait_ge(rot_done, 2 * n)
                    v = tokm[:, t, 1 + qk, :].rearrange("p (h a f) -> p h a f", h=N_RET, a=2)
                    x1, x2 = v[:, :, 0, :], v[:, :, 1, :]
                    c = rot[:, t, 2 * qk, :].rearrange("p (h f) -> p h f", h=N_RET)
                    s = rot[:, t, 2 * qk + 1, :].rearrange("p (h f) -> p h f", h=N_RET)
                    w = [rot_t[:, m, :].rearrange("p (h f) -> p h f", h=N_RET) for m in range(4)]
                    dve.tensor_tensor(w[0], x1, c, ALU.mult).then_inc(rot_step, 1)
                    dve.tensor_tensor(w[1], x2, s, ALU.mult).then_inc(rot_step, 1)
                    dve.tensor_tensor(w[2], x1, s, ALU.mult).then_inc(rot_step, 1)
                    dve.tensor_tensor(w[3], x2, c, ALU.mult).then_inc(rot_step, 1)
                    dve.wait_ge(rot_step, 4 * (n + 1))
                    dve.tensor_tensor(x1, w[0], w[1], ALU.subtract).then_inc(rot_done, 1)
                    dve.tensor_tensor(x2, w[2], w[3], ALU.add).then_inc(rot_done, 1)

            def ret_centre():
                dve.wait_ge(ret_pv, 4)
                for t in range(TT):
                    dve.tensor_reduce(gn_s[:, 0, t, :], heads(bank(6 + t)), AX, ALU.add).then_inc(gn_step, 1)
                    dve.wait_ge(gn_step, 2 * t + 1)
                    dve.scalar_tensor_tensor(out=heads(ret_o[:, t, :]), in0=per_head(gn_s[:, 0, t, :]),
                                             scalar=-1.0 / HD, in1=heads(bank(6 + t)), op0=ALU.mult,
                                             op1=ALU.add).then_inc(gn_step, 1)
                for t in range(TT):
                    dve.wait_ge(gn_sq, t + 1)
                    dve.tensor_reduce(gn_s[:, 1, t, :], heads(ret_sq[:, t, :]), AX, ALU.add).then_inc(gn_step, 1)

            def ret_scale(t):
                dve.wait_ge(aux_landed[3], 16)
                n = 4 + TT + 3 * t
                dve.wait_ge(gn_std, t + 1)
                dve.reciprocal(gn_s[:, 0, t, :], gn_s[:, 2, t, :]).then_inc(gn_step, 1)
                dve.wait_ge(gn_step, n + 1)
                dve.tensor_tensor(heads(ret_o[:, t, :]), heads(ret_o[:, t, :]), per_head(gn_s[:, 0, t, :]),
                                  ALU.mult).then_inc(gn_step, 1)
                dve.wait_ge(gn_step, n + 2)
                dve.tensor_tensor(ret_o[:, t, :], ret_o[:, t, :], gn_row, ALU.mult).then_inc(gn_step, 1)

            def ret_gate():
                for t in range(TT):
                    dve.wait_ge(gn_step, 4 + TT + 3 * (t + 1))
                    dve.wait_ge(in_out, 2 * 5 + t + 1)
                    dve.tensor_tensor(ret_o[:, t, :], ret_o[:, t, :], tokm[:, t, 4, :], ALU.mult).then_inc(ret_out, 1)

            for step, n in PLAN_0:
                if step == "rest":
                    rest_unit(U_IN + n)
                elif step == "rotate":
                    rotate(n)
                elif step == "ret_scores":
                    dve.wait_ge(ret_scored, n + 1)
                    if n >= 2:
                        dve.wait_ge(ret_pv, n - 1)
                    dve.tensor_copy(ret_s[:, n % 2], ps[:, 4:6, 0:384]).then_inc(ret_copied, 1)
                elif step == "ret_centre":
                    ret_centre()
                elif step == "ret_scale":
                    ret_scale(n)
                elif step == "ret_gate":
                    ret_gate()
                elif step == "ret_turn":
                    for j in range(2):
                        dve.wait_ge(ret_oT_hi_ready, j + 1)
                        c = slice(2 * j, 2 * j + 2)
                        rest(ret_oT_lo[:, c, :].rearrange("p a t -> p (a t)"), bank(2 + j),
                             ret_oT_hi[:, c, :].rearrange("p a t -> p (a t)"), ret_oT_lo_ready)
                elif step == "sb_scores":
                    b0 = 4 + 2 * (n % 2)
                    dve.wait_ge(sb_log, n + 1)
                    if n >= 2:
                        dve.wait_ge(sb_summed, n - 1)
                    dve.scalar_tensor_tensor(out=sb_l[:, n % 2], in0=ps[:, b0:b0 + 2, 0:384], scalar=0.0,
                                             in1=sb_e[:, n % 2], op0=ALU.max, op1=ALU.add).then_inc(sb_softplus, 1)
                elif step == "sb_values":
                    b0 = 4 + 2 * (n % 2)
                    dve.wait_ge(oT_hi_ready, n + 1)
                    rest(by_tile(oT_lo[:, n, :]), ps[:, b0:b0 + 2, 384:512], by_tile(oT_hi[:, n, :]), oT_lo_ready)

            def norm(n, v, b0):
                def centre(t):
                    dve.wait_ge(ln_mean, TT * n + t + 1)
                    dve.scalar_tensor_tensor(out=ps[:, b0 + 2 * t:b0 + 2 * t + 2, :], in0=two(v[:, t, :]),
                                             scalar=neg_mean[:, t:t + 1], in1=two(norm_gb[:, 0, :]),
                                             op0=ALU.add, op1=ALU.mult).then_inc(ln_centred, 1)

                def scale(t):
                    dve.wait_ge(ln_std, TT * n + t + 1)
                    dve.reciprocal(rstd[:, t:t + 1], std[:, t:t + 1]).then_inc(ln_rstd, 1)
                    dve.wait_ge(ln_rstd, TT * n + t + 1)
                    dve.wait_ge(ln_centred, TT * n + t + 1)
                    for h in range(2):
                        c = slice(h * 512, (h + 1) * 512)
                        dve.scalar_tensor_tensor(out=v[:, t, c], in0=bank(b0 + 2 * t + h), scalar=rstd[:, t:t + 1],
                                                 in1=norm_gb[:, 1, c], op0=ALU.mult, op1=ALU.add
                                                 ).then_inc(ln_done, 1)

                for t in range(TT):
                    if n < 3:
                        if t == 0:
                            dve.wait_ge(tile0_done, n + 1)
                        else:
                            dve.wait_ge(unit_used, (U_FF, U_QKV, U_MOE)[n])
                        for h in range(2):
                            r = v[:, t, h * 512:(h + 1) * 512]
                            if n == 0 and t == 0 and h == 0:
                                dve.wait_ge(aux_landed[0], 16)
                            dve.scalar_tensor_tensor(out=r, in0=r, scalar=ALPHA, in1=bank(b0 + 2 * t + h),
                                                     op0=ALU.mult, op1=ALU.add,
                                                     accum_out=sums[:, t, h:h + 1]).then_inc(ln_res, 1)
                        dve.wait_ge(ln_res, 4 * n + 2 * (t + 1))
                    else:
                        for h in range(2):
                            add_output(n_second + (N_EXP - 1), 2 * t + h, bank(2 * t + h))
                        dve.wait_ge(y_added, n_second * 4 + ((N_EXP - 1) * 4 + 1 + 2 * (t + 1)))
                    dve.tensor_scalar(neg_mean[:, t:t + 1], sums[:, t, 0:1], sums[:, t, 1:2], -1.0 / D, ALU.add,
                                      ALU.mult).then_inc(ln_mean, 1)
                    if t == 0:
                        dve.wait_ge(aux_landed[2], 32 * (n + 1))
                        centre(0)
                scale(0)
                centre(1)
                scale(1)

            def split_xT(n, b0):
                for j in range(4):
                    dve.wait_ge(xT_hi_ready, 4 * (n + 1) + j + 1)
                    c = slice(2 * j, 2 * j + 2)
                    rest(xT_lo[:, c, :].rearrange("p a t -> p (a t)"), bank(b0 + j),
                         xT_hi[:, c, :].rearrange("p a t -> p (a t)"), xT_lo_ready)

            norm(0, x_tok, 0)
            split_xT(0, 4)
            rest_unit(U_FF - 2 + SPLIT)
            rest_unit(U_FF - 1 + SPLIT)

            def ff_lo(b):
                dve.wait_ge(hT_hi_ready, b + 1)
                c = slice(2 * b, 2 * b + 2)
                rest(hT_lo[:, c, :].rearrange("p a t -> p (a t)"), ff_h[:, b % 2, :],
                     hT_hi[:, c, :].rearrange("p a t -> p (a t)"), hT_lo_ready)

            for b in range(FF_BLOCKS):
                rest_unit(U_FF + 2 * b + SPLIT)
                if b >= 1:
                    ff_lo(b - 1)
                dve.wait_ge(ff_silu, b + 1)
                dve.wait_ge(unit_used, U_FF + 2 * b + 2)
                dve.tensor_tensor(ff_h[:, b % 2, :], ff_g[:, b % 2, :], bank(2 * (b % 2) + 1),
                                  ALU.mult).then_inc(ff_prod, 1)
                rest_unit(U_FF + 2 * b + 1 + SPLIT)
            ff_lo(FF_BLOCKS - 1)
            for k in range(DOWN_UNITS - 2):
                rest_unit(U_DOWN + k + SPLIT)
            norm(1, x_tok, 4)
            split_xT(1, 0)
            rest_unit(U_QKV - 2 + SPLIT)
            rest_unit(U_QKV - 1 + SPLIT)
            dve.wait_ge(aux_landed[4], 16)
            for step, n in PLAN_1:
                b0 = 4 + 2 * (n % 2)
                if step == "rest":
                    rest_unit(U_QKV + n)
                elif step == "scores":
                    dve.wait_ge(c_scored, n + 1)
                    if n >= 2:
                        dve.wait_ge(c_exped, 4 * (n - 1))
                    bias = c_bias[:, 2 * n:2 * n + 2, :]
                    dve.scalar_tensor_tensor(out=c_s[:, n % 2, :, 0:P], in0=ps[:, b0:b0 + 2, 0:P],
                                             scalar=HD ** -0.5, in1=bias[:, :, P:T], op0=ALU.mult,
                                             op1=ALU.add).then_inc(c_biased, 1)
                    dve.scalar_tensor_tensor(out=c_s[:, n % 2, :, P:P + T], in0=ps[:, b0:b0 + 2, P:P + T],
                                             scalar=HD ** -0.5, in1=bias, op0=ALU.mult,
                                             op1=ALU.add).then_inc(c_biased, 1)
                    dve.wait_ge(c_masked, 2 * (n + 1))
                    dve.tensor_reduce(c_max[:, n, :, 0], c_s[:, n % 2, :, 0:P], AX, ALU.max,
                                      negate=True).then_inc(c_maxed, 1)
                    dve.tensor_reduce(c_max[:, n, :, 1], c_s[:, n % 2, :, P:P + T], AX, ALU.max,
                                      negate=True).then_inc(c_maxed, 1)
                elif step == "weights":
                    dve.wait_ge(c_exped, 4 * (n + 1))
                    dve.reciprocal(c_inv[:, n], c_sum[:, n]).then_inc(c_recip, 1)
                    dve.wait_ge(c_recip, n + 1)
                    for h in range(2):
                        for t, s in ((0, slice(0, P)), (1, slice(P, P + T))):
                            dve.tensor_scalar(c_p[:, n % 2, h, s], c_p[:, n % 2, h, s], c_inv[:, n, h, t:t + 1],
                                              None, ALU.mult).then_inc(c_normed, 1)
                elif step == "values":
                    dve.wait_ge(c_o_hi_ready, n + 1)
                    rest(by_tile(c_out(n, False)), ps[:, b0:b0 + 2, 384:512], by_tile(c_out(n, True)),
                         c_o_lo_ready)
            norm(2, x_tok, 0)

            dve.wait_ge(wr_split, 1)
            rest(wr_lo[:, :, 0:N_EXP], wr[:, :, :], wr_hi[:, :, 0:N_EXP], wr_split)
            split_xT(2, 4)
            rest_unit(U_MOE - 2 + SPLIT)
            done = [4]

            def step(i, wait=True):
                i.then_inc(r_step, 1)
                done[0] += 1
                if wait:
                    dve.wait_ge(r_step, done[0])

            dve.wait_ge(logits_turned, 1)
            dve.wait_ge(aux_landed[6], 16)
            dve.wait_ge(r_step, 4)
            step(dve.tensor_tensor(logit[:, :, :], bank(5)[:, 64:64 + TT * N_EXP].rearrange("p (t e) -> p t e", t=TT),
                                   br[:, :].unsqueeze(1).broadcast_to((P, TT, N_EXP)), ALU.add))
            step(dve.tensor_reduce(top[:, 0, :], logit[:, :, :], AX, ALU.max, negate=True), False)
            every = (P, TT, N_EXP, N_EXP)
            other = logit[:, :, :].unsqueeze(2).broadcast_to(every)
            own = logit[:, :, :].unsqueeze(3).broadcast_to(every)
            step(dve.tensor_tensor(gt[:, :, :, :], other, own, ALU.is_gt), False)
            step(dve.tensor_tensor(eq[:, :, :, :], other, own, ALU.is_equal))
            step(dve.tensor_tensor(eq[:, :, :, :], eq[:, :, :, :], tri8[:, 0:1].broadcast_to(every), ALU.mult))
            step(dve.tensor_tensor(gt[:, :, :, :], gt[:, :, :, :], eq[:, :, :, :], ALU.add))
            step(dve.tensor_reduce(rank[:, :, :], gt[:, :, :, :], AX, ALU.add))
            dve.tensor_scalar(picked[:, :, :], rank[:, :, :], 2.0, None, ALU.is_lt).then_inc(picked_ready, 1)
            dve.wait_ge(picked_ready, 1)
            dve.wait_ge(slots_done, 1)
            c5 = bank(5)
            step(dve.scalar_tensor_tensor(out=rank[:, :, :].rearrange("p t e -> p (t e)"), in0=c5[:, 0:16], scalar=1.0,
                                          in1=picked[:, :, :].rearrange("p t e -> p (t e)"), op0=ALU.add,
                                          op1=ALU.mult))
            step(dve.tensor_scalar(route[:, 0:N_EXP, 0, :], rank[:, :, :].rearrange("p t e -> p e t"), -1.0, None,
                                   ALU.add))

            def weigh():
                step(dve.tensor_copy(over[:, 0, :], c5[:, 16:24]), False)
                step(dve.tensor_copy(over[:, 1, :], c5[:, 24:32]))
                dve.wait_ge(r_exp, 2)
                step(dve.tensor_tensor(ex[:, :, :], ex[:, :, :], picked[:, :, :], ALU.mult))
                step(dve.tensor_reduce(top[:, 2, :], ex[:, :, :], AX, ALU.add))
                step(dve.reciprocal(top[:, 3, :], top[:, 2, :]))
                for t in range(TT):
                    step(dve.tensor_scalar(route[:, 0:N_EXP, 1, t], ex[:, t, :], top[:, 3, t:t + 1], None, ALU.mult))

            def over_128():
                step(dve.tensor_tensor(over[:, 1, :], over[:, 0, :], over[:, 1, :], ALU.add))
                step(dve.tensor_scalar(over[:, 2, :], over[:, 1, :], -float(P), None, ALU.is_lt))
                step(dve.tensor_tensor(gt[:, 0], over[:, 2, :].unsqueeze(1).broadcast_to((P, N_EXP, N_EXP)),
                                       tri8[:, 1], ALU.mult))
                step(dve.tensor_reduce(over[:, 3, :], gt[:, 0], AX, ALU.add))
                step(dve.tensor_reduce(second_f[:, 0:1], over[:, 2, :], AX, ALU.add))
                step(dve.memset(route[:, N_ITEMS, :, :], -1.0))

            def second_item(s):
                step(dve.scalar_tensor_tensor(out=over[:, 0, :], in0=over[:, 3, :], scalar=float(s + 1),
                                              in1=over[:, 2, :], op0=ALU.is_equal, op1=ALU.mult))
                step(dve.tensor_tensor(over[:, 4, :], over[:, 0, :], num8[:, :], ALU.mult))
                step(dve.tensor_reduce(second_f[:, s + 1:s + 2], over[:, 4, :], AX, ALU.add))
                v = gt[:, 0].rearrange("p a b -> p (a b)")[:, 0:4 * N_EXP].rearrange("p (n e) -> p n e", n=4)
                step(dve.tensor_tensor(v, route[:, 0:N_EXP].rearrange("p e a t -> p (a t) e"),
                                       over[:, 0, :].unsqueeze(1).broadcast_to((P, 4, N_EXP)), ALU.mult))
                r = route[:, N_EXP + s]
                step(dve.tensor_reduce(r.rearrange("p a t -> p (a t)"), v, AX, ALU.add))
                step(dve.tensor_scalar(r[:, 0, :], r[:, 0, :], -float(P), None, ALU.add))

            def item_rest(item, j):
                u = U_MOE + j
                dve.wait_ge(hi_ready, item * ITEM_UNITS + (u + 1))
                dve.tensor_tensor(w_lo[:, u % SPLIT, :], raw[:, u % RAW, :], w_hi[:, u % SPLIT, :].bitcast(F32),
                                  ALU.subtract).then_inc(lo_ready, 1)

            def pick_tokens(item):
                dve.tensor_copy(cur[:, :], route[:, bass.ds(item + 1, 1), 0, :].rearrange("p a t -> p (a t)")
                                ).then_inc(cur_ready, 1)
                dve.wait_ge(cur_ready, item + 2)
                for t in range(TT):
                    m = dve.tensor_scalar(pick[:, t, :], slots, cur[:, t:t + 1], None, ALU.is_equal)
                m.then_inc(pick_ready, 1)

            def tokens_lo(item):
                for h in range(2):
                    dve.wait_ge(g_hi_ready, item * 2 + (h + 3))
                    rest(g_lo[:, 4 * h:4 * h + 4, :].rearrange("p a t -> p (a t)"), bank(2 + h),
                         g_hi[:, 4 * h:4 * h + 4, :].rearrange("p a t -> p (a t)"), g_lo_ready)

            def output_lo(item):
                for h in range(2):
                    dve.wait_ge(y_hi_ready, item * 2 + (h + 1))
                    c = slice(h * 512, (h + 1) * 512)
                    rest(y_lo[:, c], bank(4 + h), y_hi[:, c], y_lo_ready)

            def hidden_lo(item, b):
                dve.wait_ge(mT_hi_ready, item * E_BLOCKS + (b + 1))
                rest(mT_lo[:, b % 2].rearrange("p a t -> p (a t)"), bank(6),
                     mT_hi[:, b % 2].rearrange("p a t -> p (a t)"), mT_lo_ready)

            def add_output(item, n, b):
                t, h = n // 2, n % 2
                dve.wait_ge(scattered, item * 4 + (n + 1))
                v = y_sum[:, t, h * 512:(h + 1) * 512]
                dve.scalar_tensor_tensor(out=v, in0=b, scalar=weight[:, t:t + 1], in1=v, op0=ALU.mult,
                                         op1=ALU.add, accum_out=sums[:, t, h:h + 1]).then_inc(y_added, 1)

            def next_item(item):
                item_rest(item + 1, 0)
                tokens_lo(item)
                for n in range(1, SPLIT):
                    item_rest(item + 1, n)

            def run_item(item, first):
                blocks = item * E_BLOCKS
                base = item * ITEM_UNITS + U_MOE
                j = 0
                for b in range(E_BLOCKS):
                    item_rest(item, j + SPLIT)
                    if b == 0 and not first:
                        output_lo(item - 1)
                    item_rest(item, j + 1 + SPLIT)
                    if b >= 1:
                        hidden_lo(item, b - 1)
                    if 1 <= b <= 4 and not first:
                        add_output(item - 1, b - 1, bank(7))
                    if first and b == 1:
                        over_128()
                    if first and b == E_BLOCKS - 1:
                        dve.tensor_scalar(y_sum[:, :, :], x_tok[:, :, :], ALPHA, None, ALU.mult).then_inc(y_added, 1)
                    if first and 2 <= b <= MAX_SECOND + 1:
                        second_item(b - 2)
                    if first and b == MAX_SECOND + 2:
                        dve.tensor_copy(second[:, :], second_f[:, :]).then_inc(routed, 1)
                    if b == 5:
                        if not first:
                            dve.wait_ge(y_added, item * 4 + 1)
                        dve.tensor_copy(weight[:, :], route[:, bass.ds(item, 1), 1, :].rearrange("p a t -> p (a t)")
                                        ).then_inc(weight_ready, 1)
                        dve.wait_ge(weight_ready, item + 1)
                        dve.wait_ge(place_turned, item + 1)
                        pick_tokens(item)
                    item_rest(item, j + 2 + SPLIT)
                    dve.wait_ge(m_silu, blocks + (b + 1))
                    dve.wait_ge(unit_used, base + (j + 4))
                    dve.tensor_tensor(m_h[:, b % 2, :], m_g[:, b % 2, :], bank(2 * (b % 2) + 1),
                                      ALU.mult).then_inc(m_prod, 1)
                    item_rest(item, j + 3 + SPLIT)
                    j += 4
                    if b == E_BLOCKS - 1:
                        hidden_lo(item, b)
                    if b >= 1:
                        item_rest(item, j + SPLIT)
                        if b < E_BLOCKS - 1:
                            item_rest(item, j + 1 + SPLIT)
                        j += 2
                if first:
                    next_item(item)
                else:
                    with dve.If(n_second > item - (N_EXP - 1)):
                        next_item(item)

            pick_tokens(-1)
            rest_unit(U_MOE - 1 + SPLIT)
            tokens_lo(-1)
            weigh()
            run_item(0, True)
            dve.wait_ge(routed, 1)
            n_second = dve.value_load(second[0:1, 0:1], min_val=0, max_val=MAX_SECOND)
            with dve.Fori(1, N_EXP) as item:
                run_item(item, False)
            with dve.Fori(N_EXP, N_ITEMS) as item:
                with dve.If(n_second > item - N_EXP):
                    run_item(item, False)
            output_lo(n_second + (N_EXP - 1))
            norm(3, y_sum, 4)


def constants():
    r, c = np.arange(P)[:, None], np.arange(P)[None, :]
    full = np.ones((P, P))
    parts = [r == c, -1.0 * (r >= c), -full, r < c, full * c]
    return np.stack([np.asarray(a, np.float32) for a in parts], axis=1)


def rotation_tables():
    half = HD // 2
    pos = np.arange(T, dtype=np.float64)
    ang = pos[:, None] * 10000.0 ** (-np.arange(half, dtype=np.float64) / half)[None, :]
    gamma = 1.0 - 2.0 ** (-5.0 - np.arange(N_RET, dtype=np.float64))
    grow = gamma[None, :] ** pos[:, None]
    q, k = (grow * HD ** -0.5)[:, :, None], (1.0 / grow)[:, :, None]
    cos, sin = np.cos(ang)[:, None, :], np.sin(ang)[:, None, :]
    tab = np.stack([q * cos, q * sin, k * cos, k * sin], axis=1).reshape(T, 4, N_RET * half)
    return np.ascontiguousarray(tab.reshape(TT, P, 4, 256).transpose(1, 0, 2, 3).astype(np.float32))


def kernel(**inputs):
    import concourse.bacc as bacc
    from concourse.bass_utils import run_bass_kernel_spmd as run

    a = {k: np.asarray(v) for k, v in inputs.items()}
    x = a["x"].reshape(T, D)
    at = MAX_REL + P + np.arange(P)[:, None] - np.arange(T)[None, :]
    arrays = {
        "x": x, "xT": x.T,
        "ln_g": np.concatenate([a["even_ln1_g"], a["even_ln2_g"], a["odd_ln1_g"], a["odd_ln2_g"]]),
        "ln_b": np.concatenate([a["even_ln1_b"], a["even_ln2_b"], a["odd_ln1_b"], a["odd_ln2_b"]]),
        "w_in": a["even_w_in"][0], "gn_g": a["even_ret_gn_g"], "w_out": a["even_w_out"][0],
        "w_gate": a["even_w_gate"][0], "w_up": a["even_w_up"][0], "w_down": a["even_w_down"][0],
        "w_qkv": a["odd_w_qkv"][0], "bias_win": a["odd_rel_bias"][0][:, at].transpose(1, 0, 2),
        "w_out2": a["odd_w_out"][0], "w_router": a["odd_w_router"][0], "b_router": a["odd_b_router"],
        "e_gate": a["odd_w_gate"][0], "e_up": a["odd_w_up"][0], "e_down": a["odd_w_down"][0],
        "tables": rotation_tables(), "consts": constants(),
    }
    nc = bacc.Bacc("TRN2", target_bir_lowering=False, num_devices=1)
    arrays = {k: np.ascontiguousarray(v) for k, v in arrays.items()}
    args = [nc.dram_tensor(k, v.shape, F32, kind="ExternalInput").ap() for k, v in arrays.items()]
    out = nc.dram_tensor("out", (T, D), F32, kind="ExternalOutput").ap()
    trunk_kernel(nc, *args, out)
    return run(nc, [arrays], core_ids=[0]).results[0]["out"].reshape(1, T, D)
```
